# Optimizing a Trainium2 kernel written in Bass

```python
import math
import jax
import jax.numpy as jnp
from jax import lax
import numpy as np

D_MODEL = 1024
BATCH = 1
SEQ = 512
DEPTH = 1
DEC_BATCH = 8
DEC_SEQ = 1
PAST_LEN = 512
PAGE_SIZE = 128

D_MIX = D_MODEL
H_A = 6
DK_A = 64
DV_A = 64
CHUNK_A = 64
H_B = 6
DK_B = 32
DV_B = 64
H_C = 4
DH_C = 64
DILATED_PAIRS = ((128, 1), (512, 4), (2048, 16))
QB_C = 128
QB_B = 128
N_GROUPS = 4
EXPERTS_PER_GROUP = 4
N_EXPERTS = N_GROUPS * EXPERTS_PER_GROUP
TOP_K_IN_GROUP = 2
D_FF_E = 512
PLE_DIM = 256
RMS_EPS = 1e-6
MASK_VALUE = -1e30
COL_SIZES = (H_A * DK_A, H_A * DK_A, H_A * DV_A, H_A * DV_A,
             H_B * 2 * DK_B, H_B * 2 * DK_B, H_B * DV_B,
             H_C * DH_C, H_C * DH_C, H_C * DH_C,
             H_C * DH_C, H_C * DH_C, H_C * DH_C,
             H_C * DH_C, H_C * DH_C, H_C * DH_C)
N_IN = 2 * H_A * DK_A + 2 * H_A * DV_A + 2 * H_B * 2 * DK_B + H_B * DV_B + 3 * len(DILATED_PAIRS) * H_C * DH_C

kernel_name = 'hybrid_hgrn2_diffattn_dilated_hmoe_step'

def _rmsnorm(x, g):
    xf = x.astype(jnp.float32)
    y = xf * lax.rsqrt(jnp.mean(xf * xf, axis=-1, keepdims=True) + RMS_EPS)
    return (y * g.astype(jnp.float32)).astype(x.dtype)

def _split_projection(u, w_in_l, lb_l):
    n, t, _ = u.shape
    splits = [int(s) for s in np.cumsum(COL_SIZES)[:-1]]
    cols = jnp.split(u @ w_in_l, splits, axis=-1)
    aq, af, ai, ag, bq, bk, bv = cols[:7]
    q_a = (jax.nn.silu(aq) * DK_A ** -0.5).reshape(n, t, H_A, DK_A)
    lb = lb_l.astype(jnp.float32)
    a32 = af.astype(jnp.float32)
    f = lb + (1.0 - lb) * jax.nn.sigmoid(a32)
    logf = jnp.log(jnp.maximum(f, jnp.finfo(jnp.float32).tiny))
    k_a = (1.0 - lb) * jax.nn.sigmoid(-a32)
    hgrn = (q_a, k_a.reshape(n, t, H_A, DK_A), ai.reshape(n, t, H_A, DV_A),
            logf.reshape(n, t, H_A, DK_A), ag.reshape(n, t, H_A, DV_A))
    diff = (bq.reshape(n, t, H_B, 2, DK_B), bk.reshape(n, t, H_B, 2, DK_B), bv.reshape(n, t, H_B, DV_B))
    dil = tuple(tuple(c.reshape(n, t, H_C, DH_C) for c in cols[7 + 3 * g: 10 + 3 * g])
                for g in range(len(DILATED_PAIRS)))
    return hgrn, diff, dil

def _hgrn2_chunked(q, k, v, logf, s0):
    n, t = q.shape[:2]
    c = min(CHUNK_A, t)
    pad = (-t) % c

    def prep(a):
        a = jnp.pad(a.astype(jnp.float32), ((0, 0), (0, pad), (0, 0), (0, 0)))
        return a.reshape(n, -1, c, a.shape[2], a.shape[3]).swapaxes(0, 1)

    qs, ks, vs, gs = prep(q), prep(k), prep(v), prep(logf)
    tri = jnp.tril(jnp.ones((c, c), dtype=bool))[None, :, :, None, None]

    def step(s, inp):
        qc, kc, vc, gc = inp
        b = jnp.cumsum(gc, axis=1)
        o_inter = jnp.einsum('nthk,nhkv->nthv', qc * jnp.exp(b), s)
        diff = b[:, :, None] - b[:, None, :]
        decay = jnp.where(tri, jnp.exp(jnp.where(tri, diff, 0.0)), 0.0)
        att = jnp.einsum('nthk,ntshk,nshk->ntsh', qc, decay, kc)
        o_intra = jnp.einsum('ntsh,nshv->nthv', att, vc)
        bl = b[:, -1]
        s_new = jnp.exp(bl)[..., None] * s + jnp.einsum('nshk,nshv->nhkv', kc * jnp.exp(bl[:, None] - b), vc)
        return s_new, o_inter + o_intra

    s_fin, o = lax.scan(step, s0.astype(jnp.float32), (qs, ks, vs, gs))
    o = o.swapaxes(0, 1).reshape(n, -1, H_A, DV_A)[:, :t]
    return o, s_fin

def _hgrn2_readout(o, g, gain):
    n, t = o.shape[:2]
    return (_rmsnorm(o, gain) * jax.nn.silu(g.astype(jnp.float32))).reshape(n, t, H_A * DV_A)

def _diff_lambda(lam_l, layer):
    lam_init = 0.8 - 0.6 * math.exp(-0.3 * layer)
    lp = lam_l.astype(jnp.float32)
    lam = jnp.exp(jnp.sum(lp[0] * lp[1])) - jnp.exp(jnp.sum(lp[2] * lp[3])) + lam_init
    return lam, lam_init

def _diff_core(q, k, v, q_pos, k_pos, lam):
    s = jnp.einsum('nqhmd,nkhmd->nhmqk', q, k).astype(jnp.float32) * DK_B ** -0.5
    mask = k_pos[None, :] <= q_pos[:, None]
    p = jax.nn.softmax(jnp.where(mask, s, MASK_VALUE), axis=-1)
    a = p[:, :, 0] - lam * p[:, :, 1]
    return jnp.einsum('nhqk,nkhv->nqhv', a.astype(v.dtype), v)

def _diff_readout(o, gain, lam_init):
    n, t = o.shape[:2]
    return (_rmsnorm(o, gain).astype(jnp.float32) * (1.0 - lam_init)).reshape(n, t, H_B * DV_B)

def _diff_prompt(q, k, v, lam):
    n, s = q.shape[:2]
    nb = s // QB_B
    pos = jnp.arange(s)
    qb = q.reshape(n, nb, QB_B, H_B, 2, DK_B).swapaxes(0, 1)
    o = lax.map(lambda a: _diff_core(a[0], k, v, a[1], pos, lam), (qb, pos.reshape(nb, QB_B)))
    return o.swapaxes(0, 1).reshape(n, s, H_B, DV_B)

def _diff_sample(q, k_new, v_new, k_pages, v_pages, page_table, lam):
    nb_s, t = q.shape[:2]
    kp = k_pages[page_table].reshape(nb_s, -1, H_B, 2, DK_B)
    vp = v_pages[page_table].reshape(nb_s, -1, H_B, DV_B)
    past = kp.shape[1]
    k_all = jnp.concatenate([kp, k_new], axis=1)
    v_all = jnp.concatenate([vp, v_new], axis=1)
    return _diff_core(q, k_all, v_all, past + jnp.arange(t), jnp.arange(past + t), lam)

def _masked_softmax_stats(s, mask):
    s = jnp.where(mask, s, MASK_VALUE)
    m = jnp.max(s, axis=-1, keepdims=True)
    e = jnp.where(mask, jnp.exp(s - m), 0.0)
    den = jnp.sum(e, axis=-1, keepdims=True)
    return e / den, (m + jnp.log(den))[..., 0]

def _band_attn(q, k, v, wd):
    assert wd <= QB_C
    n, l, h, d = q.shape
    pad = (-l) % QB_C
    def blocks(a):
        a = jnp.pad(a, ((0, 0), (0, pad), (0, 0), (0, 0)))
        return a.reshape(n, -1, QB_C, h, d)
    qb, kb, vb = blocks(q), blocks(k), blocks(v)
    nb = qb.shape[1]
    kcat = jnp.concatenate([jnp.concatenate([jnp.zeros_like(kb[:, :1]), kb[:, :-1]], axis=1), kb], axis=2)
    vcat = jnp.concatenate([jnp.concatenate([jnp.zeros_like(vb[:, :1]), vb[:, :-1]], axis=1), vb], axis=2)
    s = jnp.einsum('nbqhd,nbkhd->nbhqk', qb, kcat).astype(jnp.float32) * DH_C ** -0.5
    qi = jnp.arange(QB_C)[:, None]
    kj = jnp.arange(2 * QB_C)[None, :]
    dist = qi + QB_C - kj
    kpos = jnp.arange(nb)[:, None, None] * QB_C - QB_C + kj[None]
    mask = (dist >= 0)[None] & (dist <= wd)[None] & (kpos >= 0)
    p, lse = _masked_softmax_stats(s, mask[None, :, None])
    o = jnp.einsum('nbhqk,nbkhd->nbqhd', p.astype(v.dtype), vcat)
    o = o.reshape(n, -1, h, d)[:, :l]
    lse = lse.transpose(0, 1, 3, 2).reshape(n, -1, h)[:, :l]
    return o, lse

def _dilated_prompt(q, k, v, dil, wd):
    n, l, h, d = q.shape
    ls = l // dil
    def to_streams(a):
        return a.reshape(n, ls, dil, h, d).transpose(0, 2, 1, 3, 4).reshape(n * dil, ls, h, d)
    o, lse = _band_attn(to_streams(q), to_streams(k), to_streams(v), wd)
    o = o.reshape(n, dil, ls, h, d).transpose(0, 2, 1, 3, 4).reshape(n, l, h, d)
    lse = lse.reshape(n, dil, ls, h).transpose(0, 2, 1, 3).reshape(n, l, h)
    return o, lse

def _dilated_sample(q, kbuf, vbuf, k_new, v_new, dil, wd):
    n, t = q.shape[:2]
    lb = kbuf.shape[1]
    k_all = jnp.concatenate([kbuf, k_new], axis=1)
    v_all = jnp.concatenate([vbuf, v_new], axis=1)
    idx = lb + jnp.arange(t)[:, None] - dil * jnp.arange(wd + 1)[None, :]
    valid = idx >= 0
    idxc = jnp.maximum(idx, 0)
    kg = k_all[:, idxc]
    vg = v_all[:, idxc]
    s = jnp.einsum('nthd,ntjhd->nthj', q, kg).astype(jnp.float32) * DH_C ** -0.5
    p, lse = _masked_softmax_stats(s, valid[None, :, None, :])
    o = jnp.einsum('nthj,ntjhd->nthd', p.astype(vg.dtype), vg)
    return o, lse

def _combine_dilated(outs, lses):
    w = jax.nn.softmax(jnp.stack(lses, axis=0), axis=0)
    o = jnp.sum(w[..., None] * jnp.stack(outs, axis=0).astype(jnp.float32), axis=0)
    n, t = o.shape[:2]
    return o.reshape(n, t, H_C * DH_C)

def _hier_moe(u, rgw, rgb, rew, reb, wg, wu, wd):
    n, t, d = u.shape
    x = u.reshape(n * t, d)
    g_logits = (x @ rgw + rgb).astype(jnp.float32)
    g_prob = jax.nn.softmax(g_logits, axis=-1)
    g_sel = jnp.argmax(g_logits, axis=-1)
    g_w = jnp.take_along_axis(g_prob, g_sel[:, None], axis=-1)
    e_logits = (x @ rew + reb).astype(jnp.float32).reshape(-1, N_GROUPS, EXPERTS_PER_GROUP)
    e_sel = jnp.take_along_axis(e_logits, g_sel[:, None, None], axis=1)[:, 0]
    top_v, top_i = lax.top_k(e_sel, TOP_K_IN_GROUP)
    e_w = jax.nn.softmax(top_v, axis=-1) * g_w
    e_idx = g_sel[:, None] * EXPERTS_PER_GROUP + top_i
    gates = jnp.sum(jax.nn.one_hot(e_idx, N_EXPERTS, dtype=jnp.float32) * e_w[..., None], axis=1)
    y = jnp.zeros((n * t, d), jnp.float32)
    for e in range(N_EXPERTS):
        h = jax.nn.silu(x @ wg[e]) * (x @ wu[e])
        y = y + gates[:, e:e + 1] * (h @ wd[e]).astype(jnp.float32)
    return y.reshape(n, t, d).astype(u.dtype)

def _post_mixer(h, mix, p_l, w_out_l, norm_ffn_l, rgw, rgb, rew, reb, wg, wu, wd, norm_ple_l, pgw, ppw):
    h = h + mix.astype(h.dtype) @ w_out_l
    h = h + _hier_moe(_rmsnorm(h, norm_ffn_l), rgw, rgb, rew, reb, wg, wu, wd)
    gate = jax.nn.sigmoid(_rmsnorm(h, norm_ple_l) @ pgw)
    return h + gate * (p_l @ ppw)

def setup_inputs(seed: int = 0) -> dict:
    key = jax.random.key(seed)
    ks = jax.random.split(key, 32)
    f32 = jnp.float32
    n_pages = PAST_LEN // PAGE_SIZE
    n_used = DEC_BATCH * n_pages
    n_pool = n_used + max(1, n_used // 4)

    def nrm(k, shape, scale):
        return jax.random.normal(k, shape, f32) * scale

    wins = [min(w, PAST_LEN) for w, _ in DILATED_PAIRS]
    return {
        'x_prompt': nrm(ks[0], (BATCH, SEQ, D_MODEL), 1.0),
        'x_sample': nrm(ks[1], (DEC_BATCH, DEC_SEQ, D_MODEL), 1.0),
        'state_hgrn': nrm(ks[4], (DEPTH, DEC_BATCH, H_A, DK_A, DV_A), 0.5),
        'cache_k_diff': nrm(ks[5], (DEPTH, n_pool, PAGE_SIZE, H_B, 2, DK_B), 1.0),
        'cache_v_diff': nrm(ks[6], (DEPTH, n_pool, PAGE_SIZE, H_B, DV_B), 1.0),
        'cache_win128': nrm(ks[7], (DEPTH, DEC_BATCH, wins[0], 2, H_C, DH_C), 1.0),
        'cache_win512': nrm(ks[8], (DEPTH, DEC_BATCH, wins[1], 2, H_C, DH_C), 1.0),
        'cache_win2048': nrm(ks[9], (DEPTH, DEC_BATCH, wins[2], 2, H_C, DH_C), 1.0),
        'page_table': jax.random.permutation(ks[10], n_pool)[:n_used].reshape(DEC_BATCH, n_pages).astype(jnp.int32),
        'p_prompt': nrm(ks[2], (DEPTH, BATCH, SEQ, PLE_DIM), 1.0),
        'p_sample': nrm(ks[3], (DEPTH, DEC_BATCH, DEC_SEQ, PLE_DIM), 1.0),
        'norm_mix': 1.0 + nrm(ks[11], (DEPTH, D_MODEL), 0.02),
        'w_in': nrm(ks[12], (DEPTH, D_MODEL, N_IN), D_MODEL ** -0.5),
        'hgrn_lb_logits': nrm(ks[13], (DEPTH, H_A * DK_A), 0.5),
        'hgrn_norm': 1.0 + nrm(ks[14], (DEPTH, DV_A), 0.02),
        'diff_lambda': nrm(ks[15], (DEPTH, 4, DK_B), 0.1),
        'diff_norm': 1.0 + nrm(ks[16], (DEPTH, DV_B), 0.02),
        'w_out': nrm(ks[17], (DEPTH, D_MIX, D_MODEL), D_MIX ** -0.5),
        'norm_ffn': 1.0 + nrm(ks[18], (DEPTH, D_MODEL), 0.02),
        'router_group_w': nrm(ks[19], (DEPTH, D_MODEL, N_GROUPS), D_MODEL ** -0.5),
        'router_group_b': nrm(ks[20], (DEPTH, N_GROUPS), 0.01),
        'router_expert_w': nrm(ks[21], (DEPTH, D_MODEL, N_EXPERTS), D_MODEL ** -0.5),
        'router_expert_b': nrm(ks[22], (DEPTH, N_EXPERTS), 0.01),
        'moe_w_gate': nrm(ks[23], (DEPTH, N_EXPERTS, D_MODEL, D_FF_E), D_MODEL ** -0.5),
        'moe_w_up': nrm(ks[24], (DEPTH, N_EXPERTS, D_MODEL, D_FF_E), D_MODEL ** -0.5),
        'moe_w_down': nrm(ks[25], (DEPTH, N_EXPERTS, D_FF_E, D_MODEL), D_FF_E ** -0.5),
        'norm_ple': 1.0 + nrm(ks[26], (DEPTH, D_MODEL), 0.02),
        'ple_w_gate': nrm(ks[27], (DEPTH, D_MODEL, D_MODEL), D_MODEL ** -0.5),
        'ple_w_proj': nrm(ks[28], (DEPTH, PLE_DIM, D_MODEL), PLE_DIM ** -0.5),
        'norm_final': 1.0 + nrm(ks[29], (D_MODEL,), 0.02),
    }

def reference(x_prompt, x_sample, state_hgrn, cache_k_diff, cache_v_diff, cache_win128, cache_win512,
              cache_win2048, page_table, p_prompt, p_sample, norm_mix, w_in, hgrn_lb_logits, hgrn_norm,
              diff_lambda, diff_norm, w_out, norm_ffn, router_group_w, router_group_b, router_expert_w,
              router_expert_b, moe_w_gate, moe_w_up, moe_w_down, norm_ple, ple_w_gate, ple_w_proj, norm_final):
    lb_sm = jax.nn.softmax(hgrn_lb_logits.astype(jnp.float32), axis=0)
    lower_bounds = jnp.cumsum(lb_sm, axis=0) - lb_sm[0]
    win_caches = (cache_win128, cache_win512, cache_win2048)
    seq = x_prompt.shape[1]

    hp, hs = x_prompt, x_sample
    st_p, st_s, kd_p, kd_s, vd_p, vd_s = [], [], [], [], [], []
    win_p = [[] for _ in DILATED_PAIRS]
    win_s = [[] for _ in DILATED_PAIRS]
    for l in range(DEPTH):
        lam, lam_init = _diff_lambda(diff_lambda[l], l)
        post_args = (w_out[l], norm_ffn[l], router_group_w[l], router_group_b[l], router_expert_w[l],
                     router_expert_b[l], moe_w_gate[l], moe_w_up[l], moe_w_down[l], norm_ple[l],
                     ple_w_gate[l], ple_w_proj[l])

        (qa, ka, va, fa, ga), (qb, kb, vb), dil = _split_projection(_rmsnorm(hp, norm_mix[l]), w_in[l], lower_bounds[l])
        s0 = jnp.zeros((hp.shape[0], H_A, DK_A, DV_A), jnp.float32)
        oa, sa = _hgrn2_chunked(qa, ka, va, fa, s0)
        ob = _diff_prompt(qb, kb, vb, lam)
        outs, lses = [], []
        for g, ((win, rate), (qc, kc, vc)) in enumerate(zip(DILATED_PAIRS, dil)):
            o, lse = _dilated_prompt(qc, kc, vc, rate, win // rate)
            outs.append(o)
            lses.append(lse)
            win_p[g].append(jnp.stack([kc, vc], axis=2)[:, max(seq - win, 0):])
        mix = jnp.concatenate([_hgrn2_readout(oa, ga, hgrn_norm[l]), _diff_readout(ob, diff_norm[l], lam_init),
                               _combine_dilated(outs, lses)], axis=-1)
        hp = _post_mixer(hp, mix, p_prompt[l], *post_args)
        st_p.append(sa)
        kd_p.append(kb)
        vd_p.append(vb)

        (qa, ka, va, fa, ga), (qb, kb, vb), dil = _split_projection(_rmsnorm(hs, norm_mix[l]), w_in[l], lower_bounds[l])
        oa, sa = _hgrn2_chunked(qa, ka, va, fa, state_hgrn[l])
        ob = _diff_sample(qb, kb, vb, cache_k_diff[l], cache_v_diff[l], page_table, lam)
        outs, lses = [], []
        for g, ((win, rate), (qc, kc, vc)) in enumerate(zip(DILATED_PAIRS, dil)):
            buf = win_caches[g][l]
            o, lse = _dilated_sample(qc, buf[:, :, 0], buf[:, :, 1], kc, vc, rate, win // rate)
            outs.append(o)
            lses.append(lse)
            win_s[g].append(jnp.concatenate([buf, jnp.stack([kc, vc], axis=2)], axis=1)[:, -buf.shape[1]:])
        mix = jnp.concatenate([_hgrn2_readout(oa, ga, hgrn_norm[l]), _diff_readout(ob, diff_norm[l], lam_init),
                               _combine_dilated(outs, lses)], axis=-1)
        hs = _post_mixer(hs, mix, p_sample[l], *post_args)
        st_s.append(sa)
        kd_s.append(kb)
        vd_s.append(vb)

    y_prompt = _rmsnorm(hp, norm_final)
    y_sample = _rmsnorm(hs, norm_final)
    state_hgrn_prompt = jnp.stack(st_p, axis=0)
    state_hgrn_sample = jnp.stack(st_s, axis=0)
    k_diff_prompt = jnp.stack(kd_p, axis=0)
    k_diff_sample = jnp.stack(kd_s, axis=0)
    v_diff_prompt = jnp.stack(vd_p, axis=0)
    v_diff_sample = jnp.stack(vd_s, axis=0)
    win128_prompt = jnp.stack(win_p[0], axis=0)
    win128_sample = jnp.stack(win_s[0], axis=0)
    win512_prompt = jnp.stack(win_p[1], axis=0)
    win512_sample = jnp.stack(win_s[1], axis=0)
    win2048_prompt = jnp.stack(win_p[2], axis=0)
    win2048_sample = jnp.stack(win_s[2], axis=0)
    return (y_prompt, y_sample, state_hgrn_prompt, state_hgrn_sample, k_diff_prompt, k_diff_sample,
            v_diff_prompt, v_diff_sample, win128_prompt, win128_sample, win512_prompt, win512_sample,
            win2048_prompt, win2048_sample)


_drawn_inputs = setup_inputs


def setup_inputs(seed=0):
    import zlib

    import numpy as np

    out = dict(_drawn_inputs(seed))
    spreads = {}
    factors = {'hgrn_norm': 6.206,
     'diff_norm': 2.881,
     'norm_ffn': 2.709,
     'router_group_b': 7.481,
     'router_expert_b': 4.863,
     'norm_ple': 8.0,
     'norm_final': 2.891}
    for name, (base, spread) in spreads.items():
        noise = np.random.default_rng([zlib.crc32(name.encode()), seed]).standard_normal(out[name].shape)
        drawn = base * np.exp(spread * noise) if base else spread * noise
        out[name] = jnp.asarray(drawn.astype(out[name].dtype))
    for name, factor in factors.items():
        out[name] = (out[name] * factor).astype(out[name].dtype)
    return out
```

```python
import numpy as np
import concourse.bass as bass
from concourse import mybir
from contextlib import ExitStack

F32 = mybir.dt.float32
BF16 = mybir.dt.bfloat16
I32 = mybir.dt.int32
U8 = mybir.dt.uint8
ALU = mybir.AluOpType
ACT = mybir.ActivationFunctionType
AX = mybir.AxisListType

P = 128
D = 1024
DC = D // P
SEQ = 512
NT = SEQ // P
NS = 8
NTOK = SEQ + NS
N_IN = 4992
SLAB = 384
NSLAB = N_IN // SLAB
PAST = 512
PAGES = PAST // P
NPOOL = 40
HA = HB = 6
HC = 4
NG = 3
WIN = (128, 512, 512)
DIL = (1, 4, 16)
NEG = -1e30
EPS = 1e-6
NGRP = 4
EPG = 4
NE = 16
FF = 512
FC = FF // P
PLE = 256
PC = PLE // P
MAXT = NE + (2 * NTOK - NE) // P
CAPW = FF * DC * 2 + D * FC
BIG = 1e30
SCALE_A = 64 ** -0.5
SCALE_B = 32 ** -0.5
SCALE_C = 64 ** -0.5
LAM_INIT = 0.8 - 0.6
LEVELS = 7
BIGT = 1e9
LN_SPLIT = 2.0 ** -63

C_COL = 7 * SLAB


def tile_rows(i):
    return P if i < NT else NS


def projection_units():
    units = []
    for s in range(NSLAB):
        col = s * SLAB
        if s < 7:
            kinds = ("FM", "FM", "TM", "TM", "FM", "FM", "TM")[s]
            if kinds == "FM":
                units += [("FM", s, c * P, P, (s, c)) for c in range(3)]
            else:
                units += [("TM", s, 0, SLAB, (s, i)) for i in range(NT)]
        else:
            g, half = divmod(col - C_COL, 768)
            if half == 0:
                units += [("FM", s, c * P, P, (7 + g, c)) for c in range(3)]
            else:
                units += [("FM", s, 0, P, (7 + g, 3))]
                units += [("TM", s, P, 2 * P, (7 + g, i)) for i in range(NT)]
        units.append(("SM", s, 0, SLAB, None))
    return units


def dilated_blocks(i):
    lo = max(i - 1, 0)
    out = [(0, kt, (kt - lo) * P) for kt in range(lo, i + 1)]
    for g in (1, 2):
        out += [(g, kt, g * SEQ + kt * P) for kt in range(i + 1)]
    return out


def dilated_groups():
    out = []
    for n in range(NT * HC):
        b = dilated_blocks(n // HC)
        parts = [b[k:k + 4] for k in range(0, len(b), 4)]
        out += [(n, p, k == 0, k == len(parts) - 1) for k, p in enumerate(parts)]
    return out


def schedule(units):
    last = {sl: max(u for u in range(len(units)) if units[u][1] == sl) for sl in range(NSLAB)}
    steps, todo = [], list(range(len(units)))

    def project(upto):
        while todo and todo[0] <= upto:
            steps.append(("proj", todo.pop(0)))

    def weave(seq, every):
        for k, st in enumerate(seq):
            steps.append(st)
            if k % every == every - 1 and todo:
                steps.append(("proj", todo.pop(0)))

    project(last[3])
    steps.append(("samp_t",))
    project(last[3] + 1)
    steps.append(("prep",))
    h = []
    nlev = NT * LEVELS
    j = 0
    h.append(("lev_d", 0))
    for i in range(NT):
        h += [("io_a", i), ("lev_mm", i, 0), ("io_b", i)]
        for l in range(1, LEVELS + 1):
            j = i * LEVELS + l - 1
            if j + 1 < nlev:
                h.append(("lev_d", j + 1))
            h += [("lev_q", j), ("lev_cp", i, l - 1), ("lev_mm", i, l)]
            if l == 3:
                h.append(("kt", i))
        h += [("lev_cp", i, LEVELS), ("h_out", i), ("h_state", i)]
    weave(h, 7)
    project(last[6])
    nd = NT * HB
    d = []
    for n in range(nd + 2):
        if n < nd:
            d.append(("d_s", n))
        if 1 <= n <= nd:
            d.append(("d_t", n - 1))
        if n >= 2:
            d.append(("d_pv", n - 2))
    weave(d, 2)
    project(len(units))
    groups = dilated_groups()
    c = [("c_s", 0)]
    for gi in range(len(groups) + 1):
        if gi < len(groups):
            if groups[gi][2] and groups[gi][0] + 1 < NT * HC:
                c.append(("c_s", groups[gi][0] + 1))
            c.append(("c_t", gi))
        if gi >= 1:
            c.append(("c_pv", gi - 1))
    weave(c, 4)
    steps += [("krows", i) for i in range(NT)]
    for i in range(NT):
        steps += [("ro", i), ("mt", i)]
    steps.append(("dec_new",))
    steps += [("dec_k", b) for b in range(NS)]
    steps.append(("dec_soft",))
    steps.append(("dec_state",))
    steps += [("dec_v", b) for b in range(NS)]
    steps += [("dec_out",), ("ro", NT), ("mt", NT)]
    return steps


def hybrid_kernel(nc, a, o):
    ctx = ExitStack()
    with ctx:
        def sb(name, shape, dt=F32):
            return ctx.enter_context(nc.sbuf_tensor(name, shape, dt))

        def sem(name):
            return ctx.enter_context(nc.semaphore(name))

        def dram(name, shape, dt=F32):
            return nc.dram_tensor(name, shape, dt, kind="Internal").ap()

        ctx.enter_context(nc.allow_non_contiguous_dma(reason="short rows of small tables"))
        EXPERT = sb("EXPERT", [P, 2 * CAPW])
        slab = [EXPERT[:, k * DC * SLAB:(k + 1) * DC * SLAB].rearrange("p (c n) -> p c n", c=DC) for k in range(2)]
        at0 = 2 * DC * SLAB
        cF = EXPERT[:, at0:at0 + 12 * SEQ].rearrange("p (g q t) -> p g q t", g=NG, q=4)
        at0 += 12 * SEQ
        iT = EXPERT[:, at0:at0 + NT * SLAB].rearrange("p (i n) -> p i n", i=NT)
        at0 += NT * SLAB
        gT = EXPERT[:, at0:at0 + (NT + 1) * SLAB].rearrange("p (i n) -> p i n", i=NT + 1)
        at0 += (NT + 1) * SLAB
        bvT = EXPERT[:, at0:at0 + NT * SLAB].rearrange("p (i n) -> p i n", i=NT)
        at0 += NT * SLAB
        cvT = EXPERT[:, at0:at0 + NT * NG * 256].rearrange("p (g i n) -> p g i n", g=NG, i=NT)
        at0 += NT * NG * 256
        stS = EXPERT[:, at0:at0 + NS * SLAB // 2].rearrange("p (b c v) -> p b c v", b=NS, c=3)
        at0 += NS * SLAB // 2
        kdil = [EXPERT[:, at0 + k * NG * 256:at0 + (k + 1) * NG * 256].rearrange("p (g n) -> p g n", g=NG)
                for k in range(2)]
        at0 += 2 * NG * 256
        S = EXPERT[:, at0:at0 + SLAB].rearrange("p (c n) -> p c n", c=3)
        at0 += SLAB
        blk = EXPERT[:, at0:at0 + P]
        at0 += P
        Sadd = EXPERT[:, at0:at0 + SLAB].rearrange("p (c n) -> p c n", c=3)
        at0 += SLAB
        assert at0 <= 2 * CAPW, at0
        kpage = [EXPERT[:, k * PAGES * SLAB:(k + 1) * PAGES * SLAB].rearrange("p (j n) -> p j n", j=PAGES)
                 for k in range(2)]
        stK = EXPERT[:, 2 * PAGES * SLAB:2 * PAGES * SLAB + NS * SLAB // 2].rearrange(
            "p (b c v) -> p b c v", b=NS, c=3)

        xT = sb("xT", [P, DC, NTOK])
        XM = sb("XM", [P, NT + 1, D])
        samp_ = sb("samp", [P, N_IN])
        samp = samp_[0:NS, :]
        aF_ = sb("aF", [P, 9 * NTOK])
        aF = aF_[:].rearrange("p (a c t) -> p a c t", a=3, c=3)
        qF, bF, kF = aF[:, 0], aF[:, 1], aF[:, 2]
        dF_ = sb("dF", [P, 6 * SEQ])
        dF = dF_[:].rearrange("p (a c t) -> p a c t", a=2, c=3)
        rw = sb("rw", [P, DC, 20])
        rbias = sb("rbias", [P, 20])
        wk = sb("wk", [P, 2, 3 * SEQ])
        work, work2 = wk[:, 0], wk[:, 1]
        PT = sb("PT", [P, 2, SEQ])
        ident = sb("ident", [P, P])
        ones = sb("ones", [P, P])
        identb = sb("identb", [P, P], BF16)
        mband = sb("mband", [P, 2 * P], BF16)
        mstride = sb("mstride", [P, 2, NT * P], BF16)
        lmask = sb("lmask", [P, LEVELS, P], U8)
        small = sb("small", [P, 512])
        gains = sb("gains", [P, 27])
        npage = sb("npage", [1, NS * PAGES], I32)
        hg = sb("hg", [P, 64])
        dg = sb("dg", [P, 64])
        lamb = sb("lamb", [P, 4 * 32])

        ps = ctx.enter_context(nc.psum_tensor("ps", [P, 8, 512], F32))

        ssq = small[:, 0:8]
        rstd = small[:, 8:16]
        lb = small[:, 16:19]
        omlb = small[:, 19:22]
        lam = small[:, 24:25]
        nlam = small[:, 25:26]
        negm = small[:, 32:36]
        den = small[:, 36:40]
        rec = small[:, 40:44]
        ebl = small[:, 44:47]
        epsc = small[:, 47:48]
        lnb = small[:, 48:49]
        tmp = small[:, 64:128]

        SD = dF[:, 0, 0, 0:384].rearrange("p (j r) -> p j r", j=PAGES)
        SC = dF[:, 0, 1, 0:96].rearrange("p (g r) -> p g r", g=NG)
        AD = dF[:, 0, 2, 0:192].rearrange("p (j r) -> p j r", j=PAGES)
        AC = dF[:, 0, 2, 192:288].rearrange("p (g r) -> p g r", g=NG)
        RD = work[0:96, 0:PAST + 1]
        RC = work2[0:32, 0:2 * P + 32 + NG]
        NDIL = 2 * P + 32
        hms = dF[0:96, 1, 0, 0:12]
        mB = dF[0:96, 1, 0, 16:24]
        hsel = dF[0:32, 1, 0, 32:36]
        mC = dF[0:32, 1, 0, 40:48]
        LD = dF[0:96, 1, 0, 48:56]
        LC = dF[0:32, 1, 0, 64:88].rearrange("p (g b) -> p g b", g=NG)
        st96 = dF[0:96, 1, 0, 96:104]
        st32 = dF[0:32, 1, 0, 112:120]
        anew = dF[0:8, 1, 0, 128:152]
        snd = dF[0:8, 1, 0, 160:172]
        snc = dF[0:8, 1, 0, 176:188].rearrange("p (g h) -> p g h", g=NG)
        MD = dF[0:8, 1, 0, 192:288]
        MC = dF[0:8, 1, 0, 288:384].rearrange("p (g b h) -> p g b h", g=NG, b=NS)
        oDF = dF[:, 1, 1, 0:24].rearrange("p (c b) -> p c b", c=3)
        oCF = dF[:, 1, 1, 24:40].rearrange("p (c b) -> p c b", c=2)
        fex = dF[:, 1, 1, 64:88].rearrange("p (c b) -> p c b", c=3)
        id8 = dF[:, 1, 1, 128:192]
        Qz = dF[:, 1, 2, 0:192].rearrange("p (c b e) -> p c b e", c=3, b=NS)
        vt = dF[0:8, 1, 2, 192:448]
        dcst = PT[0:8, 0, :]

        names = """act_seq dve_seq pool_seq cload consts rstd_ok xn_ok xt_pe xt_ok gain_pe gain_ok unit_pe unit_ok outs
            tab_ok lb_e lb_ok lam_s lam_e  samp_t_pe samp_t_ok prep_e prep_q prep_f prep_ln prep_ok
            gate_e gate_ok lev_d lev_e lev_q lev_pe lev_cp io_d io_e io_ok kt_pe kt_ok h_out_pe h_out_ok h_st_pe h_st_ok
            d_s_pe d_max d_exp d_a d_t_pe d_t_ok d_o_pe d_o_ok c_s_pe c_max c_exp c_t_pe c_t_ok c_o_pe c_o_ok
            kr_pe kr_ok  stload kused bq_pe new_ok vused sc_pe row_ok row_e w_ok wt_pe aw_ok of_ok
            ot_pe dec_done vb_pe kv_ok fx_ok s_new s_o_pe
            ro_sq ro_e ro_ok mt_pe mt_ok woload wo_pe hres_ok n2_e u_ok u_st ut_pe ut_ok rl_pe  rt_e gexp
            c_ok rank_pe rank_ok scat idxld pool_past tab_rdy xg_idx mx_pe mx_ok g_pe u_pe sil_ok h_ok ht_pe ht_ok y_pe
            ya_ok yb_ok   comb_ok hn_e hn_ok hnt_pe hnt_ok  pg_pe pg_sig po_ok n4_e y_ok pleload  iot
            """.split()
        S_ = {n: sem(n) for n in names}
        xload = [sem(f"xload{i}") for i in range(NT + 1)]
        slabload = [sem(f"slabload{k}") for k in range(2)]
        kr_out = [sem(f"kr_out{k}") for k in range(2)]
        kvload = [sem(f"kvload{k}") for k in range(2)]

        wload = {k: [sem(f"{k}load{b}") for b in range(2)] for k in ("wg", "wu", "wd")}
        xgload = [sem(f"xgload{k}") for k in range(2)]
        ystore = [sem(f"ystore{k}") for k in range(2)]
        yload = [sem(f"yload{k}") for k in range(2)]
        pload = [sem(f"pload{k}") for k in range(2)]

        W = [EXPERT[:, k * CAPW:(k + 1) * CAPW] for k in range(2)]
        wg_ = [w[:, 0:DC * FF].rearrange("p (c n) -> p c n", c=DC) for w in W]
        wu_ = [w[:, DC * FF:2 * DC * FF].rearrange("p (c n) -> p c n", c=DC) for w in W]
        wd_ = [w[:, 2 * DC * FF:].rearrange("p (c n) -> p c n", c=FC) for w in W]
        wout_ = EXPERT[:, 0:DC * D].rearrange("p (c n) -> p c n", c=DC)
        aflat = aF_[:]
        dflat = dF_[:]
        wflat = wk[:].rearrange("p a n -> p (a n)")
        xg = [aflat[:, k * D:(k + 1) * D] for k in range(2)]
        xgT = [aflat[:, (2 + k) * D:(3 + k) * D].rearrange("p (c t) -> p c t", c=DC) for k in range(2)]
        hb = [dflat[:, k * FF:(k + 1) * FF] for k in range(2)]
        hT = [dflat[:, (2 + k) * FF:(3 + k) * FF].rearrange("p (c t) -> p c t", c=FC) for k in range(2)]
        yb_ = [wflat[:, k * D:(k + 1) * D] for k in range(2)]
        Ub = [wflat[:, k * D:(k + 1) * D] for k in range(3)]
        RT = [aflat[:, k * D:(k + 1) * D].rearrange("p (c t) -> p c t", c=DC) for k in range(4)]
        u2d = dram("u2d", [NTOK, D])
        Yd = dram("Yd", [MAXT * P, D])
        list_d = dram("list_d", [MAXT * P, 1], I32)
        off = [0]

        def take(*shape, dt=F32):
            k = int(np.prod(shape))
            v_ = samp_[:, off[0]:off[0] + k]
            off[0] += k
            if dt != F32:
                v_ = v_.bitcast(dt)
            if len(shape) == 2:
                v_ = v_.rearrange("p (a b) -> p a b", a=shape[0])
            return v_

        T5 = NT + 1
        L = take(T5, 20)
        jrow = take(4)
        erow = take(NE)
        tokf = take(T5)
        toki = take(T5, dt=I32)
        tri = take(P)
        gm, gs, gw, m1, m2, mn, e2, w1, w2 = (take(T5) for _ in range(9))
        og, o1, o2, es, es2, t4 = (take(T5, 4) for _ in range(6))
        O1, O2, C, rank, q_, tl, t16, slotY, slotL = (take(T5, NE) for _ in range(9))
        cnt, nx, incl, exc = (take(NE) for _ in range(4))
        xrow = take(8)
        xcmp = take(8, NE)
        tabf = take(MAXT)
        tabi = take(MAXT, dt=I32)
        npf = take(2)
        npi = take(2, dt=I32)
        sel = take(4, T5)
        seli = take(4, T5, dt=I32)
        idxall = take(MAXT, dt=I32)
        idxc = [take(1, dt=I32) for _ in range(2)]
        zi = take(MAXT, dt=I32)
        iti = take(24, dt=I32)
        assert off[0] <= N_IN, off[0]

        ple_ = EXPERT[:, 0:DC * D].rearrange("p (c n) -> p c n", c=DC)
        plp_ = EXPERT[:, DC * D:(DC + PC) * D].rearrange("p (c n) -> p c n", c=PC)
        nfin = EXPERT[:, (DC + PC) * D:(DC + PC + 1) * D]
        q0 = (DC + PC + 1) * D
        prow = [EXPERT[:, q0 + k * PLE:q0 + (k + 1) * PLE] for k in range(2)]
        pTt = [EXPERT[:, q0 + (2 + k) * PLE:q0 + (3 + k) * PLE].rearrange("p (c t) -> p c t", c=PC) for k in range(2)]
        q0 += 4 * PLE
        hnT = [EXPERT[:, q0 + k * D:q0 + (k + 1) * D].rearrange("p (c t) -> p c t", c=DC) for k in range(2)]
        q0 += 2 * D
        sig = [EXPERT[:, q0 + k * D:q0 + (k + 1) * D] for k in range(2)]
        q0 += 2 * D
        ybuf = [[aflat[:, k * D:(k + 1) * D] for k in range(2)], [aflat[:, (2 + k) * D:(3 + k) * D] for k in range(2)]]

        UNITS = projection_units()
        NU = len(UNITS)
        LASTU = {sl: max(u for u in range(NU) if UNITS[u][1] == sl) for sl in range(NSLAB)}
        STEPS = schedule(UNITS)
        DG = dilated_groups()
        KROWS = [(1, 2) if i < NT - 1 else (1, 2, 0) for i in range(NT)]
        KPER = 2 * PAGES // 2 + NG
        block = ctx.enter_context(nc.Block())

        def f2(ap, n):
            return ap.unsqueeze(2).to_broadcast([ap.shape[0], ap.shape[1], n])

        def rows_of(buf, i):
            return buf[:, :, i * P:(i + 1) * P]

        @block.sync
        def _(sp):
            n_out = 0
            for i in range(NT + 1):
                src = a["x_prompt"][0, i * P:(i + 1) * P, :] if i < NT else a["x_sample"].rearrange("b t d -> (b t) d")
                sp.dma_start(XM[0:tile_rows(i), i, :], src).then_inc(xload[i], 16)
            w = a["w_in"][0].rearrange("(c p) n -> p c n", p=P)
            for s in range(NSLAB):
                if s >= 2:
                    sp.wait_ge(S_["unit_pe"], 1 + LASTU[s - 2])
                sp.dma_start(slab[s % 2], w[:, :, s * SLAB:(s + 1) * SLAB]).then_inc(slabload[s % 2], 16)
            for g in range(NG):
                src = a[("cache_win128", "cache_win512", "cache_win2048")[g]][0]
                dst = o["win_sample"][g][0]
                n = WIN[g] - 1
                sp.dma_start(dst[:, 0:n].rearrange("b r k h d -> b (r k h d)"),
                             src[:, 1:n + 1].rearrange("b r k h d -> b (r k h d)")).then_inc(S_["outs"], 16)
                n_out += 1
            st = a["state_hgrn"][0].rearrange("b (c e) k v -> e k b c v", e=2)
            for e in range(2):
                for c in range(3):
                    sp.dma_start(stS[64 * e:64 * e + 64, :, c], st[e, :, :, c]).then_inc(S_["stload"], 16)
            sp.wait_ge(S_["unit_ok"], NU)
            sp.dma_start(o["k_diff_sample"].rearrange("l b t h m d -> (l b t) (h m d)"),
                         samp[:, 5 * SLAB:6 * SLAB]).then_inc(S_["outs"], 16)
            sp.dma_start(o["v_diff_sample"].rearrange("l b t h d -> (l b t) (h d)"),
                         samp[:, 6 * SLAB:7 * SLAB]).then_inc(S_["outs"], 16)
            for g in range(NG):
                c = C_COL + g * 768 + 256
                sp.dma_start(o["win_sample"][g][0, :, WIN[g] - 1].rearrange("b k h d -> b (k h d)"),
                             samp[:, c:c + 512]).then_inc(S_["outs"], 16)
            n_out += 5
            sp.wait_ge(S_["cload"], 16 * 10)
            wins = [a["cache_win128"], a["cache_win512"], a["cache_win2048"]]

            def cached(b, kv):
                buf, ld = b % 2, kvload[b % 2]
                pool_ = a[("cache_k_diff", "cache_v_diff")[kv]]
                pool_ = pool_[0].rearrange("n t h m d -> n t (h m d)") if kv == 0 else pool_[0].rearrange(
                    "n t h d -> n t (h d)")
                for j in range(PAGES):
                    page = sp.value_load(npage[0:1, b * PAGES + j:b * PAGES + j + 1], min_val=0, max_val=NPOOL - 1)
                    sp.dma_start(kpage[buf][:, j, :].unsqueeze(1),
                                 pool_[bass.ds(page, 1)].rearrange("o t n -> t o n")).then_inc(ld, 16)
                for g in range(NG):
                    r = (P, P, 32)[g]
                    src = wins[g][0, b].rearrange("(r s) k h d -> r s k (h d)", s=DIL[g])[:, 0, kv]
                    sp.dma_start(kdil[buf][0:r, g], src).then_inc(ld, 16)

            for b in range(NS):
                if b >= 2:
                    sp.wait_ge(S_["kused"], b - 1)
                cached(b, 0)
            for i in range(NT):
                sp.dma_start(o["v_diff_prompt"][0, 0, i * P:(i + 1) * P].rearrange("t h d -> t (h d)"),
                             bvT[:, i]).then_inc(S_["outs"], 16)
                n_out += 1
                for g in range(NG):
                    lo = i * P - (SEQ - WIN[g])
                    if lo >= 0:
                        sp.dma_start(o["win_prompt"][g][0, 0, lo:lo + P, 1].rearrange("t h d -> t (h d)"),
                                     cvT[:, g, i]).then_inc(S_["outs"], 16)
                        n_out += 1
            for b in range(NS):
                if b < 2:
                    sp.wait_ge(S_["kused"], NS - 1 + b)
                else:
                    sp.wait_ge(S_["vused"], b - 1)
                cached(b, 1)
            st = o["state_hgrn_sample"][0].rearrange("b (c e) k v -> e k b c v", e=2)
            sp.wait_ge(S_["s_new"], 1)
            for e in range(2):
                for c in range(3):
                    sp.dma_start(st[e, :, :, c], stS[64 * e:64 * e + 64, :, c]).then_inc(S_["outs"], 16)
            sp.wait_ge(S_["h_st_ok"], NT)
            st = o["state_hgrn_prompt"][0, 0].rearrange("(c e) k v -> e k c v", e=2)
            for e in range(2):
                sp.dma_start(st[e], S[64 * e:64 * e + 64, :, 64 * e:64 * e + 64]).then_inc(S_["outs"], 16)
            n_out += 8
            sp.wait_ge(S_["vused"], NS)
            sp.wait_ge(S_["mt_pe"], NT)
            sp.dma_start(wout_, a["w_out"][0].rearrange("(c p) n -> p c n", p=P)).then_inc(S_["woload"], 16)
            for i in range(NT + 1):
                src = a["x_prompt"][0, i * P:(i + 1) * P, :] if i < NT else a["x_sample"].rearrange("b t d -> (b t) d")
                sp.wait_ge(S_["mt_pe"], i + 1)
                sp.dma_start(XM[0:tile_rows(i), i, :], src).then_inc(xload[i], 16)
            sp.wait_ge(S_["outs"], 16 * n_out)
            wsrc = dict(wg=a["moe_w_gate"][0].rearrange("e (c p) n -> p (e c) n", p=P),
                        wu=a["moe_w_up"][0].rearrange("e (c p) n -> p (e c) n", p=P),
                        wd=a["moe_w_down"][0].rearrange("e (c p) n -> p (e c) n", p=P))
            nch = dict(wg=DC, wu=DC, wd=FC)
            wdst = dict(wg=wg_, wu=wu_, wd=wd_)
            sp.wait_ge(S_["ro_ok"], NT + 1)
            for k in ("wg", "wu", "wd"):
                sp.dma_start(wdst[k][1], wsrc[k][:, nch[k]:2 * nch[k]]).then_inc(wload[k][1], 16)
            for i in range(NT + 1):
                sp.wait_ge(S_["u_ok"], i + 1)
                sp.dma_start(u2d[i * P:i * P + tile_rows(i), :], Ub[i % 3][0:tile_rows(i), :]).then_inc(S_["u_st"], 16)
            sp.wait_ge(S_["wo_pe"], NT + 1)
            for k in ("wg", "wu", "wd"):
                sp.dma_start(wdst[k][0], wsrc[k][:, 0:nch[k]]).then_inc(wload[k][0], 16)
            sp.wait_ge(S_["tab_rdy"], 1)
            npairs = sp.value_load(npi[0:1, 0:1], min_val=NE // 2, max_val=MAXT // 2)
            with sp.Fori(1, npairs) as i:
                for b in range(2):
                    e = sp.value_load(tabi[0:1, bass.ds(2 * i + b, 1)], min_val=0, max_val=NE - 1)
                    for k, done in (("wg", "g_pe"), ("wu", "u_pe"), ("wd", "y_pe")):
                        sp.wait_ge(S_[done], 2 * i + b - 1)
                        sp.dma_start(wdst[k][b], wsrc[k][:, bass.ds(e * nch[k], nch[k])]).then_inc(wload[k][b], 16)
            sp.wait_ge(S_["y_pe"], npairs * 2)
            sp.dma_start(ple_[:, :, :], a["ple_w_gate"][0].rearrange("(c p) n -> p c n", p=P)).then_inc(S_["pleload"], 16)
            sp.dma_start(plp_[:, :, :], a["ple_w_proj"][0].rearrange("(c p) n -> p c n", p=P)).then_inc(S_["pleload"], 16)
            sp.dma_start(nfin, a["norm_final"].rearrange("(o n) -> o n", o=1).to_broadcast([P, D])).then_inc(S_["pleload"], 16)
            for i in range(NT + 1):
                r = tile_rows(i)
                if i >= 2:
                    sp.wait_ge(S_["hnt_pe"], i - 1)
                src = a["p_prompt"][0, 0, i * P:(i + 1) * P, :] if i < NT else a["p_sample"][0].rearrange("b t d -> (b t) d")
                sp.dma_start(prow[i % 2][0:r, :], src).then_inc(pload[i % 2], 16)
            for i in range(NT + 1):
                r = tile_rows(i)
                sp.wait_ge(S_["y_ok"], i + 1)
                dst = o["y_prompt"][0, i * P:(i + 1) * P, :] if i < NT else o["y_sample"].rearrange("b t d -> (b t) d")
                sp.dma_start(dst, XM[0:r, i, :]).then_inc(S_["outs"], 16)
                n_out += 1
            sp.wait_ge(kr_out[0], 16 * 6)
            sp.wait_ge(kr_out[1], 16 * 7)
            sp.wait_ge(S_["outs"], 16 * n_out)

        @block.gpsimd
        def _(pool):
            n = [0]

            def seq(ins):
                n[0] += 1
                ins.then_inc(S_["pool_seq"], 1)
                pool.wait_ge(S_["pool_seq"], n[0])

            g = nc.gpsimd
            g.memset(ones[:], 1.0)
            seq(g.memset(PT[:], 0.0))
            seq(g.memset(identb[:], 0.0))
            seq(g.memset(ident[:], 0.0))
            g.affine_select(out=identb[:], in_=identb[:], compare_op=ALU.not_equal, fill=1.0, base=0,
                            pattern=[[-1, P]], channel_multiplier=1).then_inc(S_["consts"], 1)
            g.affine_select(out=ident[:], in_=ident[:], compare_op=ALU.not_equal, fill=1.0, base=0,
                            pattern=[[-1, P]], channel_multiplier=1).then_inc(S_["consts"], 1)
            dist = iT[:, 0, 0:P].bitcast(I32)
            rowi = iT[:, 0, P:2 * P].bitcast(I32)
            coli = iT[:, 0, 2 * P:3 * P].bitcast(I32)
            seq(g.iota(dist, pattern=[[-1, P]], base=P, channel_multiplier=1))
            seq(g.iota(rowi, pattern=[[0, P]], base=0, channel_multiplier=1))
            g.iota(coli, pattern=[[1, P]], base=0, channel_multiplier=0).then_inc(S_["consts"], 1)
            seq(g.memset(mband[:], 0.0))
            seq(g.affine_select(out=mband[:, 0:P], in_=mband[:, 0:P], compare_op=ALU.is_ge, fill=NEG, base=0,
                                pattern=[[1, P]], channel_multiplier=-1))
            g.affine_select(out=mband[:, P:2 * P], in_=mband[:, P:2 * P], compare_op=ALU.is_ge, fill=NEG, base=0,
                            pattern=[[-1, P]], channel_multiplier=1).then_inc(S_["consts"], 1)
            seq(g.memset(blk[:], 0.0))
            seq(g.memset(blk[0:64, 0:64], 1.0))
            g.memset(blk[64:P, 64:P], 1.0).then_inc(S_["consts"], 1)
            pool.wait_ge(S_["consts"], 5)
            pool.wait_ge(S_["tab_ok"], 1)
            own = mstride[:, :, (NT - 1) * P:NT * P]
            g.affine_select(out=own, in_=own, compare_op=ALU.is_ge, fill=NEG, base=0,
                            pattern=[[0, 2], [-1, P]], channel_multiplier=1).then_inc(S_["consts"], 1)
            pool.dma_start(Yd[NE * P:MAXT * P].rearrange("(j p) n -> p j n", p=P),
                           PT[:].rearrange("p a n -> p (a n)").unsqueeze(1).to_broadcast([P, MAXT - NE, D])
                           ).then_inc(S_["idxld"], 16)
            pool.wait_ge(S_["dec_done"], 1)
            seq(g.memset(zi, 0))
            pool.dma_start(list_d.rearrange("(p j) o -> p (j o)", p=P), zi).then_inc(S_["idxld"], 16)
            seq(g.iota(toki, pattern=[[P, T5]], base=0, channel_multiplier=1))
            seq(g.memset(tri, 1.0))
            seq(g.affine_select(out=tri, in_=tri, compare_op=ALU.is_ge, fill=0.0, base=-1,
                                pattern=[[1, P]], channel_multiplier=-1))
            seq(g.iota(iti, pattern=[[1, 24]], base=0, channel_multiplier=0))
            seq(g.memset(L, 0.0))
            g.memset(q_, 0.0).then_inc(S_["iot"], 1)
            pool.wait_ge(S_["idxld"], 32)
            pool.wait_ge(S_["rank_ok"], 1)
            for i in range(T5):
                r = tile_rows(i)
                for k in range(2):
                    g.indirect_dma_start(out=list_d, out_offset=bass.IndirectOffsetOnAxis(ap=seli[0:r, 2 + k, i:i + 1], axis=0),
                                         in_=toki[0:r, i:i + 1], in_offset=None).then_inc(S_["scat"], 16)
            pool.wait_ge(S_["scat"], 16 * 2 * T5)
            pool.dma_start(idxall, list_d.rearrange("(p j) o -> p (j o)", p=P)).then_inc(S_["idxld"], 16)
            pool.wait_ge(S_["idxld"], 48)
            pool.wait_ge(S_["u_st"], 16 * T5)
            pool.wait_ge(S_["rl_pe"], T5)
            pool.wait_ge(S_["tab_rdy"], 1)
            npairs = pool.value_load(npi[0:1, 0:1], min_val=NE // 2, max_val=MAXT // 2)

            def gather(j, b, count):
                g.tensor_copy(idxc[b], idxall[:, j]).then_inc(S_["xg_idx"], 1)
                pool.wait_ge(S_["xg_idx"], count)
                pool.sem_inc(S_["pool_past"], 1)
                g.indirect_dma_start(out=xg[b], out_offset=None, in_=u2d,
                                     in_offset=bass.IndirectOffsetOnAxis(ap=idxc[b], axis=0)).then_inc(xgload[b], 16)

            for b in range(2):
                gather(slice(b, b + 1), b, b + 1)
            with pool.Fori(1, npairs) as i:
                for b in range(2):
                    pool.wait_ge(S_["mx_pe"], 2 * i + b - 1)
                    gather(bass.ds(2 * i + b, 1), b, 2 * i + b + 1)
            for b in range(2):
                pool.wait_ge(ystore[b], npairs * 16)
            pool.wait_ge(S_["y_pe"], npairs * 2)
            pool.sem_inc(S_["pool_past"], 1)
            for i in range(T5):
                r = tile_rows(i)
                if i >= 2:
                    pool.wait_ge(S_["comb_ok"], i - 1)
                for k in range(2):
                    g.indirect_dma_start(out=ybuf[i % 2][k][0:r, :], out_offset=None, in_=Yd,
                                         in_offset=bass.IndirectOffsetOnAxis(ap=seli[0:r, k, i:i + 1], axis=0)
                                         ).then_inc(yload[i % 2], 16)

        @block.scalar
        def _(act):
            n = [0]
            s = nc.scalar

            def seq(ins):
                n[0] += 1
                ins.then_inc(S_["act_seq"], 1)
                act.wait_ge(S_["act_seq"], n[0])

            act.dma_start(work2[0:24, 0:P], a["norms"]).then_inc(S_["cload"], 16)
            act.dma_start(work2[24:27, 0:P],
                          a["hgrn_lb_logits"].rearrange("l (c p) -> (l c) p", p=P)).then_inc(S_["cload"], 16)
            act.dma_start(hg[:], a["hgrn_norm"].to_broadcast([P, 64])).then_inc(S_["cload"], 16)
            act.dma_start(dg[:], a["diff_norm"].to_broadcast([P, 64])).then_inc(S_["cload"], 16)
            act.dma_start(lamb[:], a["diff_lambda"].rearrange("l r d -> l (r d)").to_broadcast([P, P])).then_inc(S_["cload"], 16)
            act.dma_start(npage[:], a["page_table"].rearrange("(o b) j -> o (b j)", o=1)).then_inc(S_["cload"], 16)
            act.dma_start(rw[:, :, 0:NGRP], a["router_group_w"][0].rearrange("(c p) n -> p c n", p=P)).then_inc(S_["cload"], 16)
            act.dma_start(rw[:, :, NGRP:20], a["router_expert_w"][0].rearrange("(c p) n -> p c n", p=P)).then_inc(S_["cload"], 16)
            act.dma_start(rbias[:, 0:NGRP], a["router_group_b"].to_broadcast([P, NGRP])).then_inc(S_["cload"], 16)
            act.dma_start(rbias[:, NGRP:20], a["router_expert_b"].to_broadcast([P, NE])).then_inc(S_["cload"], 16)
            act.wait_ge(S_["gain_ok"], 1)
            for i in range(NT + 1):
                r = tile_rows(i)
                act.wait_ge(xload[i], 16)
                seq(s.activation(work[0:r, 0:D], XM[0:r, i, :], ACT.Square, accum_out=ssq[0:r, i:i + 1]))
                seq(s.activation(ssq[0:r, i:i + 1], ssq[0:r, i:i + 1], ACT.Ln, bias=epsc[0:r, :], scale=1.0 / D))
                s.activation(rstd[0:r, i:i + 1], ssq[0:r, i:i + 1], ACT.Exp, scale=-0.5).then_inc(S_["rstd_ok"], 1)
            act.wait_ge(S_["lb_e"], 1)
            s.activation(lb, lb, ACT.Exp).then_inc(S_["lb_ok"], 1)
            act.wait_ge(S_["lam_s"], 1)
            s.activation(tmp[:, 0:2], tmp[:, 0:2], ACT.Exp).then_inc(S_["lam_e"], 1)

            def proj(u):
                kind, sl, c0, w, at = UNITS[u]
                act.wait_ge(S_["unit_pe"], u + 1)
                src = ps[:, u % 2, :]
                scale = 1.0
                if u == 0:
                    act.wait_ge(S_["tab_ok"], 1)
                if kind == "SM":
                    src, dst = src[0:NS, 0:SLAB], samp[:, sl * SLAB:(sl + 1) * SLAB]
                elif kind == "TM":
                    g, i = at
                    dst = iT[:, i] if g == 2 else gT[:, i] if g == 3 else bvT[:, i] if g == 6 else cvT[:, g - 7, i]
                    src = src[:, 0:w]
                else:
                    g, c = at
                    if g < 2:
                        dst = aF[:, g, c, 0:SEQ]
                    elif g < 7:
                        dst, scale = dF[:, g - 4, c], SCALE_B if g == 4 else 1.0
                    else:
                        dst, scale = cF[:, g - 7, c], SCALE_C if c < 2 else 1.0
                s.activation(dst, src, ACT.Copy, scale=scale).then_inc(S_["unit_ok"], 1)

            def samp_t():
                act.wait_ge(S_["samp_t_pe"], 1)
                s.activation(aF[:, 0:2, :, SEQ:NTOK].rearrange("p a c t -> p (a c) t"),
                             ps[:, 2, 0:48].rearrange("p (a t) -> p a t", a=6), ACT.Copy).then_inc(S_["samp_t_ok"], 1)

            def prep():
                act.wait_ge(S_["samp_t_ok"], 1)
                act.wait_ge(S_["unit_ok"], LASTU[3] + 1)
                s.activation(kF, qF, ACT.Exp, scale=-1.0).then_inc(S_["prep_e"], 1)
                act.wait_ge(S_["prep_q"], 1)
                seq(s.activation(kF, bF, ACT.Exp))
                s.activation(bF, bF, ACT.Exp, scale=-1.0).then_inc(S_["prep_e"], 1)
                act.wait_ge(S_["gate_e"], 1)
                s.activation(wk[:].rearrange("p a n -> p (a n)")[:, 0:5 * SLAB], gT.rearrange("p i n -> p (i n)"),
                             ACT.Exp, scale=-1.0).then_inc(S_["gate_ok"], 1)
                act.wait_ge(S_["prep_f"], 3)
                for c in range(3):
                    fb = wk[:].rearrange("p a n -> p (a n)")[:, c * NTOK:(c + 1) * NTOK]
                    s.activation(bF[:, c], bF[:, c], ACT.Ln)
                    s.activation(fb, fb, ACT.Ln).then_inc(S_["prep_ln"], 1)

            def lev_q(j):
                act.wait_ge(S_["lev_d"], j + 1)
                B = 2 ** (j % LEVELS)
                Dv = work[:, (j % 2) * SLAB:(j % 2 + 1) * SLAB].rearrange("p (n e t) -> p n e t", e=2, t=B)
                s.activation(Dv[:, :, 1], Dv[:, :, 1], ACT.Exp)
                s.activation(Dv[:, :, 0], Dv[:, :, 0], ACT.Exp, scale=-1.0).then_inc(S_["lev_e"], 1)

            def io_a(i):
                act.wait_ge(S_["io_d"], i + 1)
                if i:
                    act.wait_ge(S_["h_out_pe"], i)
                s.activation(work2[:, 768:1152].rearrange("p (c t) -> p c t", c=3), rows_of(bF, i), ACT.Exp)
                s.activation(work2[:, 1152:1536], work2[:, 1152:1536], ACT.Exp, scale=-1.0).then_inc(S_["io_e"], 1)

            def kt(i):
                act.wait_ge(S_["idxld"], 16)
                act.wait_ge(S_["kt_pe"], i + 1)
                if i:
                    act.wait_ge(S_["h_st_pe"], i)
                s.activation(PT[:, 0, 0:SLAB], ps[:, 7, 0:SLAB], ACT.Copy).then_inc(S_["kt_ok"], 1)

            def h_out(i):
                act.wait_ge(S_["h_out_pe"], i + 1)
                s.activation(XM[:, i, 0:SLAB].rearrange("p (c e v) -> p c e v", c=3, e=2),
                             ps[:, 6, 0:SLAB].rearrange("p (c e v) -> p c e v", c=3, e=2),
                             ACT.Copy).then_inc(S_["h_out_ok"], 1)

            def d_s(n):
                act.wait_ge(S_["d_max"], n + 1)
                if n == 0:
                    act.wait_ge(S_["h_st_ok"], NT)
                    act.wait_ge(S_["h_out_pe"], NT)
                K = (n // HB + 1) * P
                if n >= 2:
                    act.wait_ge(S_["d_t_pe"], n - 1)
                for m in range(2):
                    last = s.activation(wk[:, n % 2, m * SEQ:m * SEQ + K], ps[:, 2 + 2 * (n % 2) + m, 0:K], ACT.Exp,
                                        bias=negm[:, 2 * (n % 2) + m:2 * (n % 2) + m + 1],
                                        accum_out=den[:, 2 * (n % 2) + m:2 * (n % 2) + m + 1])
                last.then_inc(S_["d_exp"], 1)

            def d_t(n):
                K = (n // HB + 1) * P
                act.wait_ge(S_["d_t_pe"], n + 1)
                if n >= 2:
                    act.wait_ge(S_["d_o_pe"], n - 1)
                s.activation(PT[:, n % 2, 0:K], ps[:, 6, 0:K], ACT.Copy).then_inc(S_["d_t_ok"], 1)

            def d_pv(n):
                i, h = divmod(n, HB)
                if h == HB - 1:
                    act.wait_ge(S_["d_o_pe"], n + 1)
                    s.activation(XM[:, i, SLAB:2 * SLAB], ps[:, 7, 0:SLAB], ACT.Copy).then_inc(S_["d_o_ok"], 1)

            def c_s(n):
                i, h = divmod(n, HC)
                K = (i + 1) * P
                K0 = min(i + 1, 2) * P
                act.wait_ge(S_["c_max"], n + 1)
                if n < 2:
                    act.wait_ge(S_["d_t_pe"], NT * HB)
                else:
                    act.wait_ge(S_["c_t_pe"], 1 + max(k for k in range(len(DG)) if DG[k][0] == n - 2))
                d = small[:, 128 + 8 * (i % 2) + 2 * h:130 + 8 * (i % 2) + 2 * h]
                if i >= 2 and h == 0:
                    act.wait_ge(S_["c_o_ok"], i - 1)
                W = wk[:, n % 2, :].rearrange("p (g k) -> p g k", g=3)
                b = negm[:, n % 2:n % 2 + 1]
                s.activation(W[:, 0, 0:K0], ps[:, 2, 0:K0], ACT.Exp, bias=b, accum_out=d[:, 0:1])
                s.activation(W[:, 1:3, 0:K], ps[:, 3:5, 0:K], ACT.Exp, bias=b,
                             accum_out=d[:, 1:2]).then_inc(S_["c_exp"], 1)

            def c_t(k):
                N = len(DG[k][1]) * P
                act.wait_ge(S_["c_t_pe"], k + 1)
                if k >= 2:
                    act.wait_ge(S_["c_o_pe"], k - 1)
                else:
                    act.wait_ge(S_["d_o_pe"], NT * HB)
                s.activation(PT[:, k % 2, 0:N], ps[:, 5 + k % 2, 0:N], ACT.Copy).then_inc(S_["c_t_ok"], 1)

            def krows(i):
                act.wait_ge(S_["kr_pe"], i + 1)
                if i == 0:
                    act.wait_ge(S_["c_t_pe"], len(DG))
                if i >= 2:
                    act.wait_ge(kr_out[i % 2], 16 * 3)
                w = SLAB + 256 * len(KROWS[i])
                s.activation(wk[:, i % 2, 0:w], ps[:, 2:5, :].rearrange("p b n -> p (b n)")[:, 0:w],
                             ACT.Copy).then_inc(S_["kr_ok"], 1)
                act.wait_ge(S_["kr_ok"], i + 1)
                act.dma_start(o["k_diff_prompt"][0, 0, i * P:(i + 1) * P].rearrange("t h m d -> t (h m d)"),
                              wk[:, i % 2, 0:SLAB]).then_inc(kr_out[i % 2], 16)
                for k, g in enumerate(KROWS[i]):
                    lo = i * P - (SEQ - WIN[g])
                    act.dma_start(o["win_prompt"][g][0, 0, lo:lo + P, 0].rearrange("t h d -> t (h d)"),
                                  wk[:, i % 2, SLAB + 256 * k:SLAB + 256 * (k + 1)]).then_inc(kr_out[i % 2], 16)

            def dec_soft():
                act.wait_ge(S_["row_ok"], 1)
                s.activation(RD, RD, ACT.Exp, bias=st96[:, 0:1], accum_out=st96[:, 1:2])
                s.activation(RC, RC, ACT.Exp, bias=st32[:, 0:1], accum_out=st32[:, 1:2]).then_inc(S_["row_e"], 1)

            def dec_state():
                s.activation(fex, bF[:, :, SEQ:NTOK], ACT.Exp).then_inc(S_["fx_ok"], 1)

            def ro(i):
                act.wait_ge(S_["ro_sq"], i + 1)
                q = small[:, 160 + 12 * (i % 2):172 + 12 * (i % 2)]
                seq(s.activation(q, q, ACT.Ln, bias=epsc, scale=1.0 / 64))
                s.activation(q, q, ACT.Exp, scale=-0.5).then_inc(S_["ro_e"], 1)

            def mt(i):
                r = tile_rows(i)
                act.wait_ge(S_["mt_pe"], i + 1)
                s.activation(xT[:, :, i * P:i * P + r],
                             ps[:, 0:2, :].rearrange("p b (c t) -> p (b c) t", c=4)[:, :, 0:r],
                             ACT.Copy).then_inc(S_["mt_ok"], 1)

            does = dict(proj=proj, samp_t=samp_t, prep=prep, lev_q=lev_q, io_a=io_a, kt=kt, h_out=h_out, d_s=d_s,
                        d_t=d_t, d_pv=d_pv, c_s=c_s, c_t=c_t, krows=krows, dec_soft=dec_soft, dec_state=dec_state,
                        ro=ro, mt=mt)
            for step, *arg in STEPS:
                if step in does:
                    does[step](*arg)

            def inv_rms(i, sem_name):
                r = tile_rows(i)
                seq(s.activation(PT[0:r].rearrange("p a n -> p (a n)"), XM[0:r, i, :], ACT.Square,
                                 accum_out=ssq[0:r, i:i + 1]))
                seq(s.activation(ssq[0:r, i:i + 1], ssq[0:r, i:i + 1], ACT.Ln, bias=epsc[0:r, :], scale=1.0 / D))
                s.activation(rstd[0:r, i:i + 1], ssq[0:r, i:i + 1], ACT.Exp, scale=-0.5).then_inc(S_[sem_name], 1)

            for i in range(T5):
                act.wait_ge(S_["hres_ok"], i + 1)
                inv_rms(i, "n2_e")
            act.wait_ge(S_["rt_e"], 1)
            s.activation(t4, t4, ACT.Exp).then_inc(S_["gexp"], 1)
            act.wait_ge(S_["rt_e"], 2)
            s.activation(e2, e2, ACT.Exp).then_inc(S_["gexp"], 1)

            act.wait_ge(S_["tab_rdy"], 1)
            npairs = act.value_load(npi[0:1, 0:1], min_val=NE // 2, max_val=MAXT // 2)
            last_pair = act.value_load(npi[0:1, 1:2], min_val=NE // 2 - 1, max_val=MAXT // 2 - 1)
            yrow = Yd.rearrange("(j p) n -> j p n", p=P)

            def silu(j1, b):
                act.wait_ge(S_["g_pe"], j1)
                if b is not None:
                    s.activation(hb[b], ps[:, 2 + 2 * b, :], ACT.Silu).then_inc(S_["sil_ok"], 1)

            def back(j1, j, b, n_st):
                act.wait_ge(S_["ht_pe"], j1)
                s.activation(dflat[:, (2 + b) * FF:(3 + b) * FF], ps[:, 2 + 2 * b, :], ACT.Copy).then_inc(S_["ht_ok"], 1)
                act.wait_ge(S_["y_pe"], j1)
                if n_st is not None:
                    act.wait_ge(ystore[b], n_st)
                s.activation(yb_[b][:, 0:FF], ps[:, 6, :], ACT.Copy).then_inc(S_["ya_ok"], 1)
                act.wait_ge(S_["ya_ok"], j1)
                act.wait_ge(S_["yb_ok"], j1)
                act.dma_start(yrow[j].rearrange("o p n -> p o n"), yb_[b].unsqueeze(1)).then_inc(ystore[b], 16)

            silu(1, 0)
            silu(2, 1)
            act.wait_ge(S_["u_st"], 16 * T5)
            back(1, slice(0, 1), 0, None)
            silu(3, 0)
            back(2, slice(1, 2), 1, None)
            with act.Fori(1, last_pair) as i:
                silu(2 * i + 2, 1)
                back(2 * i + 1, bass.ds(2 * i, 1), 0, i * 16)
                silu(2 * i + 3, 0)
                back(2 * i + 2, bass.ds(2 * i + 1, 1), 1, i * 16)
            silu(npairs * 2, 1)
            back(last_pair * 2 + 1, bass.ds(last_pair * 2, 1), 0, last_pair * 16)
            back(npairs * 2, bass.ds(last_pair * 2 + 1, 1), 1, last_pair * 16)

            def gate(i):
                r = tile_rows(i)
                act.wait_ge(S_["pg_pe"], i + 1)
                s.activation(sig[i % 2][0:r], ps[0:r, 4:6, :].rearrange("p b n -> p (b n)"),
                             ACT.Sigmoid).then_inc(S_["pg_sig"], 1)

            for i in range(T5):
                act.wait_ge(S_["comb_ok"], i + 1)
                inv_rms(i, "hn_e")
                if i:
                    gate(i - 1)
            gate(NT)
            for i in range(T5):
                act.wait_ge(S_["po_ok"], i + 1)
                inv_rms(i, "n4_e")

        @block.vector
        def _(dve):
            n = [0]
            v = nc.vector

            def seq(ins):
                n[0] += 1
                ins.then_inc(S_["dve_seq"], 1)
                dve.wait_ge(S_["dve_seq"], n[0])

            seq(v.memset(epsc, EPS))
            dve.wait_ge(S_["gain_pe"], 1)
            v.tensor_copy(gains[:], ps[:, 7, 0:27]).then_inc(S_["gain_ok"], 1)
            dve.wait_ge(S_["gain_ok"], 1)
            dve.wait_ge(S_["consts"], 3)
            dist = iT[:, 0, 0:P].bitcast(I32)
            rowi = iT[:, 0, P:2 * P].bitcast(I32)
            coli = iT[:, 0, 2 * P:3 * P].bitcast(I32)
            md = iT[:, 1, 0:P].bitcast(I32)
            xr = iT[:, 1, P:2 * P].bitcast(I32)
            lt = iT[:, 1, 2 * P:3 * P]
            xf = iT[:, 2, 0:P]
            ge = [iT[:, 2, P:2 * P], iT[:, 2, 2 * P:3 * P]]
            for k in range(2):
                seq(v.tensor_scalar(md, dist, (3, 15)[k], None, ALU.bitwise_and))
                seq(v.tensor_scalar(mstride[:, k, 0:P], md, 0.0, NEG, ALU.is_gt, ALU.mult))
                seq(v.tensor_copy(mstride[:, k, P:NT * P].rearrange("p (b n) -> p b n", b=NT - 1),
                                  mstride[:, k, 0:P].unsqueeze(1).to_broadcast([P, NT - 1, P])))
            seq(v.tensor_tensor(xr, rowi, coli, ALU.bitwise_xor))
            seq(v.tensor_tensor(lt, coli, rowi, ALU.is_gt))
            seq(v.tensor_tensor(xf, xr, lt, ALU.mult))
            seq(v.tensor_scalar(ge[0], xf, 1.0, None, ALU.is_ge))
            for l in range(LEVELS):
                seq(v.tensor_scalar(ge[(l + 1) % 2], xf, 2.0 ** (l + 1), None, ALU.is_ge))
                seq(v.tensor_tensor(lmask[:, l], ge[l % 2], ge[(l + 1) % 2], ALU.subtract))
            v.memset(small[:, 256:257], 0.0).then_inc(S_["tab_ok"], 1)
            for i in range(NT + 1):
                r = tile_rows(i)
                dve.wait_ge(S_["rstd_ok"], i + 1)
                v.tensor_scalar(XM[0:r, i, :], XM[0:r, i, :], rstd[0:r, i:i + 1], None,
                                ALU.mult).then_inc(S_["xn_ok"], 1)
                dve.wait_ge(S_["xt_pe"], i + 1)
                for h in range(2):
                    v.tensor_tensor(xT[:, 4 * h:4 * h + 4, i * P:i * P + r],
                                    ps[:, 2 * (i % 2) + h, :].rearrange("p (c t) -> p c t", c=4)[:, :, 0:r],
                                    f2(gains[:, 4 * h:4 * h + 4], r), ALU.mult).then_inc(S_["xt_ok"], 1)
            seq(v.memset(XM[:, NT, :], 0.0))
            seq(v.memset(gT[:, NT, :], 0.0))
            seq(v.tensor_tensor(lb, gains[:, 24:27], gains[:, 24:27], ALU.subtract))
            v.memset(tmp[:, 0:4], 0.0).then_inc(S_["lb_e"], 1)
            dve.wait_ge(S_["lb_ok"], 1)
            seq(v.reciprocal(omlb, lb))
            seq(v.tensor_tensor(lb, lb, omlb, ALU.mult))
            seq(v.tensor_tensor(lb, lb, lb, ALU.subtract))
            seq(v.tensor_scalar(omlb, lb, -1.0, 1.0, ALU.mult, ALU.add))
            dve.wait_ge(S_["cload"], 16 * 10)
            lv = lamb[:].rearrange("p (a b d) -> p a b d", a=2, b=2)
            seq(v.tensor_tensor(small[:, 320:384].rearrange("p (a d) -> p a d", a=2), lv[:, :, 0], lv[:, :, 1], ALU.mult))
            v.tensor_reduce(tmp[:, 0:2], small[:, 320:384].rearrange("p (a d) -> p a d", a=2), AX.X,
                            ALU.add).then_inc(S_["lam_s"], 1)
            dve.wait_ge(S_["lam_e"], 1)
            seq(v.tensor_tensor(lam, tmp[:, 0:1], tmp[:, 1:2], ALU.subtract))
            seq(v.tensor_scalar(lam, lam, LAM_INIT, None, ALU.add))
            seq(v.tensor_scalar(nlam, lam, -1.0, None, ALU.mult))
            seq(v.tensor_scalar(dg[:], dg[:], 1.0 - LAM_INIT, None, ALU.mult))

            def prep():
                dve.wait_ge(S_["prep_e"], 1)
                seq(v.tensor_scalar(kF, kF, 1.0, None, ALU.add))
                seq(v.reciprocal(kF, kF))
                v.scalar_tensor_tensor(out=qF, in0=qF, scalar=SCALE_A, in1=kF, op0=ALU.mult,
                                       op1=ALU.mult).then_inc(S_["prep_q"], 1)
                dve.wait_ge(S_["unit_ok"], LASTU[3] + 1)
                v.tensor_copy(gT[0:NS, NT, :], samp[:, 3 * SLAB:4 * SLAB]).then_inc(S_["gate_e"], 1)
                dve.wait_ge(S_["prep_e"], 2)
                seq(v.tensor_scalar(kF, kF, 1.0, None, ALU.add))
                seq(v.reciprocal(kF, kF))
                seq(v.tensor_tensor(kF, kF, f2(omlb, NTOK), ALU.mult))
                e = wk[:].rearrange("p a n -> p (a n)")[:, 0:5 * SLAB]
                gt = gT.rearrange("p i n -> p (i n)")
                dve.wait_ge(S_["gate_ok"], 1)
                seq(v.tensor_scalar(e, e, 1.0, None, ALU.add))
                seq(v.reciprocal(e, e))
                seq(v.tensor_tensor(gt, gt, e, ALU.mult))
                seq(v.tensor_tensor(gt.rearrange("p (h v) -> p h v", v=64), gt.rearrange("p (h v) -> p h v", v=64),
                                    hg[:].unsqueeze(1).to_broadcast([P, 30, 64]), ALU.mult))
                seq(v.tensor_scalar(bF, bF, 1.0, None, ALU.add))
                seq(v.reciprocal(bF, bF))
                for c in range(3):
                    fb = wk[:].rearrange("p a n -> p (a n)")[:, c * NTOK:(c + 1) * NTOK]
                    seq(v.tensor_scalar(bF[:, c], bF[:, c], omlb[:, c:c + 1], lb[:, c:c + 1], ALU.mult, ALU.add))
                    seq(v.tensor_scalar(bF[:, c], bF[:, c], float(np.finfo(np.float32).tiny), None, ALU.max))
                    seq(v.tensor_scalar(fb, bF[:, c], LN_SPLIT, 1.0 / LN_SPLIT, ALU.min, ALU.mult))
                    v.tensor_scalar(bF[:, c], bF[:, c], LN_SPLIT, None, ALU.max).then_inc(S_["prep_f"], 1)
                for c in range(3):
                    fb = wk[:].rearrange("p a n -> p (a n)")[:, c * NTOK:(c + 1) * NTOK]
                    dve.wait_ge(S_["prep_ln"], c + 1)
                    seq(v.tensor_tensor(bF[:, c], bF[:, c], fb, ALU.add))
                    for i in range(NT):
                        sl = bF[:, c, i * P:(i + 1) * P]
                        seq(v.tensor_tensor_scan(sl, ones[:], sl, 0.0, ALU.mult, ALU.add))
                v.memset(small[:, 257:258], 0.0).then_inc(S_["prep_ok"], 1)

            def lev_d(j):
                i, l = divmod(j, LEVELS)
                B = 2 ** l
                b4 = rows_of(bF, i).rearrange("p c (n w) -> p c n w", w=2 * B)
                N = P // (2 * B)
                out = work[:, (j % 2) * SLAB:(j % 2 + 1) * SLAB].rearrange("p (c n w) -> p c n w", c=3, n=N)
                if N == 1:
                    v.tensor_tensor(out[:, :, 0], b4[:, :, 0], f2(b4[:, :, 0, B - 1], 2 * B),
                                    ALU.subtract).then_inc(S_["lev_d"], 1)
                else:
                    v.tensor_tensor(out, b4, b4[:, :, :, B - 1:B].to_broadcast([P, 3, N, 2 * B]),
                                    ALU.subtract).then_inc(S_["lev_d"], 1)

            def lev_q(j):
                i, l = divmod(j, LEVELS)
                B = 2 ** l
                N = P // (2 * B)
                dve.wait_ge(S_["lev_e"], j + 1)
                if j >= 2:
                    i2, l2 = divmod(j - 2, LEVELS)
                    dve.wait_ge(S_["lev_pe"], i2 * (LEVELS + 1) + l2 + 2)
                E = work[:, (j % 2) * SLAB:(j % 2 + 1) * SLAB].rearrange("p (c n e t) -> p c n e t", c=3, n=N, e=2)
                QK = work[:, (2 + j % 2) * SLAB:(3 + j % 2) * SLAB].rearrange("p (c n e t) -> p c n e t", c=3, n=N, e=2)
                src = [rows_of(f, i).rearrange("p c (n e t) -> p c n e t", n=N, e=2) for f in (kF, qF)]
                for e in (0, 1):
                    o_, a_, b_ = QK[:, :, :, e], E[:, :, :, e], src[e][:, :, :, e]
                    if N == 1:
                        o_, a_, b_ = o_[:, :, 0], a_[:, :, 0], b_[:, :, 0]
                    last = v.tensor_tensor(o_, a_, b_, ALU.mult)
                last.then_inc(S_["lev_q"], 1)

            def lev_cp(i, l):
                k = i * (LEVELS + 1) + l
                dve.wait_ge(S_["lev_pe"], k + 1)
                if l == 0 and i:
                    dve.wait_ge(S_["h_out_pe"], i)
                for e in range(2):
                    att = work2[:, e * SLAB:(e + 1) * SLAB].rearrange("p (c t) -> p c t", c=3)
                    src = ps[:, 2 + 2 * (k % 2) + e, 0:SLAB].rearrange("p (c t) -> p c t", c=3)
                    if l == 0:
                        last = v.tensor_tensor(att, src, ident[:].unsqueeze(1).to_broadcast([P, 3, P]), ALU.mult)
                    else:
                        last = v.copy_predicated(att, lmask[:, l - 1].unsqueeze(1).to_broadcast([P, 3, P]), src)
                last.then_inc(S_["lev_cp"], 1)
                dve.wait_ge(S_["lev_cp"], k + 1)

            def io_a(i):
                if i:
                    dve.wait_ge(S_["kt_pe"], i)
                b = rows_of(bF, i)
                v.tensor_tensor(work2[:, 1152:1536].rearrange("p (c t) -> p c t", c=3), b,
                                f2(b[:, :, P - 1], P), ALU.subtract).then_inc(S_["io_d"], 1)

            def io_b(i):
                dve.wait_ge(S_["io_e"], i + 1)
                qI = work2[:, 768:1152].rearrange("p (c t) -> p c t", c=3)
                kI = work2[:, 1152:1536].rearrange("p (c t) -> p c t", c=3)
                seq(v.tensor_copy(ebl, qI[:, :, P - 1]))
                v.tensor_tensor(qI, qI, rows_of(qF, i), ALU.mult)
                v.tensor_tensor(kI, kI, rows_of(kF, i), ALU.mult).then_inc(S_["io_ok"], 1)

            def h_state(i):
                dve.wait_ge(S_["h_st_pe"], i + 1)
                src = ps[:, 7, 0:SLAB].rearrange("p (c n) -> p c n", c=3)
                bm = blk[:].unsqueeze(1).to_broadcast([P, 3, P])
                if i:
                    dve.wait_ge(S_["h_out_pe"], i + 1)
                    seq(v.tensor_tensor(Sadd, src, bm, ALU.mult))
                    seq(v.tensor_tensor(S, S, f2(ebl, P), ALU.mult))
                    v.tensor_tensor(S, S, Sadd, ALU.add).then_inc(S_["h_st_ok"], 1)
                else:
                    dve.wait_ge(S_["consts"], 5)
                    v.tensor_tensor(S, src, bm, ALU.mult).then_inc(S_["h_st_ok"], 1)
                dve.wait_ge(S_["h_st_ok"], i + 1)

            def d_s(n):
                K = (n // HB + 1) * P
                dve.wait_ge(S_["d_s_pe"], n + 1)
                if n >= 2:
                    dve.wait_ge(S_["d_exp"], n - 1)
                v.tensor_reduce(negm[:, 2 * (n % 2):2 * (n % 2) + 2], ps[:, 2 + 2 * (n % 2):4 + 2 * (n % 2), 0:K],
                                AX.X, ALU.max, negate=True).then_inc(S_["d_max"], 1)

            def d_t(n):
                K = (n // HB + 1) * P
                dve.wait_ge(S_["d_exp"], n + 1)
                r = rec[:, 2 * (n % 2):2 * (n % 2) + 2]
                W = wk[:, n % 2, :]
                seq(v.reciprocal(r, den[:, 2 * (n % 2):2 * (n % 2) + 2]))
                seq(v.tensor_scalar(r[:, 1:2], r[:, 1:2], nlam, None, ALU.mult))
                seq(v.tensor_scalar(W[:, 0:K], W[:, 0:K], r[:, 0:1], None, ALU.mult))
                v.scalar_tensor_tensor(out=W[:, 0:K], in0=W[:, SEQ:SEQ + K], scalar=r[:, 1:2], in1=W[:, 0:K],
                                       op0=ALU.mult, op1=ALU.add).then_inc(S_["d_a"], 1)

            def c_s(n):
                i, h = divmod(n, HC)
                K = (i + 1) * P
                K0 = min(i + 1, 2) * P
                dve.wait_ge(S_["c_s_pe"], n + 1)
                if n >= 2:
                    dve.wait_ge(S_["c_exp"], n - 1)
                v.tensor_reduce(tmp[:, 8:9], ps[:, 2, 0:K0], AX.X, ALU.max, negate=True)
                seq(v.tensor_reduce(tmp[:, 9:10], ps[:, 3:5, 0:K], AX.XY, ALU.max, negate=True))
                v.tensor_tensor(negm[:, n % 2:n % 2 + 1], tmp[:, 8:9], tmp[:, 9:10], ALU.min).then_inc(S_["c_max"], 1)
                dve.wait_ge(S_["c_max"], n + 1)

            def c_pv(k):
                n = DG[k][0]
                i, h = divmod(n, HC)
                if DG[k][3] and h == HC - 1:
                    dve.wait_ge(S_["c_exp"], n + 1)
                    d = small[:, 128 + 8 * (i % 2):136 + 8 * (i % 2)].rearrange("p (h e) -> p h e", e=2)
                    r = small[:, 144:148]
                    seq(v.tensor_tensor(r, d[:, :, 0], d[:, :, 1], ALU.add))
                    seq(v.reciprocal(r, r))
                    dve.wait_ge(S_["c_o_pe"], k + 1)
                    v.tensor_tensor(XM[:, i, 2 * SLAB:D].rearrange("p (h d) -> p h d", h=HC),
                                    ps[:, 7, 0:256].rearrange("p (h d) -> p h d", h=HC), f2(r, 64),
                                    ALU.mult).then_inc(S_["c_o_ok"], 1)

            samp3 = samp[:, C_COL:].rearrange("b (g s n) -> b g s n", g=NG, s=3)

            def dec_new():
                dve.wait_ge(S_["kr_pe"], NT)
                seq(v.tensor_reduce(hms, ident[0:96, 0:96].rearrange("p (b r) -> p r b", b=NS), AX.X, ALU.add))
                seq(v.tensor_reduce(mB, ident[0:96, 0:96].rearrange("p (b r) -> p b r", b=NS), AX.X, ALU.add))
                seq(v.tensor_reduce(hsel, ident[0:32, 0:32].rearrange("p (b r) -> p r b", b=NS), AX.X, ALU.add))
                seq(v.tensor_reduce(mC, ident[0:32, 0:32].rearrange("p (b r) -> p b r", b=NS), AX.X, ALU.add))
                seq(v.tensor_reduce(st96[:, 3:4], hms.rearrange("p (h m) -> p m h", m=2)[:, 1:2, :], AX.X, ALU.add))
                seq(v.tensor_scalar(st96[:, 4:5], lam[0:96, :], 1.0, None, ALU.add))
                seq(v.tensor_tensor(st96[:, 3:4], st96[:, 3:4], st96[:, 4:5], ALU.mult))
                seq(v.tensor_scalar(st96[:, 3:4], st96[:, 3:4], -1.0, 1.0, ALU.mult, ALU.add))
                seq(v.memset(id8, 0.0))
                seq(v.memset(id8[:, 0:64:9], 1.0))
                seq(v.tensor_tensor(dcst[:, 0:SLAB], samp[:, 4 * SLAB:5 * SLAB], samp[:, 5 * SLAB:6 * SLAB], ALU.mult))
                seq(v.tensor_reduce(snd, dcst[:, 0:SLAB].rearrange("p (r d) -> p r d", d=32), AX.X, ALU.add))
                for g in range(NG):
                    seq(v.tensor_tensor(dcst[:, 0:256], samp3[:, g, 0], samp3[:, g, 1], ALU.mult))
                    seq(v.tensor_reduce(snc[:, g], dcst[:, 0:256].rearrange("p (r d) -> p r d", d=64), AX.X, ALU.add))
                seq(v.tensor_tensor(MD.rearrange("p (b r) -> p b r", b=NS), snd.unsqueeze(1).to_broadcast([NS, NS, 12]),
                                    f2(ident[0:NS, 0:NS], 12), ALU.mult))
                for g in range(NG):
                    last = v.tensor_tensor(MC[:, g], snc[:, g].unsqueeze(1).to_broadcast([NS, NS, HC]),
                                           f2(ident[0:NS, 0:NS], HC), ALU.mult)
                last.then_inc(S_["new_ok"], 1)

            def dec_k(b):
                dve.wait_ge(S_["bq_pe"], b + 1)
                dve.wait_ge(kvload[b % 2], 16 * KPER * (b // 2 + 1))
                base = 2 + 3 * (b % 2)
                kp, kd = kpage[b % 2], kdil[b % 2]
                seq(v.tensor_tensor(kp, kp, ps[:, base, 0:SLAB].unsqueeze(1).to_broadcast([P, PAGES, SLAB]), ALU.mult))
                seq(v.tensor_tensor(kd[:, 0:2], kd[:, 0:2], ps[:, base + 1, :].rearrange("p (g n) -> p g n", g=2), ALU.mult))
                seq(v.tensor_tensor(kd[0:32, 2], kd[0:32, 2], ps[0:32, base + 2, 0:256], ALU.mult))
                v.tensor_reduce(SD[:, :, 12 * b:12 * b + 12], kp.rearrange("p j (r d) -> p j r d", d=32), AX.X, ALU.add)
                v.tensor_reduce(SC[:, 0:2, 4 * b:4 * b + 4], kd[:, 0:2].rearrange("p g (r d) -> p g r d", d=64), AX.X, ALU.add)
                v.tensor_reduce(SC[0:32, 2, 4 * b:4 * b + 4], kd[0:32, 2].rearrange("p (r d) -> p r d", d=64), AX.X,
                                ALU.add).then_inc(S_["kused"], 1)

            def dec_soft():
                dve.wait_ge(S_["sc_pe"], 1)
                dve.wait_ge(kr_out[0], 16 * 6)
                dve.wait_ge(kr_out[1], 16 * 7)
                seq(v.tensor_scalar(RD[:, 0:PAST], ps[0:96, 2, :], SCALE_B, None, ALU.mult))
                seq(v.tensor_scalar(RD[:, PAST:PAST + 1], ps[0:96, 4, 0:1], SCALE_B, None, ALU.mult))
                seq(v.tensor_scalar(RC[:, 0:NDIL], ps[0:32, 3, 0:NDIL], SCALE_C, None, ALU.mult))
                seq(v.tensor_scalar(RC[:, NDIL:NDIL + NG], ps[0:32, 4, 1:1 + NG], SCALE_C, None, ALU.mult))
                v.tensor_reduce(st96[:, 0:1], RD, AX.X, ALU.max, negate=True)
                v.tensor_reduce(st32[:, 0:1], RC, AX.X, ALU.max, negate=True).then_inc(S_["row_ok"], 1)
                dve.wait_ge(S_["row_e"], 1)
                seq(v.reciprocal(st96[:, 2:3], st96[:, 1:2]))
                seq(v.reciprocal(st32[:, 2:3], st32[:, 1:2]))
                seq(v.tensor_tensor(st96[:, 2:3], st96[:, 2:3], st96[:, 3:4], ALU.mult))
                seq(v.tensor_scalar(RD, RD, st96[:, 2:3], None, ALU.mult))
                seq(v.tensor_scalar(RC, RC, st32[:, 2:3], None, ALU.mult))
                seq(v.tensor_scalar(LD, mB, RD[:, PAST:PAST + 1], None, ALU.mult))
                for g in range(NG):
                    last = v.tensor_scalar(LC[:, g], mC, RC[:, NDIL + g:NDIL + g + 1], None, ALU.mult)
                last.then_inc(S_["w_ok"], 1)
                dve.wait_ge(S_["wt_pe"], 1)
                v.tensor_reduce(AD, ps[:, 2, 0:384].rearrange("p (j r m) -> p j r m", j=PAGES, m=2), AX.X, ALU.add)
                v.tensor_copy(AC[:, 0:2], ps[:, 3, 0:64].rearrange("p (g r) -> p g r", g=2))
                v.tensor_copy(AC[0:32, 2], ps[0:32, 3, 64:96])
                v.tensor_reduce(anew[:, 0:6], ps[0:NS, 4, 0:12].rearrange("p (h m) -> p h m", m=2), AX.X, ALU.add)
                v.tensor_copy(anew[:, 8:20], ps[0:NS, 5, 0:12]).then_inc(S_["aw_ok"], 1)

            def dec_state():
                dve.wait_ge(S_["stload"], 16 * 6)
                for b in range(NS):
                    dve.wait_ge(S_["vb_pe"], b + 1)
                    vb = ps[:, 6 + b % 2, 0:SLAB].rearrange("p (c e v) -> p c e v", c=3, e=2)
                    for e in range(2):
                        h = slice(64 * e, 64 * e + 64)
                        last = v.tensor_tensor(stK[h, b], vb[h, :, e],
                                               f2(kF[h, :, SEQ + b], 64), ALU.mult)
                    last.then_inc(S_["kv_ok"], 1)
                dve.wait_ge(S_["kv_ok"], NS)
                dve.wait_ge(S_["fx_ok"], 1)
                for c in range(3):
                    seq(v.tensor_tensor(stS[:, :, c], stS[:, :, c], f2(fex[:, c], 64), ALU.mult))
                seq(v.tensor_tensor(Qz, id8.rearrange("p (b e) -> p b e", b=NS).unsqueeze(1).to_broadcast([P, 3, NS, NS]),
                                    qF[:, :, SEQ:NTOK].unsqueeze(3).to_broadcast([P, 3, NS, NS]), ALU.mult))
                v.tensor_tensor(stS, stS, stK, ALU.add).then_inc(S_["s_new"], 1)
                dve.wait_ge(S_["s_o_pe"], 1)
                for e in range(2):
                    seq(v.tensor_copy(XM[0:NS, NT, 0:SLAB].rearrange("p (c e v) -> p c e v", c=3, e=2)[:, :, e],
                                      ps[0:NS, 6 + e, 0:192].rearrange("p (c v) -> p c v", c=3)))

            def dec_out():
                dve.wait_ge(S_["vused"], NS)
                for e in range(2):
                    h = slice(64 * e, 64 * e + 64)
                    v.tensor_copy(oDF[h], ps[h, 2, 0:48].rearrange("p (c b e) -> p c b e", c=3, b=NS)[:, :, :, e])
                    last = v.tensor_copy(oCF[h], ps[h, 3, 0:32].rearrange("p (c b e) -> p c b e", c=2, b=NS)[:, :, :, e])
                last.then_inc(S_["of_ok"], 1)
                dve.wait_ge(S_["ot_pe"], 1)
                md = dcst[:, 0:SLAB].rearrange("p (h d) -> p h d", h=HB)
                seq(v.tensor_tensor(md, samp[:, 6 * SLAB:7 * SLAB].rearrange("p (h d) -> p h d", h=HB),
                                    f2(anew[:, 0:6], 64), ALU.mult))
                seq(v.tensor_tensor(XM[0:NS, NT, SLAB:2 * SLAB], dcst[:, 0:SLAB], ps[0:NS, 4, 0:SLAB], ALU.add))
                out = XM[0:NS, NT, 2 * SLAB:D]
                seq(v.tensor_copy(out, ps[0:NS, 5, 0:256]))
                for g in range(NG):
                    seq(v.tensor_tensor(dcst[:, 0:256].rearrange("p (h d) -> p h d", h=HC),
                                        samp3[:, g, 2].rearrange("p (h d) -> p h d", h=HC),
                                        f2(anew[:, 8 + 4 * g:12 + 4 * g], 64), ALU.mult))
                    ins = v.tensor_tensor(out, out, dcst[:, 0:256], ALU.add)
                    if g < NG - 1:
                        seq(ins)
                ins.then_inc(S_["dec_done"], 1)
                dve.wait_ge(S_["dec_done"], 1)

            def ro(i):
                r = P
                if i < NT:
                    dve.wait_ge(S_["h_out_ok"], i + 1)
                    dve.wait_ge(S_["d_o_ok"], i + 1)
                if i == 0:
                    dve.wait_ge(S_["c_o_pe"], len(DG))
                q = small[:, 160 + 12 * (i % 2):172 + 12 * (i % 2)]
                X = XM[:, i, 0:2 * SLAB]
                sq = PT[:].rearrange("p a n -> p (a n)")[:, 0:2 * SLAB]
                X3 = X.rearrange("p (h v) -> p h v", h=12)
                seq(v.tensor_tensor(sq, X, X, ALU.mult))
                v.tensor_reduce(q, sq.rearrange("p (h v) -> p h v", h=12), AX.X, ALU.add).then_inc(S_["ro_sq"], 1)
                dve.wait_ge(S_["ro_e"], i + 1)
                seq(v.tensor_tensor(X3, X3, f2(q, 64), ALU.mult))
                v.tensor_tensor(X[:, 0:SLAB], X[:, 0:SLAB], gT[:, i], ALU.mult)
                v.tensor_tensor(X3[:, 6:12], X3[:, 6:12], dg[:].unsqueeze(1).to_broadcast([P, 6, 64]),
                                ALU.mult).then_inc(S_["ro_ok"], 1)

            def finish(i):
                r = tile_rows(i)
                b = i % 2
                dve.wait_ge(S_["pg_sig"], i + 1)
                seq(v.tensor_tensor(sig[b][0:r], sig[b][0:r], ps[0:r, 6:8, :].rearrange("p b n -> p (b n)"), ALU.mult))
                v.tensor_tensor(XM[0:r, i, :], XM[0:r, i, :], sig[b][0:r], ALU.add).then_inc(S_["po_ok"], 1)

            def last_norm(i):
                r = tile_rows(i)
                dve.wait_ge(S_["n4_e"], i + 1)
                dve.wait_ge(S_["pleload"], 48)
                v.scalar_tensor_tensor(out=XM[0:r, i, :], in0=XM[0:r, i, :], scalar=rstd[0:r, i:i + 1],
                                       in1=nfin[0:r, :], op0=ALU.mult, op1=ALU.mult).then_inc(S_["y_ok"], 1)

            does = dict(prep=prep, lev_d=lev_d, lev_q=lev_q, lev_cp=lev_cp, io_a=io_a, io_b=io_b, h_state=h_state,
                        d_s=d_s, d_t=d_t, c_s=c_s, c_pv=c_pv, dec_new=dec_new, dec_k=dec_k, dec_soft=dec_soft,
                        dec_state=dec_state, dec_out=dec_out, ro=ro)
            for step, *arg in STEPS:
                if step in does:
                    does[step](*arg)

            for i in range(T5):
                r = tile_rows(i)
                bk = 2 + 2 * (i % 2)
                dve.wait_ge(xload[i], 32)
                dve.wait_ge(S_["wo_pe"], i + 1)
                v.tensor_tensor(XM[0:r, i, :], XM[0:r, i, :], ps[0:r, bk:bk + 2, :].rearrange("p b n -> p (b n)"),
                                ALU.add).then_inc(S_["hres_ok"], 1)
                dve.wait_ge(S_["n2_e"], i + 1)
                if i >= 3:
                    dve.wait_ge(S_["u_st"], 16 * i)
                    dve.wait_ge(S_["ut_pe"], i - 2)
                if i == 0:
                    dve.wait_ge(kr_out[0], 16 * 6)
                    dve.wait_ge(kr_out[1], 16 * 7)
                v.tensor_scalar(Ub[i % 3][0:r, :], XM[0:r, i, :], rstd[0:r, i:i + 1], None,
                                ALU.mult).then_inc(S_["u_ok"], 1)
                dve.wait_ge(S_["ut_pe"], i + 1)
                if i >= 4:
                    dve.wait_ge(S_["rl_pe"], i - 3)
                v.tensor_tensor(RT[i % 4][:, :, 0:r], ps[:, 6:8, :].rearrange("p b (c t) -> p (b c) t", c=4)[:, :, 0:r],
                                f2(gains[:, 8:16], r), ALU.mult).then_inc(S_["ut_ok"], 1)
            dve.wait_ge(S_["iot"], 1)
            dve.wait_ge(S_["rl_pe"], T5)
            seq(v.tensor_tensor(L[:, 0:NT], ps[:, 0, 0:80].rearrange("p (i n) -> p i n", i=NT),
                                rbias[:].unsqueeze(1).to_broadcast([P, NT, 20]), ALU.add))
            seq(v.tensor_tensor(L[0:NS, NT], ps[0:NS, 0, 80:100], rbias[0:NS, :], ALU.add))
            seq(v.tensor_copy(erow, iti[:, 0:NE]))
            seq(v.tensor_copy(jrow, iti[:, 0:4]))
            seq(v.tensor_copy(xrow, iti[:, 0:8]))
            seq(v.tensor_copy(tokf, toki))
            gl = L[:, :, 0:4]
            el = L[:, :, 4:20].rearrange("p i (g e) -> p i g e", g=NGRP)

            def onehot(out, vals, best, tmp4):
                seq(v.tensor_reduce(best, vals, AX.X, ALU.max))
                seq(v.tensor_tensor(tmp4, vals, f2(best, 4), ALU.is_equal))
                seq(v.scalar_tensor_tensor(out=tmp4, in0=tmp4, scalar=-1000.0,
                                           in1=jrow.unsqueeze(1).to_broadcast([P, T5, 4]), op0=ALU.mult, op1=ALU.add))
                seq(v.tensor_reduce(mn, tmp4, AX.X, ALU.min))
                seq(v.tensor_tensor(out, tmp4, f2(mn, 4), ALU.is_equal))

            onehot(og, gl, gm, t4)
            v.tensor_tensor(t4, gl, f2(gm, 4), ALU.subtract).then_inc(S_["rt_e"], 1)
            t44 = t16.rearrange("p i (g e) -> p i g e", g=NGRP)
            seq(v.tensor_tensor(t44, el, og.unsqueeze(3).to_broadcast([P, T5, 4, 4]), ALU.mult))
            seq(v.tensor_reduce(es, t44.rearrange("p i g e -> p i e g"), AX.X, ALU.add))
            dve.wait_ge(S_["gexp"], 1)
            seq(v.tensor_reduce(gs, t4, AX.X, ALU.add))
            seq(v.reciprocal(gw, gs))
            onehot(o1, es, m1, t4)
            seq(v.scalar_tensor_tensor(out=es2, in0=o1, scalar=-BIG, in1=es, op0=ALU.mult, op1=ALU.add))
            onehot(o2, es2, m2, t4)
            v.tensor_tensor(e2, m2, m1, ALU.subtract).then_inc(S_["rt_e"], 1)
            for O, o_ in ((O1, o1), (O2, o2)):
                seq(v.tensor_tensor(O.rearrange("p i (g e) -> p i g e", g=NGRP), og.unsqueeze(3).to_broadcast([P, T5, 4, 4]),
                                    o_.unsqueeze(2).to_broadcast([P, T5, 4, 4]), ALU.mult))
            seq(v.tensor_scalar(mn, tokf, float(NTOK), None, ALU.is_lt))
            seq(v.tensor_tensor(C, O1, O2, ALU.add))
            v.tensor_tensor(C, C, f2(mn, NE), ALU.mult).then_inc(S_["c_ok"], 1)
            dve.wait_ge(S_["gexp"], 2)
            seq(v.tensor_scalar(gs, e2, 1.0, None, ALU.add))
            seq(v.reciprocal(w1, gs))
            seq(v.tensor_tensor(w1, w1, gw, ALU.mult))
            seq(v.tensor_tensor(w2, w1, e2, ALU.mult))
            dve.wait_ge(S_["rank_pe"], 1)
            seq(v.tensor_copy(rank, ps[:, 1, 0:T5 * NE].rearrange("p (i e) -> p i e", i=T5)))
            seq(v.tensor_copy(cnt, ps[:, 1, T5 * NE:(T5 + 1) * NE]))
            seq(v.tensor_scalar(nx, cnt, float(P), None, ALU.is_gt))
            for k in range(2, (NTOK + P - 1) // P):
                seq(v.scalar_tensor_tensor(out=nx, in0=cnt, scalar=float(k * P), in1=nx, op0=ALU.is_gt, op1=ALU.add))
            for k in range(1, (NTOK + P - 1) // P):
                seq(v.scalar_tensor_tensor(out=q_, in0=rank, scalar=float(k * P), in1=q_, op0=ALU.is_ge, op1=ALU.add))
            seq(v.tensor_tensor_scan(incl, ones[:, 0:NE], nx, 0.0, ALU.mult, ALU.add))
            seq(v.tensor_tensor(exc, incl, nx, ALU.subtract))
            seq(v.scalar_tensor_tensor(out=exc, in0=exc, scalar=float(NE - 1), in1=erow, op0=ALU.add, op1=ALU.subtract))
            eb = exc.unsqueeze(1).to_broadcast([P, T5, NE])
            seq(v.tensor_tensor(tl, q_, eb, ALU.add))
            seq(v.tensor_scalar(t16, q_, 1.0, None, ALU.min))
            seq(v.tensor_tensor(tl, tl, t16, ALU.mult))
            seq(v.tensor_tensor(tl, tl, erow.unsqueeze(1).to_broadcast([P, T5, NE]), ALU.add))
            seq(v.scalar_tensor_tensor(out=rank, in0=q_, scalar=-float(P), in1=rank, op0=ALU.mult, op1=ALU.add))
            seq(v.scalar_tensor_tensor(out=slotY, in0=tl, scalar=float(P), in1=rank, op0=ALU.mult, op1=ALU.add))
            seq(v.scalar_tensor_tensor(out=slotL, in0=rank, scalar=float(MAXT), in1=tl, op0=ALU.mult, op1=ALU.add))
            for k, (O, sl) in enumerate(((O1, slotY), (O2, slotY), (O1, slotL), (O2, slotL))):
                seq(v.tensor_tensor(t16, O, sl, ALU.mult))
                seq(v.tensor_reduce(sel[:, k], t16, AX.X, ALU.add))
            v.tensor_copy(seli, sel).then_inc(S_["rank_ok"], 1)
            seq(v.tensor_tensor(xcmp, incl.unsqueeze(1).to_broadcast([P, 8, NE]), f2(xrow, NE), ALU.is_le))
            seq(v.tensor_reduce(tabf[:, NE:MAXT], xcmp, AX.X, ALU.add))
            seq(v.tensor_scalar(tabf[:, NE:MAXT], tabf[:, NE:MAXT], float(NE - 1), None, ALU.min))
            seq(v.tensor_copy(tabf[:, 0:NE], erow))
            seq(v.tensor_copy(tabi, tabf))
            seq(v.memset(npf, NE / 2))
            for k in range((MAXT - NE) // 2):
                seq(v.scalar_tensor_tensor(out=npf[:, 0:1], in0=incl[:, NE - 1:NE], scalar=float(2 * k), in1=npf[:, 0:1],
                                           op0=ALU.is_gt, op1=ALU.add))
            seq(v.tensor_scalar(npf[:, 1:2], npf[:, 0:1], -1.0, None, ALU.add))
            v.tensor_copy(npi, npf).then_inc(S_["tab_rdy"], 1)
            dve.wait_ge(S_["tab_rdy"], 1)
            npairs = dve.value_load(npi[0:1, 0:1], min_val=NE // 2, max_val=MAXT // 2)
            last_pair = dve.value_load(npi[0:1, 1:2], min_val=NE // 2 - 1, max_val=MAXT // 2 - 1)

            def front(j1, b):
                dve.wait_ge(S_["mx_pe"], j1)
                v.tensor_tensor(xgT[b], ps[:, 0:2, :].rearrange("p b (c t) -> p (b c) t", c=4),
                                f2(gains[:, 8:16], P), ALU.mult).then_inc(S_["mx_ok"], 1)

            def product(j1, b):
                dve.wait_ge(S_["sil_ok"], j1)
                dve.wait_ge(S_["u_pe"], j1)
                v.tensor_tensor(hb[b], hb[b], ps[:, 3 + 2 * b, :], ALU.mult).then_inc(S_["h_ok"], 1)

            def yhalf(j1, b, n_st):
                dve.wait_ge(S_["y_pe"], j1)
                if n_st is not None:
                    dve.wait_ge(ystore[b], n_st)
                v.tensor_copy(yb_[b][:, FF:D], ps[:, 7, :]).then_inc(S_["yb_ok"], 1)

            front(1, 0)
            front(2, 1)
            product(1, 0)
            front(3, 0)
            product(2, 1)
            dve.wait_ge(S_["u_st"], 16 * T5)
            yhalf(1, 0, None)
            front(4, 1)
            product(3, 0)
            yhalf(2, 1, None)
            with dve.Fori(1, last_pair) as i:
                front(2 * i + 3, 0)
                product(2 * i + 2, 1)
                yhalf(2 * i + 1, 0, i * 16)
                front(2 * i + 4, 1)
                product(2 * i + 3, 0)
                yhalf(2 * i + 2, 1, i * 16)
            product(npairs * 2, 1)
            yhalf(last_pair * 2 + 1, 0, last_pair * 16)
            yhalf(npairs * 2, 1, last_pair * 16)

            for i in range(T5):
                r = tile_rows(i)
                dve.wait_ge(yload[i % 2], 32 * (i // 2 + 1))
                seq(v.scalar_tensor_tensor(out=XM[0:r, i, :], in0=ybuf[i % 2][0][0:r, :], scalar=w1[0:r, i:i + 1],
                                           in1=XM[0:r, i, :], op0=ALU.mult, op1=ALU.add))
                v.scalar_tensor_tensor(out=XM[0:r, i, :], in0=ybuf[i % 2][1][0:r, :], scalar=w2[0:r, i:i + 1],
                                       in1=XM[0:r, i, :], op0=ALU.mult, op1=ALU.add).then_inc(S_["comb_ok"], 1)
                dve.wait_ge(S_["hn_e"], i + 1)
                if i == 0:
                    for b in range(2):
                        dve.wait_ge(ystore[b], npairs * 16)
                if i >= 3:
                    dve.wait_ge(S_["hnt_pe"], i - 2)
                v.tensor_scalar(Ub[i % 3][0:r, :], XM[0:r, i, :], rstd[0:r, i:i + 1], None,
                                ALU.mult).then_inc(S_["hn_ok"], 1)
                dve.wait_ge(S_["hnt_pe"], i + 1)
                if i >= 2:
                    dve.wait_ge(S_["pg_pe"], i - 1)
                v.tensor_tensor(hnT[i % 2][:, :, 0:r], ps[:, 0:2, :].rearrange("p b (c t) -> p (b c) t", c=4)[:, :, 0:r],
                                f2(gains[:, 16:24], r), ALU.mult)
                v.tensor_copy(pTt[i % 2][:, :, 0:r],
                              ps[:, 2, 0:2 * P].rearrange("p (c t) -> p c t", c=PC)[:, :, 0:r]).then_inc(S_["hnt_ok"], 1)
                if i:
                    finish(i - 1)
            finish(NT)
            for i in range(T5):
                last_norm(i)

        @block.tensor
        def _(pe):
            t = nc.tensor
            pe.wait_ge(S_["consts"], 2)
            pe.wait_ge(S_["cload"], 16 * 10)
            t.transpose(ps[:, 7, 0:27], work2[0:27, 0:P], ident[0:27, 0:27]).then_inc(S_["gain_pe"], 1)
            for i in range(NT + 1):
                r = tile_rows(i)
                pe.wait_ge(S_["xn_ok"], i + 1)
                if i >= 2:
                    pe.wait_ge(S_["xt_ok"], 2 * (i - 1))
                for c in range(DC):
                    last = t.transpose(ps[:, 2 * (i % 2) + c // 4, (c % 4) * P:(c % 4) * P + r],
                                       XM[0:r, i, c * P:(c + 1) * P], ident[0:r, 0:r])
                last.then_inc(S_["xt_pe"], 1)
            pe.wait_ge(S_["xt_ok"], 2 * (NT + 1))

            def proj(u):
                kind, sl, c0, w, at = UNITS[u]
                pe.wait_ge(slabload[sl % 2], 16 * (sl // 2 + 1))
                if u >= 2:
                    pe.wait_ge(S_["unit_ok"], u - 1)
                for c in range(DC):
                    if kind == "FM":
                        last = t.matmul(ps[:, u % 2, :], slab[sl % 2][:, c, c0:c0 + w], xT[:, c, 0:SEQ],
                                        start=(c == 0), stop=(c == DC - 1))
                    elif kind == "TM":
                        i = at[1]
                        last = t.matmul(ps[:, u % 2, 0:w], xT[:, c, i * P:(i + 1) * P],
                                        slab[sl % 2][:, c, c0:c0 + w], start=(c == 0), stop=(c == DC - 1))
                    else:
                        last = t.matmul(ps[0:NS, u % 2, 0:w], xT[:, c, SEQ:NTOK],
                                        slab[sl % 2][:, c, :], start=(c == 0), stop=(c == DC - 1))
                last.then_inc(S_["unit_pe"], 1)

            def samp_t():
                pe.wait_ge(S_["unit_ok"], LASTU[3] + 1)
                for c in range(6):
                    last = t.transpose(ps[:, 2, 8 * c:8 * c + 8], samp[:, c * P:(c + 1) * P], ident[0:NS, 0:NS])
                last.then_inc(S_["samp_t_pe"], 1)

            def lev_mm(i, l):
                k = i * (LEVELS + 1) + l
                if l == 0:
                    pe.wait_ge(S_["prep_ok"], 1)
                    L, R = kF, qF
                    L, R = rows_of(L, i), rows_of(R, i)
                else:
                    j = i * LEVELS + l - 1
                    pe.wait_ge(S_["lev_q"], j + 1)
                    L = R = work[:, (2 + j % 2) * SLAB:(3 + j % 2) * SLAB].rearrange("p (c t) -> p c t", c=3)
                if k >= 2:
                    pe.wait_ge(S_["lev_cp"], k - 1)
                for e in range(2):
                    h = slice(64 * e, 64 * e + 64)
                    for c in range(3):
                        last = t.matmul(ps[:, 2 + 2 * (k % 2) + e, c * P:(c + 1) * P], L[h, c, :], R[h, c, :],
                                        start=True, stop=True)
                last.then_inc(S_["lev_pe"], 1)

            def kt(i):
                pe.wait_ge(S_["io_ok"], i + 1)
                if i:
                    pe.wait_ge(S_["h_st_ok"], i)
                for c in range(3):
                    last = t.transpose(ps[:, 7, c * P:(c + 1) * P], work2[:, 1152 + c * P:1152 + (c + 1) * P], ident[:])
                last.then_inc(S_["kt_pe"], 1)

            def h_out(i):
                pe.wait_ge(S_["lev_cp"], (i + 1) * (LEVELS + 1))
                if i:
                    pe.wait_ge(S_["h_out_ok"], i)
                    pe.wait_ge(S_["h_st_ok"], i)
                for c in range(3):
                    for e in range(2):
                        h = 2 * c + e
                        if i:
                            t.matmul(ps[:, 6, h * 64:h * 64 + 64], work2[:, 768 + c * P:768 + (c + 1) * P],
                                     S[:, c, e * 64:e * 64 + 64], start=True, stop=False)
                        last = t.matmul(ps[:, 6, h * 64:h * 64 + 64], work2[:, e * SLAB + c * P:e * SLAB + (c + 1) * P],
                                        iT[:, i, h * 64:h * 64 + 64], start=(i == 0), stop=True)
                last.then_inc(S_["h_out_pe"], 1)

            def h_state(i):
                pe.wait_ge(S_["kt_ok"], i + 1)
                for c in range(3):
                    last = t.matmul(ps[:, 7, c * P:(c + 1) * P], PT[:, 0, c * P:(c + 1) * P],
                                    iT[:, i, c * P:(c + 1) * P], start=True, stop=True)
                last.then_inc(S_["h_st_pe"], 1)

            def d_s(n):
                i, h = divmod(n, HB)
                K = (i + 1) * P
                if n == 0:
                    pe.wait_ge(S_["unit_ok"], LASTU[6] + 1)
                    pe.wait_ge(S_["consts"], 6)
                    pe.wait_ge(S_["lev_cp"], NT * (LEVELS + 1))
                if n >= 2:
                    pe.wait_ge(S_["d_exp"], n - 1)
                c, e = divmod(h, 2)
                for m in range(2):
                    r = slice(64 * e + 32 * m, 64 * e + 32 * m + 32)
                    bank = 2 + 2 * (n % 2) + m
                    q = dF[r, 0, c, i * P:(i + 1) * P]
                    if i:
                        t.matmul(ps[:, bank, 0:i * P], q, dF[r, 1, c, 0:i * P], start=True, stop=True)
                    t.matmul(ps[:, bank, i * P:K], q, dF[r, 1, c, i * P:K], start=True, stop=False)
                    last = t.matmul(ps[:, bank, i * P:K], identb[:], mband[:, P:2 * P], start=False, stop=True)
                last.then_inc(S_["d_s_pe"], 1)

            def d_t(n):
                i = n // HB
                pe.wait_ge(S_["d_a"], n + 1)
                if n >= 1:
                    pe.wait_ge(S_["d_t_ok"], n)
                else:
                    pe.wait_ge(S_["h_out_ok"], NT)
                for k in range(i + 1):
                    last = t.transpose(ps[:, 6, k * P:(k + 1) * P], wk[:, n % 2, k * P:(k + 1) * P], ident[:])
                last.then_inc(S_["d_t_pe"], 1)

            def d_pv(n):
                i, h = divmod(n, HB)
                pe.wait_ge(S_["d_t_ok"], n + 1)
                if h == 0:
                    if i:
                        pe.wait_ge(S_["d_o_ok"], i)
                    else:
                        pe.wait_ge(S_["h_st_ok"], NT)
                for k in range(i + 1):
                    last = t.matmul(ps[:, 7, h * 64:h * 64 + 64], PT[:, n % 2, k * P:(k + 1) * P],
                                    bvT[:, k, h * 64:h * 64 + 64], start=(k == 0), stop=(k == i))
                last.then_inc(S_["d_o_pe"], 1)

            def c_s(n):
                i, h = divmod(n, HC)
                K = (i + 1) * P
                lo = max(i - 1, 0) * P
                if n == 0:
                    pe.wait_ge(S_["unit_ok"], NU)
                    pe.wait_ge(S_["d_exp"], NT * HB)
                else:
                    pe.wait_ge(S_["c_exp"], n)
                c, e = divmod(h, 2)
                r = slice(64 * e, 64 * e + 64)
                for g in range(NG):
                    k0 = lo if g == 0 else 0
                    q, k = cF[r, g, c, i * P:K], cF[r, g, 2 + c, k0:K]
                    mk = mband[:, 2 * P - (K - k0):2 * P] if g == 0 else mstride[:, g - 1, (NT - 1 - i) * P:NT * P]
                    t.matmul(ps[:, 2 + g, 0:K - k0], q, k, start=True, stop=False)
                    last = t.matmul(ps[:, 2 + g, 0:K - k0], identb[:], mk, start=False, stop=True)
                last.then_inc(S_["c_s_pe"], 1)

            def c_t(k):
                n, blocks, _, _ = DG[k]
                pe.wait_ge(S_["c_exp"], n + 1)
                if k >= 2:
                    pe.wait_ge(S_["c_t_ok"], k - 1)
                else:
                    pe.wait_ge(S_["d_t_ok"], NT * HB)
                for x, (g, kt_, col) in enumerate(blocks):
                    last = t.transpose(ps[:, 5 + k % 2, x * P:(x + 1) * P], wk[:, n % 2, col:col + P], ident[:])
                last.then_inc(S_["c_t_pe"], 1)

            def c_pv(k):
                n, blocks, first, final = DG[k]
                i, h = divmod(n, HC)
                pe.wait_ge(S_["c_t_ok"], k + 1)
                if first and h == 0:
                    if i:
                        pe.wait_ge(S_["c_o_ok"], i)
                    else:
                        pe.wait_ge(S_["d_o_ok"], NT)
                for x, (g, kt_, col) in enumerate(blocks):
                    last = t.matmul(ps[:, 7, h * 64:h * 64 + 64], PT[:, k % 2, x * P:(x + 1) * P],
                                    cvT[:, g, kt_, h * 64:h * 64 + 64], start=(first and x == 0),
                                    stop=(final and x == len(blocks) - 1))
                last.then_inc(S_["c_o_pe"], 1)

            def krows(i):
                if i == 0:
                    pe.wait_ge(S_["c_exp"], NT * HC)
                else:
                    pe.wait_ge(S_["kr_ok"], i)
                blocks = [dF[:, 1, c, i * P:(i + 1) * P] for c in range(3)]
                for g in KROWS[i]:
                    blocks += [cF[:, g, 2 + c, i * P:(i + 1) * P] for c in range(2)]
                for k, b in enumerate(blocks):
                    last = t.transpose(ps[:, 2 + k // 4, (k % 4) * P:(k % 4 + 1) * P], b, ident[:])
                last.then_inc(S_["kr_pe"], 1)

            def dec_k(b):
                if b == 0:
                    pe.wait_ge(S_["kr_ok"], NT)
                    pe.wait_ge(S_["c_o_ok"], NT)
                if b >= 2:
                    pe.wait_ge(S_["kused"], b - 1)
                one = ident[0:NS, b:b + 1].to_broadcast([NS, P])
                base = 2 + 3 * (b % 2)
                t.matmul(ps[:, base, 0:SLAB], one, samp[:, 4 * SLAB:5 * SLAB], start=True, stop=True)
                q = samp[:, C_COL:].rearrange("b (g s n) -> b g s n", g=NG, s=3)
                for g in range(NG):
                    last = t.matmul(ps[:, base + 1 + g // 2, (g % 2) * 256:(g % 2) * 256 + 256], one, q[:, g, 0],
                                    start=True, stop=True)
                last.then_inc(S_["bq_pe"], 1)

            def dec_soft():
                pe.wait_ge(S_["kused"], NS)
                pe.wait_ge(S_["new_ok"], 1)
                for j in range(PAGES):
                    t.transpose(ps[0:96, 2, j * P:(j + 1) * P], SD[:, j, :], ident[:])
                t.transpose(ps[0:32, 3, 0:P], SC[:, 0, :], ident[:])
                t.transpose(ps[0:32, 3, P:2 * P], SC[:, 1, :], ident[:])
                t.transpose(ps[0:32, 3, 2 * P:2 * P + 32], SC[0:32, 2, :], ident[0:32, 0:32])
                t.matmul(ps[0:96, 4, 0:1], MD, ones[0:NS, 0:1], start=True, stop=True)
                for g in range(NG):
                    last = t.matmul(ps[0:32, 4, 1 + g:2 + g], MC[:, g].rearrange("p b h -> p (b h)"), ones[0:NS, 0:1],
                                    start=True, stop=True)
                last.then_inc(S_["sc_pe"], 1)
                pe.wait_ge(S_["w_ok"], 1)
                for j in range(PAGES):
                    t.transpose(ps[:, 2, j * 96:(j + 1) * 96], RD[:, j * P:(j + 1) * P], ident[0:96, 0:96])
                t.transpose(ps[:, 3, 0:32], RC[:, 0:P], ident[0:32, 0:32])
                t.transpose(ps[:, 3, 32:64], RC[:, P:2 * P], ident[0:32, 0:32])
                t.transpose(ps[0:32, 3, 64:96], RC[:, 2 * P:2 * P + 32], ident[0:32, 0:32])
                t.matmul(ps[0:NS, 4, 0:12], LD, hms, start=True, stop=True)
                for g in range(NG):
                    last = t.matmul(ps[0:NS, 5, 4 * g:4 * g + 4], LC[:, g], hsel, start=True, stop=True)
                last.then_inc(S_["wt_pe"], 1)

            def dec_state():
                for b in range(NS):
                    if b >= 2:
                        pe.wait_ge(S_["kv_ok"], b - 1)
                    t.matmul(ps[:, 6 + b % 2, 0:SLAB], ident[0:NS, b:b + 1].to_broadcast([NS, P]),
                             samp[:, 2 * SLAB:3 * SLAB], start=True, stop=True).then_inc(S_["vb_pe"], 1)
                pe.wait_ge(S_["s_new"], 1)
                for e in range(2):
                    h = slice(64 * e, 64 * e + 64)
                    for c in range(3):
                        for b in range(NS):
                            last = t.matmul(ps[0:NS, 6 + e, c * 64:c * 64 + 64], Qz[h, c, b, :], stS[h, b, c, :],
                                            start=(b == 0), stop=(b == NS - 1))
                last.then_inc(S_["s_o_pe"], 1)

            def dec_v(b):
                if b == 0:
                    pe.wait_ge(S_["aw_ok"], 1)
                pe.wait_ge(kvload[b % 2], 16 * KPER * ((NS + b) // 2 + 1))
                for c in range(3):
                    for j in range(PAGES):
                        last = t.matmul(ps[:, 2, (c * NS + b) * 2:(c * NS + b) * 2 + 2], kpage[b % 2][:, j, c * P:(c + 1) * P],
                                        AD[:, j, 6 * b + 2 * c:6 * b + 2 * c + 2], start=(j == 0), stop=(j == PAGES - 1))
                for c in range(2):
                    for g in range(NG):
                        r = (P, P, 32)[g]
                        last = t.matmul(ps[:, 3, (c * NS + b) * 2:(c * NS + b) * 2 + 2], kdil[b % 2][0:r, g, c * P:(c + 1) * P],
                                        AC[0:r, g, 4 * b + 2 * c:4 * b + 2 * c + 2], start=(g == 0), stop=(g == NG - 1))
                last.then_inc(S_["vused"], 1)
                if b == NS - 1:
                    pe.wait_ge(S_["vused"], NS)

            def dec_out():
                pe.wait_ge(S_["of_ok"], 1)
                for c in range(3):
                    t.transpose(ps[0:NS, 4, c * P:(c + 1) * P], oDF[:, c], ident[:])
                for c in range(2):
                    last = t.transpose(ps[0:NS, 5, c * P:(c + 1) * P], oCF[:, c], ident[:])
                last.then_inc(S_["ot_pe"], 1)

            def mt(i):
                r = tile_rows(i)
                pe.wait_ge(S_["ro_ok"], i + 1)
                pe.wait_ge(S_["c_o_ok"], min(i + 1, NT))
                if i:
                    pe.wait_ge(S_["mt_ok"], i)
                if i == NT:
                    pe.wait_ge(S_["dec_done"], 1)
                for c in range(DC):
                    last = t.transpose(ps[:, c // 4, (c % 4) * P:(c % 4) * P + r], XM[0:r, i, c * P:(c + 1) * P],
                                       ident[0:r, 0:r])
                last.then_inc(S_["mt_pe"], 1)

            does = dict(proj=proj, samp_t=samp_t, lev_mm=lev_mm, kt=kt, h_out=h_out, h_state=h_state, d_s=d_s,
                        d_t=d_t, d_pv=d_pv, c_s=c_s, c_t=c_t, c_pv=c_pv, krows=krows, dec_k=dec_k, dec_soft=dec_soft,
                        dec_state=dec_state, dec_v=dec_v, dec_out=dec_out, mt=mt)
            for step, *arg in STEPS:
                if step in does:
                    does[step](*arg)

            def rows_to_columns(src, r, bank):
                for c in range(DC):
                    last = t.transpose(ps[:, bank + c // 4, (c % 4) * P:(c % 4) * P + r], src[0:r, c * P:(c + 1) * P],
                                       ident[0:r, 0:r])
                return last

            pe.wait_ge(S_["dec_done"], 1)
            pe.wait_ge(S_["woload"], 16)

            def wout(i):
                r = tile_rows(i)
                pe.wait_ge(S_["mt_ok"], i + 1)
                if i >= 2:
                    pe.wait_ge(S_["hres_ok"], i - 1)
                for hf in range(2):
                    for c in range(DC):
                        last = t.matmul(ps[0:r, 2 + 2 * (i % 2) + hf, :], xT[:, c, i * P:i * P + r],
                                        wout_[:, c, hf * 512:(hf + 1) * 512], start=(c == 0), stop=(c == DC - 1))
                last.then_inc(S_["wo_pe"], 1)

            def router(i):
                r = tile_rows(i)
                pe.wait_ge(S_["u_ok"], i + 1)
                if i:
                    pe.wait_ge(S_["ut_ok"], i)
                rows_to_columns(Ub[i % 3], r, 6).then_inc(S_["ut_pe"], 1)
                pe.wait_ge(S_["ut_ok"], i + 1)
                for c in range(DC):
                    last = t.matmul(ps[0:r, 0, i * 20:i * 20 + 20], RT[i % 4][:, c, 0:r], rw[:, c, :],
                                    start=(c == 0), stop=(c == DC - 1))
                last.then_inc(S_["rl_pe"], 1)

            wout(0)
            for i in range(1, T5):
                wout(i)
                router(i - 1)
            router(NT)
            pe.wait_ge(S_["c_ok"], 1)
            for i in range(T5):
                for k in range(i):
                    t.matmul(ps[:, 1, i * NE:(i + 1) * NE], ones[:], C[:, k], start=(k == 0), stop=False)
                t.matmul(ps[:, 1, i * NE:(i + 1) * NE], tri, C[:, i], start=(i == 0), stop=True)
            for k in range(T5):
                last = t.matmul(ps[:, 1, T5 * NE:(T5 + 1) * NE], ones[:], C[:, k], start=(k == 0), stop=(k == T5 - 1))
            last.then_inc(S_["rank_pe"], 1)

            pe.wait_ge(S_["tab_rdy"], 1)
            npairs = pe.value_load(npi[0:1, 0:1], min_val=NE // 2, max_val=MAXT // 2)
            last_pair = pe.value_load(npi[0:1, 1:2], min_val=NE // 2 - 1, max_val=MAXT // 2 - 1)

            def gate(j1, b, n_ld, prev):
                pe.wait_ge(S_["mx_ok"], j1)
                pe.wait_ge(wload["wg"][b], n_ld)
                if prev is not None:
                    pe.wait_ge(S_["ht_ok"], prev)
                for c in range(DC):
                    last = t.matmul(ps[:, 2 + 2 * b, :], xgT[b][:, c, :], wg_[b][:, c, :], start=(c == 0), stop=(c == DC - 1))
                last.then_inc(S_["g_pe"], 1)

            def up(j1, b, n_ld):
                pe.wait_ge(wload["wu"][b], n_ld)
                for c in range(DC):
                    last = t.matmul(ps[:, 3 + 2 * b, :], xgT[b][:, c, :], wu_[b][:, c, :], start=(c == 0), stop=(c == DC - 1))
                last.then_inc(S_["u_pe"], 1)

            def rows(j, b, n_ld):
                pe.wait_ge(xgload[b], n_ld)
                if j is not None:
                    pe.wait_ge(S_["mx_ok"], j)
                rows_to_columns(xg[b], P, 0).then_inc(S_["mx_pe"], 1)

            def products(j1, b):
                pe.wait_ge(S_["h_ok"], j1)
                for c in range(FC):
                    last = t.transpose(ps[:, 2 + 2 * b, c * P:(c + 1) * P], hb[b][:, c * P:(c + 1) * P], ident[:])
                last.then_inc(S_["ht_pe"], 1)

            def down(j1, b, n_ld, prev):
                pe.wait_ge(S_["ht_ok"], j1)
                pe.wait_ge(wload["wd"][b], n_ld)
                if prev is not None:
                    pe.wait_ge(S_["ya_ok"], prev)
                    pe.wait_ge(S_["yb_ok"], prev)
                for hf in range(2):
                    for c in range(FC):
                        last = t.matmul(ps[:, 6 + hf, :], hT[b][:, c, :], wd_[b][:, c, hf * 512:(hf + 1) * 512],
                                        start=(c == 0), stop=(c == FC - 1))
                last.then_inc(S_["y_pe"], 1)

            pe.wait_ge(S_["rank_ok"], 1)
            rows(None, 0, 16)
            gate(1, 0, 16, None)
            rows(1, 1, 16)
            up(1, 0, 16)
            gate(2, 1, 16, None)
            rows(2, 0, 32)
            products(1, 0)
            up(2, 1, 16)
            down(1, 0, 16, None)
            gate(3, 0, 32, 1)
            rows(3, 1, 32)
            products(2, 1)
            up(3, 0, 32)
            down(2, 1, 16, 1)
            with pe.Fori(1, last_pair) as i:
                gate(2 * i + 2, 1, i * 16 + 16, i * 2)
                rows(2 * i + 2, 0, i * 16 + 32)
                products(2 * i + 1, 0)
                up(2 * i + 2, 1, i * 16 + 16)
                down(2 * i + 1, 0, i * 16 + 16, i * 2)
                gate(2 * i + 3, 0, i * 16 + 32, i * 2 + 1)
                rows(2 * i + 3, 1, i * 16 + 32)
                products(2 * i + 2, 1)
                up(2 * i + 3, 0, i * 16 + 32)
                down(2 * i + 2, 1, i * 16 + 16, i * 2 + 1)
            gate(npairs * 2, 1, npairs * 16, last_pair * 2)
            products(last_pair * 2 + 1, 0)
            up(npairs * 2, 1, npairs * 16)
            down(last_pair * 2 + 1, 0, npairs * 16, last_pair * 2)
            products(npairs * 2, 1)
            down(npairs * 2, 1, npairs * 16, last_pair * 2 + 1)

            pe.wait_ge(S_["pleload"], 48)

            def columns(i):
                r = tile_rows(i)
                pe.wait_ge(S_["hn_ok"], i + 1)
                pe.wait_ge(pload[i % 2], 16 * (i // 2 + 1))
                if i:
                    pe.wait_ge(S_["hnt_ok"], i)
                rows_to_columns(Ub[i % 3], r, 0)
                for c in range(PC):
                    last = t.transpose(ps[:, 2, c * P:c * P + r], prow[i % 2][0:r, c * P:(c + 1) * P], ident[0:r, 0:r])
                last.then_inc(S_["hnt_pe"], 1)

            def ple(i):
                r = tile_rows(i)
                pe.wait_ge(S_["hnt_ok"], i + 1)
                if i:
                    pe.wait_ge(S_["po_ok"], i)
                for hf in range(2):
                    for c in range(DC):
                        t.matmul(ps[0:r, 4 + hf, :], hnT[i % 2][:, c, 0:r], ple_[:, c, hf * 512:(hf + 1) * 512],
                                 start=(c == 0), stop=(c == DC - 1))
                for hf in range(2):
                    for c in range(PC):
                        last = t.matmul(ps[0:r, 6 + hf, :], pTt[i % 2][:, c, 0:r], plp_[:, c, hf * 512:(hf + 1) * 512],
                                        start=(c == 0), stop=(c == PC - 1))
                last.then_inc(S_["pg_pe"], 1)

            columns(0)
            for i in range(T5):
                ple(i)
                if i < NT:
                    columns(i + 1)


INS = ['x_prompt', 'x_sample', 'state_hgrn', 'cache_k_diff', 'cache_v_diff', 'cache_win128', 'cache_win512',
       'cache_win2048', 'page_table', 'p_prompt', 'p_sample', 'w_in', 'hgrn_lb_logits', 'hgrn_norm',
       'diff_lambda', 'diff_norm', 'w_out', 'router_group_w', 'router_group_b', 'router_expert_w',
       'router_expert_b', 'moe_w_gate', 'moe_w_up', 'moe_w_down', 'ple_w_gate', 'ple_w_proj', 'norm_final']
OUTS = {'y_prompt': (1, 512, 1024), 'y_sample': (8, 1, 1024),
        'state_hgrn_prompt': (1, 1, 6, 64, 64), 'state_hgrn_sample': (1, 8, 6, 64, 64),
        'k_diff_prompt': (1, 1, 512, 6, 2, 32), 'k_diff_sample': (1, 8, 1, 6, 2, 32),
        'v_diff_prompt': (1, 1, 512, 6, 64), 'v_diff_sample': (1, 8, 1, 6, 64),
        'win128_prompt': (1, 1, 128, 2, 4, 64), 'win128_sample': (1, 8, 128, 2, 4, 64),
        'win512_prompt': (1, 1, 512, 2, 4, 64), 'win512_sample': (1, 8, 512, 2, 4, 64),
        'win2048_prompt': (1, 1, 512, 2, 4, 64), 'win2048_sample': (1, 8, 512, 2, 4, 64)}


def kernel(**inputs):
    import numpy as _np
    import concourse.bacc as _bacc
    from concourse import mybir as _mybir
    from concourse.bass_utils import run_bass_kernel_spmd as _run

    nc = _bacc.Bacc("TRN2", target_bir_lowering=False, num_devices=1)
    host = {name: _np.ascontiguousarray(inputs[name]) for name in INS}
    host["norms"] = _np.concatenate([_np.asarray(inputs[k]).reshape(8, 128) for k in ("norm_mix", "norm_ffn", "norm_ple")])
    a, arrays = {}, {}
    for name, x in host.items():
        arrays["in_" + name] = x
        a[name] = nc.dram_tensor("in_" + name, x.shape, _mybir.dt.from_np(x.dtype), kind="ExternalInput").ap()
    o = {name: nc.dram_tensor("out_" + name, shape, _mybir.dt.float32, kind="ExternalOutput").ap()
         for name, shape in OUTS.items()}
    o["win_prompt"] = [o["win128_prompt"], o["win512_prompt"], o["win2048_prompt"]]
    o["win_sample"] = [o["win128_sample"], o["win512_sample"], o["win2048_sample"]]
    hybrid_kernel(nc, a, o)
    r = _run(nc, [arrays], core_ids=[0])
    return tuple(r.results[0]["out_" + name] for name in OUTS)
```

```python
import numpy as np
import concourse.bass as bass
from concourse import mybir
from contextlib import ExitStack

F32 = mybir.dt.float32
BF16 = mybir.dt.bfloat16
I32 = mybir.dt.int32
U8 = mybir.dt.uint8
ALU = mybir.AluOpType
ACT = mybir.ActivationFunctionType
AX = mybir.AxisListType

P = 128
D = 1024
DC = D // P
SEQ = 512
NT = SEQ // P
NS = 8
NTOK = SEQ + NS
N_IN = 4992
SLAB = 384
NSLAB = N_IN // SLAB
PAST = 512
PAGES = PAST // P
NPOOL = 40
HA = HB = 6
HC = 4
NG = 3
WIN = (128, 512, 512)
DIL = (1, 4, 16)
NEG = -1e30
EPS = 1e-6
NGRP = 4
EPG = 4
NE = 16
FF = 512
FC = FF // P
PLE = 256
PC = PLE // P
MAXT = NE + (2 * NTOK - NE) // P
CAPW = FF * DC * 2 + D * FC
BIG = 1e30
SCALE_A = 64 ** -0.5
SCALE_B = 32 ** -0.5
SCALE_C = 64 ** -0.5
LAM_INIT = 0.8 - 0.6
LEVELS = 7
BIGT = 1e9
LN_SPLIT = 2.0 ** -63

C_COL = 7 * SLAB


def tile_rows(i):
    return P if i < NT else NS


PART = 2
PE_STEPS = ("lev_mm", "kt", "h_out", "h_state", "dst_v", "dst_o")
H_SHARE = 1.6
D_SHARE = 1.8
S_EVERY = 2
C_PACE = dict(krows=1, dec_q=4, dec_soft=2, dec_wt=2, dec_v=2)


def projection_units():
    units = []
    for s in range(NSLAB):
        col = s * SLAB
        if s < 7:
            kinds = ("FM", "FM", "TM", "TM", "FM", "FM", "TM")[s]
            if kinds == "FM":
                units += [("FM", s, c * P, P, (s, c)) for c in range(3)]
            else:
                units += [("TM", s, 0, SLAB, (s, i)) for i in range(NT)]
        else:
            g, half = divmod(col - C_COL, 768)
            if half == 0:
                units += [("FM", s, c * P, P, (7 + g, c)) for c in range(3)]
            else:
                units += [("FM", s, 0, P, (7 + g, 3))]
                units += [("TM", s, P, 2 * P, (7 + g, i)) for i in range(NT)]
        units.append(("SM", s, 0, SLAB, None))
        units[-1], units[-2] = units[-2], units[-1]
    out = []
    for n, un in enumerate(units):
        out.append(un)
        if n and units[n - 1][0] == "SM":
            out.append(("SS", units[n - 1][1], 0, SLAB, None))
    if out[-1][0] == "SM":
        out.append(("SS", out[-1][1], 0, SLAB, None))
    return out


def unit_marks(units):
    last = {sl: max(u for u in range(len(units)) if units[u][1] == sl and units[u][0] != "SS") for sl in range(NSLAB)}
    summed = {units[u][1]: u for u in range(len(units)) if units[u][0] == "SS"}
    return last, summed


def dilated_blocks(i):
    lo = max(i - 1, 0)
    out = [(0, kt, (kt - lo) * P) for kt in range(lo, i + 1)]
    for g in (1, 2):
        out += [(g, kt, g * SEQ + kt * P) for kt in range(i + 1)]
    return out


def dilated_groups():
    out = []
    for n in range(NT * HC):
        b = dilated_blocks(n // HC)
        parts = [b[k:k + 4] for k in range(0, len(b), 4)]
        out += [(n, p, k == 0, k == len(parts) - 1) for k, p in enumerate(parts)]
    return out


def schedule(units):
    last, summed = unit_marks(units)
    steps, todo = [], [(u, c, c + PART) for u, un in enumerate(units) for c in ((0,) if un[0] == "SS" else range(0, DC, PART))]

    def project(upto):
        while todo and todo[0][0] <= upto:
            steps.append(("proj", *todo.pop(0)))

    def weave(seq, share):
        owed = 0
        for st in seq:
            steps.append(st)
            if st[0] in PE_STEPS:
                owed += share
                while owed >= 1 and todo:
                    steps.append(("proj", *todo.pop(0)))
                    owed -= 1

    project(max(last[1], summed[1]))
    steps.append(("samp_t",))
    project(last[1] + 2)
    steps.append(("act_fn",))
    project(last[1] + 4)
    steps.append(("log_f",))
    project(max(last[2], summed[2]))
    h = []
    nlev = NT * LEVELS
    j = 0
    h.append(("lev_d", 0))
    for i in range(NT):
        h += [("io_a", i), ("lev_mm", i, 0), ("io_b", i)]
        for l in range(1, LEVELS + 1):
            j = i * LEVELS + l - 1
            if j + 1 < nlev:
                h.append(("lev_d", j + 1))
            h += [("lev_q", j), ("lev_cp", i, l - 1), ("lev_mm", i, l)]
            if l == 3:
                h.append(("kt", i))
        h += [("lev_cp", i, LEVELS), ("h_out", i), ("h_state", i)]
    weave(h, H_SHARE)
    weave([("dst_v", b) for b in range(NS)] + [("dst_new",), ("dst_o",)], 0.3)
    project(max(last[3], summed[3]))
    steps.append(("gate_fn",))
    project(last[6])
    nd = NT * HB
    d = []
    for n in range(nd + 2):
        if n < nd:
            d.append(("d_s", n))
        if 1 <= n <= nd:
            d.append(("d_t", n - 1))
        if n >= 2:
            d.append(("d_pv", n - 2))
    c, groups = [("c_s", 0)], dilated_groups()
    for gi in range(len(groups) + 1):
        if gi < len(groups):
            if groups[gi][2] and groups[gi][0] + 1 < NT * HC:
                c.append(("c_s", groups[gi][0] + 1))
            c.append(("c_t", gi))
        if gi >= 1:
            c.append(("c_pv", gi - 1))
    side = [("krows", u) for u in range(len(key_row_units()))] + [("dec_new",)]
    side += [("dec_q", b) for b in range(NS)] + [("dec_soft",), ("idle",), ("idle",), ("dec_wt",), ("idle",)]
    side += [("dec_v", u) for u in range(2 * NS)] + [("dec_out",)]
    owed = 0
    for k, st in enumerate(d):
        steps.append(st)
        owed += D_SHARE
        while todo and owed >= 1:
            steps.append(("proj", *todo.pop(0)))
            owed -= 1
        if not todo and k % S_EVERY == 0:
            steps.append(side.pop(0))
    project(len(units))
    free = 0
    for k, st in enumerate(c):
        steps.append(st)
        if side and k >= free:
            steps.append(side.pop(0))
            free = k + C_PACE.get(steps[-1][0], 1)
        if k % 16 == 8 and k // 16 < NT:
            steps.append(("ro", k // 16))
    steps += [("mt", i) for i in range(NT)] + side + [("ro", NT)]
    return [st for st in steps if st[0] != "idle"]


def key_row_units():
    out = []
    for i in range(NT):
        out += [(i, None), (i, (1, 2))]
    return out + [(NT - 1, (0,))]


def hybrid_kernel(nc, a, o):
    ctx = ExitStack()
    with ctx:
        def sb(name, shape, dt=F32):
            return ctx.enter_context(nc.sbuf_tensor(name, shape, dt))

        def sem(name):
            return ctx.enter_context(nc.semaphore(name))

        def dram(name, shape, dt=F32):
            return nc.dram_tensor(name, shape, dt, kind="Internal").ap()

        ctx.enter_context(nc.allow_non_contiguous_dma(reason="short rows of small tables"))
        EXPERT = sb("EXPERT", [P, 2 * CAPW])
        slab = [EXPERT[:, k * DC * SLAB:(k + 1) * DC * SLAB].rearrange("p (c n) -> p c n", c=DC) for k in range(2)]
        at0 = 2 * DC * SLAB
        cF = EXPERT[:, at0:at0 + 12 * SEQ].rearrange("p (g q t) -> p g q t", g=NG, q=4)
        at0 += 12 * SEQ
        iT = EXPERT[:, at0:at0 + NT * SLAB].rearrange("p (i n) -> p i n", i=NT)
        at0 += NT * SLAB
        gT = EXPERT[:, at0:at0 + (NT + 1) * SLAB].rearrange("p (i n) -> p i n", i=NT + 1)
        at0 += (NT + 1) * SLAB
        bvT = EXPERT[:, at0:at0 + NT * SLAB].rearrange("p (i n) -> p i n", i=NT)
        at0 += NT * SLAB
        cvT = EXPERT[:, at0:at0 + NT * NG * 256].rearrange("p (g i n) -> p g i n", g=NG, i=NT)
        at0 += NT * NG * 256
        stS = EXPERT[:, at0:at0 + NS * SLAB // 2].rearrange("p (b c v) -> p b c v", b=NS, c=3)
        at0 += NS * SLAB // 2
        kdil = [EXPERT[:, at0 + k * NG * 256:at0 + (k + 1) * NG * 256].rearrange("p (g n) -> p g n", g=NG)
                for k in range(2)]
        at0 += 2 * NG * 256
        S = EXPERT[:, at0:at0 + SLAB].rearrange("p (c n) -> p c n", c=3)
        at0 += SLAB
        blk = EXPERT[:, at0:at0 + P]
        at0 += P
        Sadd = EXPERT[:, at0:at0 + SLAB].rearrange("p (c n) -> p c n", c=3)
        at0 += SLAB
        xS = EXPERT[:, at0:at0 + DC * 32].rearrange("p (c t) -> p c t", c=DC)
        at0 += DC * 32
        part = kdil[0].rearrange("p g n -> p (g n)")[:, 0:SLAB]
        assert at0 <= 2 * CAPW, at0
        kpage = [EXPERT[:, k * PAGES * SLAB:(k + 1) * PAGES * SLAB].rearrange("p (j n) -> p j n", j=PAGES)
                 for k in range(2)]

        xT = sb("xT", [P, DC, NTOK])
        XM = sb("XM", [P, NT + 1, D])
        samp_ = sb("samp", [P, N_IN])
        samp = samp_[0:NS, :]
        aF_ = sb("aF", [P, 9 * NTOK])
        aF = aF_[:].rearrange("p (a c t) -> p a c t", a=3, c=3)
        qF, bF, kF = aF[:, 0], aF[:, 1], aF[:, 2]
        dF_ = sb("dF", [P, 6 * SEQ])
        dF = dF_[:].rearrange("p (a c t) -> p a c t", a=2, c=3)
        rw = sb("rw", [P, DC, 20])
        rbias = sb("rbias", [P, 20])
        wk = sb("wk", [P, 2, 3 * SEQ])
        work, work2 = wk[:, 0], wk[:, 1]
        PT = sb("PT", [P, 2, SEQ])
        ident = sb("ident", [P, P])
        ones = sb("ones", [P, P])
        identb = sb("identb", [P, P], BF16)
        mband = sb("mband", [P, 2 * P], BF16)
        mstride = sb("mstride", [P, 2, NT * P], BF16)
        lmask = sb("lmask", [P, LEVELS, P], U8)
        small = sb("small", [P, 512])
        gains = sb("gains", [P, 27])
        npage = sb("npage", [1, NS * PAGES], I32)
        hg = sb("hg", [P, 64])
        dg = sb("dg", [P, 64])
        lamb = sb("lamb", [P, 4 * 32])

        ps = ctx.enter_context(nc.psum_tensor("ps", [P, 8, 512], F32))

        ssq = small[:, 0:8]
        rstd = small[:, 8:16]
        lb = small[:, 16:19]
        omlb = small[:, 19:22]
        lam = small[:, 24:25]
        nlam = small[:, 25:26]
        negm = small[:, 32:36]
        den = small[:, 36:40]
        rec = small[:, 40:44]
        ebl = small[:, 44:47]
        epsc = small[:, 47:48]
        lnb = small[:, 48:49]
        tmp = small[:, 64:128]
        one_col = small[:, 400:416]
        sel4 = small[:, 184:192]

        NDIL = 2 * P + 32
        stK = work2.rearrange("p (b c v) -> p b c v", b=NS, c=3)
        kst = [aF_[:, k * SEQ:(k + 1) * SEQ] for k in range(2)]
        rosq = aF_[:, 2 * SEQ:2 * SEQ + 2 * SLAB]
        rd0 = 2 * SEQ + 2 * SLAB
        RD = aF_[0:96, rd0:rd0 + PAST + 1]
        RC = aF_[0:32, rd0 + PAST + 1:rd0 + PAST + 1 + NDIL + NG]
        sc0 = rd0 + PAST + 1 + NDIL + NG
        SD = aF_[:, sc0:sc0 + 384].rearrange("p (j r) -> p j r", j=PAGES)
        SC = aF_[:, sc0 + 384:sc0 + 480].rearrange("p (g r) -> p g r", g=NG)
        ADz = aF_[:, sc0 + 480:sc0 + 480 + PAGES * NS * 32].rearrange("p (j b r) -> p j b r", j=PAGES, b=NS)
        prodC = dF_[0:96, 0:NS * 256].rearrange("p (b n) -> p b n", b=NS)
        ACz = dF_[:, NS * 256:NS * 256 + NG * NS * 32].rearrange("p (g b r) -> p g b r", g=NG, b=NS)
        d0 = 2 * PAGES * SLAB
        prodD = EXPERT[:, d0:d0 + NS * SLAB].rearrange("p (b n) -> p b n", b=NS)
        NQ = SLAB + NG * 256
        qrep = [EXPERT[:, d0 + k * NQ:d0 + (k + 1) * NQ] for k in range(2)]
        ds = EXPERT[:, 2 * DC * SLAB + 12 * SEQ:2 * DC * SLAB + 12 * SEQ + NT * SLAB]
        hms = ds[0:96, 0:12]
        mB = ds[0:96, 16:24]
        hsel = ds[0:32, 32:36]
        mC = ds[0:32, 40:48]
        LD = ds[0:96, 48:56]
        LC = ds[0:32, 64:88].rearrange("p (g b) -> p g b", g=NG)
        st96 = ds[0:96, 96:104]
        st32 = ds[0:32, 112:120]
        anew = ds[0:8, 128:152]
        snd = ds[0:8, 160:172]
        snc = ds[0:8, 176:188].rearrange("p (g h) -> p g h", g=NG)
        MD = ds[0:8, 192:288]
        MC = ds[0:8, 288:384].rearrange("p (g b h) -> p g b h", g=NG, b=NS)
        fex = ds[:, 448:472].rearrange("p (c b) -> p c b", c=3)
        id8 = ds[:, 512:576]
        Qz = ds[:, 576:768].rearrange("p (c b e) -> p c b e", c=3, b=NS)
        dcst = ds[0:8, 768:768 + SLAB]

        names = """act_seq dve_seq pool_seq cload consts rstd_ok xn_ok xt_pe xt_ok gain_pe gain_ok unit_pe unit_ok outs
            tab_ok lb_e lb_ok lam_s lam_e  samp_t_pe samp_t_ok prep_e prep_q prep_f prep_ln prep_ok
            gate_e gate_ok lev_d lev_e lev_q lev_pe lev_cp io_d io_e io_ok kt_pe kt_ok h_out_pe h_out_ok h_st_pe h_st_ok
            d_s_pe d_max d_exp d_a d_t_pe d_t_ok d_o_pe d_o_ok c_s_pe c_max c_exp c_t_pe c_t_ok c_o_pe c_o_ok
            kr_pe kr_ok  stload kused bq_ok new_ok pv_pe pv_ok sc_pe row_ok row_e w_ok wt_pe aw_ok
            ot_pe dec_done vb_pe kv_ok fx_ok s_new s_o_pe s_o_ok
            ro_sq ro_e ro_ok mt_pe mt_ok woload woload_last wo_pe hres_ok n2_e u_ok u_st ut_pe ut_ok rl_pe  rt_e gexp
            c_ok rank_pe rank_ok scat idxld pool_past tab_rdy xg_idx mx_pe mx_ok g_pe u_pe sil_ok h_ok ht_pe ht_ok y_pe
            ya_ok yb_ok   comb_ok hn_e hn_ok hnt_pe hnt_ok  pg_pe pg_sig po_ok n4_e y_ok pleload  iot pp_t pp_c pp_m pp_o sp_pe sp_cp pload
            """.split()
        S_ = {n: sem(n) for n in names}
        xload = [sem(f"xload{i}") for i in range(NT + 1)]
        slabload = [sem(f"slabload{k}") for k in range(2)]
        kr_out = [sem(f"kr_out{k}") for k in range(2)]
        kvload = [sem(f"kvload{k}") for k in range(2)]

        wload = {k: [sem(f"{k}load{b}") for b in range(2)] for k in ("wg", "wu", "wd")}
        xgload = [sem(f"xgload{k}") for k in range(2)]
        ystore = [sem(f"ystore{k}") for k in range(2)]
        yload = [sem(f"yload{k}") for k in range(2)]

        W = [EXPERT[:, k * CAPW:(k + 1) * CAPW] for k in range(2)]
        wg_ = [w[:, 0:DC * FF].rearrange("p (c n) -> p c n", c=DC) for w in W]
        wu_ = [w[:, DC * FF:2 * DC * FF].rearrange("p (c n) -> p c n", c=DC) for w in W]
        wd_ = [w[:, 2 * DC * FF:].rearrange("p (c n) -> p c n", c=FC) for w in W]
        wout_ = EXPERT[:, 0:DC * D].rearrange("p (c n) -> p c n", c=DC)
        aflat = aF_[:]
        dflat = dF_[:]
        wflat = wk[:].rearrange("p a n -> p (a n)")
        xg = [aflat[:, k * D:(k + 1) * D] for k in range(2)]
        xgT = [aflat[:, (2 + k) * D:(3 + k) * D].rearrange("p (c t) -> p c t", c=DC) for k in range(2)]
        hb = [dflat[:, k * FF:(k + 1) * FF] for k in range(2)]
        hT = [dflat[:, (2 + k) * FF:(3 + k) * FF].rearrange("p (c t) -> p c t", c=FC) for k in range(2)]
        yb_ = [wflat[:, k * D:(k + 1) * D] for k in range(2)]
        Ub = [wflat[:, k * D:(k + 1) * D] for k in range(3)]
        RT = [aflat[:, k * D:(k + 1) * D].rearrange("p (c t) -> p c t", c=DC) for k in range(4)]
        u2d = dram("u2d", [NTOK, D])
        q_d = dram("q_d", [NS, NQ])
        Yd = dram("Yd", [MAXT * P, D])
        list_d = dram("list_d", [MAXT * P, 1], I32)
        off = [0]

        def take(*shape, dt=F32):
            k = int(np.prod(shape))
            v_ = samp_[:, off[0]:off[0] + k]
            off[0] += k
            if dt != F32:
                v_ = v_.bitcast(dt)
            if len(shape) == 2:
                v_ = v_.rearrange("p (a b) -> p a b", a=shape[0])
            return v_

        T5 = NT + 1
        L = take(T5, 20)
        jrow = take(4)
        erow = take(NE)
        tokf = take(T5)
        toki = take(T5, dt=I32)
        tri = take(P)
        gm, gs, gw, m1, m2, mn, e2, w1, w2 = (take(T5) for _ in range(9))
        og, o1, o2, es, es2, t4 = (take(T5, 4) for _ in range(6))
        O1, O2, C, rank, q_, tl, t16, slotY, slotL = (take(T5, NE) for _ in range(9))
        cnt, nx, incl, exc = (take(NE) for _ in range(4))
        xrow = take(8)
        xcmp = take(8, NE)
        tabf = take(MAXT)
        tabi = take(MAXT, dt=I32)
        npf = take(2)
        npi = take(2, dt=I32)
        sel = take(4, T5)
        seli = take(4, T5, dt=I32)
        idxall = take(MAXT, dt=I32)
        idxc = [take(1, dt=I32) for _ in range(2)]
        zi = take(MAXT, dt=I32)
        iti = take(24, dt=I32)
        assert off[0] <= N_IN, off[0]

        ple_ = EXPERT[:, 0:DC * D].rearrange("p (c n) -> p c n", c=DC)
        nfin = EXPERT[:, DC * D:(DC + 1) * D]
        q0 = CAPW
        hnT = [EXPERT[:, q0 + k * D:q0 + (k + 1) * D].rearrange("p (c t) -> p c t", c=DC) for k in range(2)]
        q0 += 2 * D
        sig = [EXPERT[:, q0 + k * D:q0 + (k + 1) * D] for k in range(2)]
        z0 = CAPW + 2 * DC * FF
        plp_ = EXPERT[:, z0:z0 + PC * D].rearrange("p (c n) -> p c n", c=PC)
        z0 += PC * D
        prow = [EXPERT[:, z0 + k * PLE:z0 + (k + 1) * PLE] for k in range(T5)]
        z0 += T5 * PLE
        pTt = [EXPERT[:, z0 + k * PLE:z0 + (k + 1) * PLE].rearrange("p (c t) -> p c t", c=PC) for k in range(2)]
        assert z0 + 2 * PLE <= at0 - DC * 32
        xflat = xT[:].rearrange("p c t -> p (c t)")
        pproj = [xflat[:, k * D:(k + 1) * D] for k in range(NT)] + [samp_[:, N_IN - D:N_IN]]
        assert off[0] <= N_IN - D
        PTf = PT[:].rearrange("p a n -> p (a n)")
        ybuf = [[aflat[:, k * D:(k + 1) * D] for k in range(2)], [aflat[:, (2 + k) * D:(3 + k) * D] for k in range(2)]]

        UNITS = projection_units()
        NU = len(UNITS)
        LASTU, SUMU = unit_marks(UNITS)
        STEPS = schedule(UNITS)
        DG = dilated_groups()
        MT_BANK = [2, 4, 2, 4, 0]
        KU = key_row_units()
        KR_DMAS = [len(gs_ or (0,)) for _, gs_ in KU]
        KR_ALL = [16 * sum(KR_DMAS[k::2]) for k in range(2)]
        KPER = 2 * PAGES // 2 + NG
        block = ctx.enter_context(nc.Block())

        def f2(ap, n):
            return ap.unsqueeze(2).to_broadcast([ap.shape[0], ap.shape[1], n])

        def rows_of(buf, i):
            return buf[:, :, i * P:(i + 1) * P]

        @block.sync
        def _(sp):
            n_out = 0
            for i in range(NT + 1):
                src = a["x_prompt"][0, i * P:(i + 1) * P, :] if i < NT else a["x_sample"].rearrange("b t d -> (b t) d")
                sp.dma_start(XM[0:tile_rows(i), i, :], src).then_inc(xload[i], 16)
            w = a["w_in"][0].rearrange("(c p) n -> p c n", p=P)
            for s in range(NSLAB):
                if s >= 2:
                    sp.wait_ge(S_["unit_pe"], 1 + LASTU[s - 2])
                sp.dma_start(slab[s % 2], w[:, :, s * SLAB:(s + 1) * SLAB]).then_inc(slabload[s % 2], 16)
                if s == 3:
                    st = a["state_hgrn"][0].rearrange("b (c e) k v -> e k b c v", e=2)
                    for e in range(2):
                        for c in range(3):
                            sp.dma_start(stS[64 * e:64 * e + 64, :, c], st[e, :, :, c]).then_inc(S_["stload"], 16)
            for g in range(NG):
                src = a[("cache_win128", "cache_win512", "cache_win2048")[g]][0]
                dst = o["win_sample"][g][0]
                n = WIN[g] - 1
                sp.dma_start(dst[:, 0:n].rearrange("b r k h d -> b (r k h d)"),
                             src[:, 1:n + 1].rearrange("b r k h d -> b (r k h d)")).then_inc(S_["outs"], 16)
                n_out += 1
            sp.wait_ge(S_["unit_ok"], NU)
            sp.dma_start(o["k_diff_sample"].rearrange("l b t h m d -> (l b t) (h m d)"),
                         samp[:, 5 * SLAB:6 * SLAB]).then_inc(S_["outs"], 16)
            sp.dma_start(o["v_diff_sample"].rearrange("l b t h d -> (l b t) (h d)"),
                         samp[:, 6 * SLAB:7 * SLAB]).then_inc(S_["outs"], 16)
            for g in range(NG):
                c = C_COL + g * 768 + 256
                sp.dma_start(o["win_sample"][g][0, :, WIN[g] - 1].rearrange("b k h d -> b (k h d)"),
                             samp[:, c:c + 512]).then_inc(S_["outs"], 16)
            n_out += 5
            sp.dma_start(q_d[:, 0:SLAB], samp[:, 4 * SLAB:5 * SLAB]).then_inc(S_["outs"], 16)
            sp.dma_start(q_d[:, SLAB:].rearrange("b (g n) -> b g n", g=NG),
                         samp[:, C_COL:].rearrange("b (g s n) -> b g s n", g=NG, s=3)[:, :, 0]).then_inc(S_["outs"], 16)
            n_out += 2
            sp.wait_ge(S_["outs"], 16 * n_out)
            sp.wait_ge(S_["cload"], 16 * 10)
            wins = [a["cache_win128"], a["cache_win512"], a["cache_win2048"]]

            def cached(b, kv):
                buf, ld = b % 2, kvload[b % 2]
                pool_ = a[("cache_k_diff", "cache_v_diff")[kv]]
                pool_ = pool_[0].rearrange("n t h m d -> n t (h m d)") if kv == 0 else pool_[0].rearrange(
                    "n t h d -> n t (h d)")
                for j in range(PAGES):
                    page = sp.value_load(npage[0:1, b * PAGES + j:b * PAGES + j + 1], min_val=0, max_val=NPOOL - 1)
                    sp.dma_start(kpage[buf][:, j, :].unsqueeze(1),
                                 pool_[bass.ds(page, 1)].rearrange("o t n -> t o n")).then_inc(ld, 16)
                for g in range(NG):
                    r = (P, P, 32)[g]
                    src = wins[g][0, b].rearrange("(r s) k h d -> r s k (h d)", s=DIL[g])[:, 0, kv]
                    sp.dma_start(kdil[buf][0:r, g], src).then_inc(ld, 16)
                if kv == 0:
                    sp.dma_start(qrep[buf], q_d[b:b + 1, :].to_broadcast([P, NQ])).then_inc(ld, 16)

            for b in range(NS):
                if b >= 2:
                    sp.wait_ge(S_["kused"], b - 1)
                cached(b, 0)
            for i in range(NT):
                sp.dma_start(o["v_diff_prompt"][0, 0, i * P:(i + 1) * P].rearrange("t h d -> t (h d)"),
                             bvT[:, i]).then_inc(S_["outs"], 16)
                n_out += 1
                for g in range(NG):
                    lo = i * P - (SEQ - WIN[g])
                    if lo >= 0:
                        sp.dma_start(o["win_prompt"][g][0, 0, lo:lo + P, 1].rearrange("t h d -> t (h d)"),
                                     cvT[:, g, i]).then_inc(S_["outs"], 16)
                        n_out += 1
            for b in range(NS):
                if b < 2:
                    sp.wait_ge(S_["kused"], NS - 1 + b)
                else:
                    sp.wait_ge(S_["pv_pe"], 2 * (b - 1))
                cached(b, 1)
            st = o["state_hgrn_sample"][0].rearrange("b (c e) k v -> e k b c v", e=2)
            sp.wait_ge(S_["s_new"], 1)
            for e in range(2):
                for c in range(3):
                    sp.dma_start(st[e, :, :, c], stS[64 * e:64 * e + 64, :, c]).then_inc(S_["outs"], 16)
            sp.wait_ge(S_["h_st_ok"], NT)
            st = o["state_hgrn_prompt"][0, 0].rearrange("(c e) k v -> e k c v", e=2)
            for e in range(2):
                sp.dma_start(st[e], S[64 * e:64 * e + 64, :, 64 * e:64 * e + 64]).then_inc(S_["outs"], 16)
            n_out += 8
            sp.wait_ge(S_["pv_pe"], 2 * NS)
            wo = a["w_out"][0].rearrange("(c p) n -> p c n", p=P)
            c0, cw = d0 // D, 2 * DC * SLAB // D
            sp.dma_start(wout_[:, 0:c0], wo[:, 0:c0]).then_inc(S_["woload"], 16)
            sp.wait_ge(S_["c_s_pe"], NT * HC)
            sp.wait_ge(S_["kr_pe"], len(KU))
            sp.dma_start(wout_[:, cw:], wo[:, cw:]).then_inc(S_["woload"], 16)
            sp.wait_ge(S_["ot_pe"], 1)
            sp.dma_start(wout_[:, c0:cw], wo[:, c0:cw]).then_inc(S_["woload_last"], 16)
            for i in range(NT + 1):
                src = a["x_prompt"][0, i * P:(i + 1) * P, :] if i < NT else a["x_sample"].rearrange("b t d -> (b t) d")
                sp.wait_ge(S_["mt_pe"], i + 1)
                sp.dma_start(XM[0:tile_rows(i), i, :], src).then_inc(xload[i], 16)
            sp.wait_ge(S_["outs"], 16 * n_out)
            wsrc = dict(wg=a["moe_w_gate"][0].rearrange("e (c p) n -> p (e c) n", p=P),
                        wu=a["moe_w_up"][0].rearrange("e (c p) n -> p (e c) n", p=P),
                        wd=a["moe_w_down"][0].rearrange("e (c p) n -> p (e c) n", p=P))
            nch = dict(wg=DC, wu=DC, wd=FC)
            wdst = dict(wg=wg_, wu=wu_, wd=wd_)
            sp.wait_ge(S_["ro_ok"], NT + 1)
            sp.dma_start(plp_, a["ple_w_proj"][0].rearrange("(c p) n -> p c n", p=P)).then_inc(S_["pload"], 16)
            for i in range(T5):
                src = a["p_prompt"][0, 0, i * P:(i + 1) * P, :] if i < NT else a["p_sample"][0].rearrange("b t d -> (b t) d")
                sp.dma_start(prow[i][0:tile_rows(i), :], src).then_inc(S_["pload"], 16)
            for k in ("wg", "wu"):
                sp.dma_start(wdst[k][1], wsrc[k][:, nch[k]:2 * nch[k]]).then_inc(wload[k][1], 16)
            for i in range(NT + 1):
                sp.wait_ge(S_["u_ok"], i + 1)
                sp.dma_start(u2d[i * P:i * P + tile_rows(i), :], Ub[i % 3][0:tile_rows(i), :]).then_inc(S_["u_st"], 16)
            sp.wait_ge(S_["wo_pe"], NT + 1)
            for k in ("wg", "wu", "wd"):
                sp.dma_start(wdst[k][0], wsrc[k][:, 0:nch[k]]).then_inc(wload[k][0], 16)
            sp.wait_ge(S_["pp_m"], T5)
            sp.dma_start(wdst["wd"][1], wsrc["wd"][:, FC:2 * FC]).then_inc(wload["wd"][1], 16)
            sp.wait_ge(S_["tab_rdy"], 1)
            npairs = sp.value_load(npi[0:1, 0:1], min_val=NE // 2, max_val=MAXT // 2)
            with sp.Fori(1, npairs) as i:
                for b in range(2):
                    e = sp.value_load(tabi[0:1, bass.ds(2 * i + b, 1)], min_val=0, max_val=NE - 1)
                    for k, done in (("wg", "g_pe"), ("wu", "u_pe"), ("wd", "y_pe")):
                        sp.wait_ge(S_[done], 2 * i + b - 1)
                        sp.dma_start(wdst[k][b], wsrc[k][:, bass.ds(e * nch[k], nch[k])]).then_inc(wload[k][b], 16)
            last_pair = sp.value_load(npi[0:1, 1:2], min_val=NE // 2 - 1, max_val=MAXT // 2 - 1)
            sp.wait_ge(S_["g_pe"], last_pair * 2 + 1)
            sp.wait_ge(S_["u_pe"], last_pair * 2 + 1)
            sp.dma_start(ple_[:, :, :], a["ple_w_gate"][0].rearrange("(c p) n -> p c n", p=P)).then_inc(S_["pleload"], 16)
            sp.wait_ge(S_["y_pe"], last_pair * 2 + 1)
            sp.dma_start(nfin, a["norm_final"].rearrange("(o n) -> o n", o=1).to_broadcast([P, D])).then_inc(S_["pleload"], 16)
            for i in range(NT + 1):
                r = tile_rows(i)
                sp.wait_ge(S_["y_ok"], i + 1)
                dst = o["y_prompt"][0, i * P:(i + 1) * P, :] if i < NT else o["y_sample"].rearrange("b t d -> (b t) d")
                sp.dma_start(dst, XM[0:r, i, :]).then_inc(S_["outs"], 16)
                n_out += 1
            sp.wait_ge(kr_out[0], KR_ALL[0])
            sp.wait_ge(kr_out[1], KR_ALL[1])
            sp.wait_ge(S_["outs"], 16 * n_out)

        @block.gpsimd
        def _(pool):
            n = [0]

            def seq(ins):
                n[0] += 1
                ins.then_inc(S_["pool_seq"], 1)
                pool.wait_ge(S_["pool_seq"], n[0])

            g = nc.gpsimd
            g.memset(ones[:], 1.0)
            seq(g.memset(PT[:], 0.0))
            seq(g.memset(identb[:], 0.0))
            seq(g.memset(ident[:], 0.0))
            g.affine_select(out=identb[:], in_=identb[:], compare_op=ALU.not_equal, fill=1.0, base=0,
                            pattern=[[-1, P]], channel_multiplier=1).then_inc(S_["consts"], 1)
            g.affine_select(out=ident[:], in_=ident[:], compare_op=ALU.not_equal, fill=1.0, base=0,
                            pattern=[[-1, P]], channel_multiplier=1).then_inc(S_["consts"], 1)
            dist = iT[:, 0, 0:P].bitcast(I32)
            rowi = iT[:, 0, P:2 * P].bitcast(I32)
            coli = iT[:, 0, 2 * P:3 * P].bitcast(I32)
            seq(g.iota(dist, pattern=[[-1, P]], base=P, channel_multiplier=1))
            seq(g.iota(rowi, pattern=[[0, P]], base=0, channel_multiplier=1))
            g.iota(coli, pattern=[[1, P]], base=0, channel_multiplier=0).then_inc(S_["consts"], 1)
            seq(g.memset(mband[:], 0.0))
            seq(g.affine_select(out=mband[:, 0:P], in_=mband[:, 0:P], compare_op=ALU.is_ge, fill=NEG, base=0,
                                pattern=[[1, P]], channel_multiplier=-1))
            g.affine_select(out=mband[:, P:2 * P], in_=mband[:, P:2 * P], compare_op=ALU.is_ge, fill=NEG, base=0,
                            pattern=[[-1, P]], channel_multiplier=1).then_inc(S_["consts"], 1)
            seq(g.memset(blk[:], 0.0))
            seq(g.memset(blk[0:64, 0:64], 1.0))
            g.memset(blk[64:P, 64:P], 1.0).then_inc(S_["consts"], 1)
            pool.wait_ge(S_["consts"], 5)
            pool.wait_ge(S_["tab_ok"], 1)
            own = mstride[:, :, (NT - 1) * P:NT * P]
            g.affine_select(out=own, in_=own, compare_op=ALU.is_ge, fill=NEG, base=0,
                            pattern=[[0, 2], [-1, P]], channel_multiplier=1).then_inc(S_["consts"], 1)
            pool.dma_start(Yd[NE * P:MAXT * P].rearrange("(j p) n -> p j n", p=P),
                           PT[:].rearrange("p a n -> p (a n)").unsqueeze(1).to_broadcast([P, MAXT - NE, D])
                           ).then_inc(S_["idxld"], 16)
            for b in range(NS):
                kp, kd, q = kpage[b % 2], kdil[b % 2], qrep[b % 2]
                pool.wait_ge(kvload[b % 2], 16 * (KPER + 1) * (b // 2 + 1))
                g.tensor_tensor(kp, kp, q[:, 0:SLAB].unsqueeze(1).to_broadcast([P, PAGES, SLAB]), ALU.mult)
                g.tensor_tensor(kd[:, 0:2], kd[:, 0:2], q[:, SLAB:SLAB + 512].rearrange("p (g n) -> p g n", g=2), ALU.mult)
                g.tensor_tensor(kd[0:32, 2], kd[0:32, 2], q[0:32, SLAB + 512:NQ], ALU.mult).then_inc(S_["bq_ok"], 1)
            pool.wait_ge(S_["dec_done"], 1)
            seq(g.memset(zi, 0))
            pool.dma_start(list_d.rearrange("(p j) o -> p (j o)", p=P), zi).then_inc(S_["idxld"], 16)
            seq(g.iota(toki, pattern=[[P, T5]], base=0, channel_multiplier=1))
            seq(g.memset(tri, 1.0))
            seq(g.affine_select(out=tri, in_=tri, compare_op=ALU.is_ge, fill=0.0, base=-1,
                                pattern=[[1, P]], channel_multiplier=-1))
            seq(g.iota(iti, pattern=[[1, 24]], base=0, channel_multiplier=0))
            seq(g.memset(L, 0.0))
            g.memset(q_, 0.0).then_inc(S_["iot"], 1)
            pool.wait_ge(S_["idxld"], 32)
            pool.wait_ge(S_["rank_ok"], 1)
            for i in range(T5):
                r = tile_rows(i)
                for k in range(2):
                    g.indirect_dma_start(out=list_d, out_offset=bass.IndirectOffsetOnAxis(ap=seli[0:r, 2 + k, i:i + 1], axis=0),
                                         in_=toki[0:r, i:i + 1], in_offset=None).then_inc(S_["scat"], 16)
            pool.wait_ge(S_["scat"], 16 * 2 * T5)
            pool.dma_start(idxall, list_d.rearrange("(p j) o -> p (j o)", p=P)).then_inc(S_["idxld"], 16)
            pool.wait_ge(S_["idxld"], 48)
            pool.wait_ge(S_["u_st"], 16 * T5)
            pool.wait_ge(S_["rl_pe"], T5)
            pool.wait_ge(S_["tab_rdy"], 1)
            npairs = pool.value_load(npi[0:1, 0:1], min_val=NE // 2, max_val=MAXT // 2)

            def gather(j, b, count):
                g.tensor_copy(idxc[b], idxall[:, j]).then_inc(S_["xg_idx"], 1)
                pool.wait_ge(S_["xg_idx"], count)
                pool.sem_inc(S_["pool_past"], 1)
                g.indirect_dma_start(out=xg[b], out_offset=None, in_=u2d,
                                     in_offset=bass.IndirectOffsetOnAxis(ap=idxc[b], axis=0)).then_inc(xgload[b], 16)

            for b in range(2):
                gather(slice(b, b + 1), b, b + 1)
            with pool.Fori(1, npairs) as i:
                for b in range(2):
                    pool.wait_ge(S_["mx_pe"], 2 * i + b - 1)
                    gather(bass.ds(2 * i + b, 1), b, 2 * i + b + 1)
            for b in range(2):
                pool.wait_ge(ystore[b], npairs * 16)
            pool.wait_ge(S_["y_pe"], npairs * 2)
            pool.sem_inc(S_["pool_past"], 1)
            for i in range(T5):
                r = tile_rows(i)
                if i >= 2:
                    pool.wait_ge(S_["comb_ok"], i - 1)
                for k in range(2):
                    g.indirect_dma_start(out=ybuf[i % 2][k][0:r, :], out_offset=None, in_=Yd,
                                         in_offset=bass.IndirectOffsetOnAxis(ap=seli[0:r, k, i:i + 1], axis=0)
                                         ).then_inc(yload[i % 2], 16)

        @block.scalar
        def _(act):
            n = [0]
            s = nc.scalar

            def seq(ins):
                n[0] += 1
                ins.then_inc(S_["act_seq"], 1)
                act.wait_ge(S_["act_seq"], n[0])

            act.dma_start(work2[0:24, 0:P], a["norms"]).then_inc(S_["cload"], 16)
            act.dma_start(work2[24:27, 0:P],
                          a["hgrn_lb_logits"].rearrange("l (c p) -> (l c) p", p=P)).then_inc(S_["cload"], 16)
            act.dma_start(hg[:], a["hgrn_norm"].to_broadcast([P, 64])).then_inc(S_["cload"], 16)
            act.dma_start(dg[:], a["diff_norm"].to_broadcast([P, 64])).then_inc(S_["cload"], 16)
            act.dma_start(lamb[:], a["diff_lambda"].rearrange("l r d -> l (r d)").to_broadcast([P, P])).then_inc(S_["cload"], 16)
            act.dma_start(npage[:], a["page_table"].rearrange("(o b) j -> o (b j)", o=1)).then_inc(S_["cload"], 16)
            act.dma_start(rw[:, :, 0:NGRP], a["router_group_w"][0].rearrange("(c p) n -> p c n", p=P)).then_inc(S_["cload"], 16)
            act.dma_start(rw[:, :, NGRP:20], a["router_expert_w"][0].rearrange("(c p) n -> p c n", p=P)).then_inc(S_["cload"], 16)
            act.dma_start(rbias[:, 0:NGRP], a["router_group_b"].to_broadcast([P, NGRP])).then_inc(S_["cload"], 16)
            act.dma_start(rbias[:, NGRP:20], a["router_expert_b"].to_broadcast([P, NE])).then_inc(S_["cload"], 16)
            act.wait_ge(S_["gain_ok"], 1)
            for i in range(NT + 1):
                r = tile_rows(i)
                act.wait_ge(xload[i], 16)
                seq(s.activation(work[0:r, 0:D], XM[0:r, i, :], ACT.Square, accum_out=ssq[0:r, i:i + 1]))
                seq(s.activation(ssq[0:r, i:i + 1], ssq[0:r, i:i + 1], ACT.Ln, bias=epsc[0:r, :], scale=1.0 / D))
                s.activation(rstd[0:r, i:i + 1], ssq[0:r, i:i + 1], ACT.Exp, scale=-0.5).then_inc(S_["rstd_ok"], 1)
            act.wait_ge(S_["lb_e"], 1)
            s.activation(lb, lb, ACT.Exp).then_inc(S_["lb_ok"], 1)
            act.wait_ge(S_["lam_s"], 1)
            s.activation(tmp[:, 0:2], tmp[:, 0:2], ACT.Exp).then_inc(S_["lam_e"], 1)

            def proj(u, k0, k1):
                kind, sl, c0, w, at = UNITS[u]
                if k1 < DC and kind != "SS":
                    return
                act.wait_ge(S_["unit_pe"], u + 1)
                src = ps[:, u % 2, :]
                scale = 1.0
                if kind == "TM" and at == (2, 0):
                    act.wait_ge(S_["tab_ok"], 1)
                if kind == "SM":
                    src, dst = src[:, 0:SLAB], part
                elif kind == "SS":
                    src, dst = src[0:NS, 0:SLAB], samp[:, sl * SLAB:(sl + 1) * SLAB]
                elif kind == "TM":
                    g, i = at
                    dst = iT[:, i] if g == 2 else gT[:, i] if g == 3 else bvT[:, i] if g == 6 else cvT[:, g - 7, i]
                    src = src[:, 0:w]
                else:
                    g, c = at
                    if g < 2:
                        dst = aF[:, g, c, 0:SEQ]
                    elif g < 7:
                        dst, scale = dF[:, g - 4, c], SCALE_B if g == 4 else 1.0
                    else:
                        dst, scale = cF[:, g - 7, c], SCALE_C if c < 2 else 1.0
                s.activation(dst, src, ACT.Copy, scale=scale).then_inc(S_["unit_ok"], 1)

            def samp_t():
                act.wait_ge(S_["samp_t_pe"], 1)
                s.activation(aF[:, 0:2, :, SEQ:NTOK].rearrange("p a c t -> p (a c) t"),
                             ps[:, 2, 0:48].rearrange("p (a t) -> p a t", a=6), ACT.Copy).then_inc(S_["samp_t_ok"], 1)

            def act_fn():
                act.wait_ge(S_["samp_t_ok"], 1)
                act.wait_ge(S_["unit_ok"], LASTU[1] + 1)
                s.activation(qF, qF, ACT.Silu).then_inc(S_["prep_q"], 1)
                s.activation(kF, bF, ACT.Sigmoid, scale=-1.0).then_inc(S_["prep_e"], 1)
                act.wait_ge(S_["prep_e"], 1)
                s.activation(bF, bF, ACT.Sigmoid).then_inc(S_["prep_e"], 1)

            def log_f():
                for c in range(3):
                    act.wait_ge(S_["prep_f"], c + 1)
                    fb = wk[:].rearrange("p a n -> p (a n)")[:, c * NTOK:(c + 1) * NTOK]
                    s.activation(bF[:, c], bF[:, c], ACT.Ln)
                    s.activation(fb, fb, ACT.Ln).then_inc(S_["prep_ln"], 1)

            def gate_fn():
                act.wait_ge(S_["gate_e"], 1)
                g_ = gT.rearrange("p i n -> p (i n)")
                s.activation(g_, g_, ACT.Silu).then_inc(S_["gate_ok"], 1)

            def lev_q(j):
                act.wait_ge(S_["lev_d"], j + 1)
                B = 2 ** (j % LEVELS)
                Dv = work[:, (j % 2) * SLAB:(j % 2 + 1) * SLAB].rearrange("p (n e t) -> p n e t", e=2, t=B)
                s.activation(Dv[:, :, 1], Dv[:, :, 1], ACT.Exp)
                s.activation(Dv[:, :, 0], Dv[:, :, 0], ACT.Exp, scale=-1.0).then_inc(S_["lev_e"], 1)

            def io_a(i):
                act.wait_ge(S_["io_d"], i + 1)
                if i:
                    act.wait_ge(S_["h_out_pe"], i)
                s.activation(work2[:, 768:1152].rearrange("p (c t) -> p c t", c=3), rows_of(bF, i), ACT.Exp)
                s.activation(work2[:, 1152:1536], work2[:, 1152:1536], ACT.Exp, scale=-1.0).then_inc(S_["io_e"], 1)

            def kt(i):
                act.wait_ge(S_["idxld"], 16)
                act.wait_ge(S_["kt_pe"], i + 1)
                if i:
                    act.wait_ge(S_["h_st_pe"], i)
                s.activation(PT[:, 0, 0:SLAB], ps[:, 7, 0:SLAB], ACT.Copy).then_inc(S_["kt_ok"], 1)

            def h_out(i):
                act.wait_ge(S_["h_out_pe"], i + 1)
                s.activation(XM[:, i, 0:SLAB].rearrange("p (c e v) -> p c e v", c=3, e=2),
                             ps[:, 6, 0:SLAB].rearrange("p (c e v) -> p c e v", c=3, e=2),
                             ACT.Copy).then_inc(S_["h_out_ok"], 1)

            def d_s(n):
                act.wait_ge(S_["d_max"], n + 1)
                if n == 0:
                    act.wait_ge(S_["s_new"], 1)
                K = (n // HB + 1) * P
                if n >= 2:
                    act.wait_ge(S_["d_t_pe"], n - 1)
                for m in range(2):
                    last = s.activation(wk[:, n % 2, m * SEQ:m * SEQ + K], ps[:, 2 + 2 * (n % 2) + m, 0:K], ACT.Exp,
                                        bias=negm[:, 2 * (n % 2) + m:2 * (n % 2) + m + 1],
                                        accum_out=den[:, 2 * (n % 2) + m:2 * (n % 2) + m + 1])
                last.then_inc(S_["d_exp"], 1)

            def d_t(n):
                K = (n // HB + 1) * P
                act.wait_ge(S_["d_t_pe"], n + 1)
                if n >= 2:
                    act.wait_ge(S_["d_o_pe"], n - 1)
                s.activation(PT[:, n % 2, 0:K], ps[:, 6, 0:K], ACT.Copy).then_inc(S_["d_t_ok"], 1)

            def d_pv(n):
                i, h = divmod(n, HB)
                if h == HB - 1:
                    act.wait_ge(S_["d_o_pe"], n + 1)
                    s.activation(XM[:, i, SLAB:2 * SLAB], ps[:, 7, 0:SLAB], ACT.Copy).then_inc(S_["d_o_ok"], 1)

            def c_s(n):
                i, h = divmod(n, HC)
                K = (i + 1) * P
                K0 = min(i + 1, 2) * P
                act.wait_ge(S_["c_max"], n + 1)
                if n < 2:
                    act.wait_ge(S_["d_t_pe"], NT * HB)
                else:
                    act.wait_ge(S_["c_t_pe"], 1 + max(k for k in range(len(DG)) if DG[k][0] == n - 2))
                d = small[:, 128 + 8 * (i % 2) + 2 * h:130 + 8 * (i % 2) + 2 * h]
                if i >= 2 and h == 0:
                    act.wait_ge(S_["c_o_ok"], i - 1)
                W = wk[:, n % 2, :].rearrange("p (g k) -> p g k", g=3)
                b = negm[:, n % 2:n % 2 + 1]
                s.activation(W[:, 0, 0:K0], ps[:, 2, 0:K0], ACT.Exp, bias=b, accum_out=d[:, 0:1])
                s.activation(W[:, 1:3, 0:K], ps[:, 3:5, 0:K], ACT.Exp, bias=b,
                             accum_out=d[:, 1:2]).then_inc(S_["c_exp"], 1)

            def c_t(k):
                N = len(DG[k][1]) * P
                act.wait_ge(S_["c_t_pe"], k + 1)
                if k >= 2:
                    act.wait_ge(S_["c_o_pe"], k - 1)
                else:
                    act.wait_ge(S_["d_o_pe"], NT * HB)
                s.activation(PT[:, k % 2, 0:N], ps[:, 5 + k % 2, 0:N], ACT.Copy).then_inc(S_["c_t_ok"], 1)

            def krows(u):
                i, groups = KU[u]
                act.wait_ge(S_["kr_pe"], u + 1)
                if u >= 2:
                    act.wait_ge(kr_out[u % 2], 16 * sum(KR_DMAS[u % 2:u:2]))
                else:
                    act.wait_ge(S_["s_o_pe"], 1)
                w = SLAB if groups is None else 256 * len(groups)
                s.activation(kst[u % 2][:, 0:w], ps[:, u % 2, 0:w], ACT.Copy).then_inc(S_["kr_ok"], 1)
                act.wait_ge(S_["kr_ok"], u + 1)
                if groups is None:
                    act.dma_start(o["k_diff_prompt"][0, 0, i * P:(i + 1) * P].rearrange("t h m d -> t (h m d)"),
                                  kst[u % 2][:, 0:SLAB]).then_inc(kr_out[u % 2], 16)
                    return
                for k, g in enumerate(groups):
                    lo = i * P - (SEQ - WIN[g])
                    act.dma_start(o["win_prompt"][g][0, 0, lo:lo + P, 0].rearrange("t h d -> t (h d)"),
                                  kst[u % 2][:, 256 * k:256 * (k + 1)]).then_inc(kr_out[u % 2], 16)

            def dec_soft():
                act.wait_ge(S_["row_ok"], 1)
                s.activation(RD, RD, ACT.Exp, bias=st96[:, 0:1], accum_out=st96[:, 1:2])
                s.activation(RC, RC, ACT.Exp, bias=st32[:, 0:1], accum_out=st32[:, 1:2]).then_inc(S_["row_e"], 1)

            def dst_v(b):
                if b == 0:
                    act.wait_ge(S_["h_st_ok"], NT)
                    act.wait_ge(S_["h_out_pe"], NT)
                    s.activation(fex, bF[:, :, SEQ:NTOK], ACT.Exp).then_inc(S_["fx_ok"], 1)

            def ro(i):
                act.wait_ge(S_["ro_sq"], i + 1)
                q = small[:, 160 + 12 * (i % 2):172 + 12 * (i % 2)]
                seq(s.activation(q, q, ACT.Ln, bias=epsc, scale=1.0 / 64))
                s.activation(q, q, ACT.Exp, scale=-0.5).then_inc(S_["ro_e"], 1)

            def mt(i):
                r = tile_rows(i)
                act.wait_ge(S_["mt_pe"], i + 1)
                s.activation(xT[:, :, i * P:i * P + r] if i < NT else xS[:, :, 0:NS],
                             ps[:, MT_BANK[i]:MT_BANK[i] + 2, :].rearrange("p b (c t) -> p (b c) t", c=4)[:, :, 0:r],
                             ACT.Copy).then_inc(S_["mt_ok"], 1)

            does = dict(proj=proj, samp_t=samp_t, act_fn=act_fn, log_f=log_f, gate_fn=gate_fn, lev_q=lev_q, io_a=io_a, kt=kt, h_out=h_out, d_s=d_s,
                        d_t=d_t, d_pv=d_pv, c_s=c_s, c_t=c_t, krows=krows, dec_soft=dec_soft, dst_v=dst_v,
                        ro=ro, mt=mt)
            for step, *arg in STEPS:
                if step in does:
                    does[step](*arg)

            mt(NT)

            def inv_rms(i, sem_name):
                r = tile_rows(i)
                seq(s.activation(PTf[0:r], XM[0:r, i, :], ACT.Square,
                                 accum_out=ssq[0:r, i:i + 1]))
                seq(s.activation(ssq[0:r, i:i + 1], ssq[0:r, i:i + 1], ACT.Ln, bias=epsc[0:r, :], scale=1.0 / D))
                s.activation(rstd[0:r, i:i + 1], ssq[0:r, i:i + 1], ACT.Exp, scale=-0.5).then_inc(S_[sem_name], 1)

            def sample_parts(bank, count):
                act.wait_ge(S_["sp_pe"], count)
                s.activation(PTf, ps[:, bank:bank + 2, :].rearrange("p b n -> p (b n)"),
                             ACT.Copy).then_inc(S_["sp_cp"], 1)

            for i in range(T5):
                if i == NT:
                    sample_parts(2, 1)
                act.wait_ge(S_["hres_ok"], i + 1)
                inv_rms(i, "n2_e")

            def pcolumns(i):
                r = tile_rows(i)
                act.wait_ge(S_["pp_t"], i + 1)
                if i >= 2:
                    act.wait_ge(S_["pp_m"], i - 1)
                s.activation(pTt[i % 2][:, :, 0:r], ps[:, 2 + i % 2, 0:2 * P].rearrange("p (c t) -> p c t", c=PC)[:, :, 0:r],
                             ACT.Copy).then_inc(S_["pp_c"], 1)

            def pproducts(i):
                r = tile_rows(i)
                act.wait_ge(S_["pp_m"], i + 1)
                s.activation(pproj[i][0:r], ps[0:r, 4 + 2 * (i % 2):6 + 2 * (i % 2), :].rearrange("p b n -> p (b n)"),
                             ACT.Copy).then_inc(S_["pp_o"], 1)

            pcolumns(0)
            pcolumns(1)
            act.wait_ge(S_["rt_e"], 1)
            s.activation(t4, t4, ACT.Exp).then_inc(S_["gexp"], 1)
            act.wait_ge(S_["rt_e"], 2)
            s.activation(e2, e2, ACT.Exp).then_inc(S_["gexp"], 1)
            pproducts(0)
            pproducts(1)
            pcolumns(2)
            pcolumns(3)
            pproducts(2)
            pcolumns(4)
            pproducts(3)
            pproducts(4)

            act.wait_ge(S_["tab_rdy"], 1)
            npairs = act.value_load(npi[0:1, 0:1], min_val=NE // 2, max_val=MAXT // 2)
            last_pair = act.value_load(npi[0:1, 1:2], min_val=NE // 2 - 1, max_val=MAXT // 2 - 1)
            yrow = Yd.rearrange("(j p) n -> j p n", p=P)

            def silu(j1, b):
                act.wait_ge(S_["g_pe"], j1)
                if b is not None:
                    s.activation(hb[b], ps[:, 2 + 2 * b, :], ACT.Silu).then_inc(S_["sil_ok"], 1)

            def back(j1, j, b, n_st):
                act.wait_ge(S_["ht_pe"], j1)
                s.activation(dflat[:, (2 + b) * FF:(3 + b) * FF], ps[:, 2 + 2 * b, :], ACT.Copy).then_inc(S_["ht_ok"], 1)
                act.wait_ge(S_["y_pe"], j1)
                if n_st is not None:
                    act.wait_ge(ystore[b], n_st)
                s.activation(yb_[b][:, 0:FF], ps[:, 6, :], ACT.Copy).then_inc(S_["ya_ok"], 1)
                act.wait_ge(S_["ya_ok"], j1)
                act.wait_ge(S_["yb_ok"], j1)
                act.dma_start(yrow[j].rearrange("o p n -> p o n"), yb_[b].unsqueeze(1)).then_inc(ystore[b], 16)

            silu(1, 0)
            silu(2, 1)
            act.wait_ge(S_["u_st"], 16 * T5)
            back(1, slice(0, 1), 0, None)
            silu(3, 0)
            back(2, slice(1, 2), 1, None)
            with act.Fori(1, last_pair) as i:
                silu(2 * i + 2, 1)
                back(2 * i + 1, bass.ds(2 * i, 1), 0, i * 16)
                silu(2 * i + 3, 0)
                back(2 * i + 2, bass.ds(2 * i + 1, 1), 1, i * 16)
            silu(npairs * 2, 1)
            back(last_pair * 2 + 1, bass.ds(last_pair * 2, 1), 0, last_pair * 16)
            back(npairs * 2, bass.ds(last_pair * 2 + 1, 1), 1, last_pair * 16)

            def gate(i):
                r = tile_rows(i)
                act.wait_ge(S_["pg_pe"], i + 1)
                b = 4 + 2 * (i % 2)
                s.activation(sig[i % 2][0:r], ps[0:r, b:b + 2, :].rearrange("p b n -> p (b n)"),
                             ACT.Sigmoid).then_inc(S_["pg_sig"], 1)

            for i in range(T5):
                act.wait_ge(S_["comb_ok"], i + 1)
                inv_rms(i, "hn_e")
                if i:
                    gate(i - 1)
                if i >= 2:
                    act.wait_ge(S_["po_ok"], i - 1)
                    inv_rms(i - 2, "n4_e")
            sample_parts(4, 2)
            gate(NT)
            for i in range(T5 - 2, T5):
                act.wait_ge(S_["po_ok"], i + 1)
                inv_rms(i, "n4_e")

        @block.vector
        def _(dve):
            n = [0]
            v = nc.vector

            def seq(ins):
                n[0] += 1
                ins.then_inc(S_["dve_seq"], 1)
                dve.wait_ge(S_["dve_seq"], n[0])

            seq(v.memset(epsc, EPS))
            dve.wait_ge(S_["gain_pe"], 1)
            v.tensor_copy(gains[:], ps[:, 7, 0:27]).then_inc(S_["gain_ok"], 1)
            dve.wait_ge(S_["gain_ok"], 1)
            for i in range(NT + 1):
                r = tile_rows(i)
                dve.wait_ge(S_["rstd_ok"], i + 1)
                v.tensor_scalar(XM[0:r, i, :], XM[0:r, i, :], rstd[0:r, i:i + 1], None,
                                ALU.mult).then_inc(S_["xn_ok"], 1)
                dve.wait_ge(S_["xt_pe"], i + 1)
                for h in range(2):
                    v.tensor_tensor(xT[:, 4 * h:4 * h + 4, i * P:i * P + r],
                                    ps[:, 2 * (i % 2) + h, :].rearrange("p (c t) -> p c t", c=4)[:, :, 0:r],
                                    f2(gains[:, 4 * h:4 * h + 4], r), ALU.mult).then_inc(S_["xt_ok"], 1)
            v.memset(xS, 0.0)
            seq(v.memset(one_col, 0.0))
            v.memset(one_col[:, NS:NS + 1], 1.0)
            seq(v.tensor_reduce(sel4, ident[:].rearrange("p (a n) -> p n a", a=4)[:, 0:NS, :], AX.X, ALU.add))
            v.tensor_copy(xS[:, :, 0:NS], xT[:, :, SEQ:NTOK]).then_inc(S_["xt_ok"], 1)
            seq(v.memset(XM[:, NT, :], 0.0))
            seq(v.memset(gT[:, NT, :], 0.0))
            seq(v.tensor_tensor(lb, gains[:, 24:27], gains[:, 24:27], ALU.subtract))
            v.memset(tmp[:, 0:4], 0.0).then_inc(S_["lb_e"], 1)
            dve.wait_ge(S_["lb_ok"], 1)
            seq(v.reciprocal(omlb, lb))
            seq(v.tensor_tensor(lb, lb, omlb, ALU.mult))
            seq(v.tensor_tensor(lb, lb, lb, ALU.subtract))
            seq(v.tensor_scalar(omlb, lb, -1.0, 1.0, ALU.mult, ALU.add))
            dve.wait_ge(S_["cload"], 16 * 10)
            lv = lamb[:].rearrange("p (a b d) -> p a b d", a=2, b=2)
            seq(v.tensor_tensor(small[:, 320:384].rearrange("p (a d) -> p a d", a=2), lv[:, :, 0], lv[:, :, 1], ALU.mult))
            v.tensor_reduce(tmp[:, 0:2], small[:, 320:384].rearrange("p (a d) -> p a d", a=2), AX.X,
                            ALU.add).then_inc(S_["lam_s"], 1)
            dve.wait_ge(S_["lam_e"], 1)
            seq(v.tensor_tensor(lam, tmp[:, 0:1], tmp[:, 1:2], ALU.subtract))
            seq(v.tensor_scalar(lam, lam, LAM_INIT, None, ALU.add))
            seq(v.tensor_scalar(nlam, lam, -1.0, None, ALU.mult))
            seq(v.tensor_scalar(dg[:], dg[:], 1.0 - LAM_INIT, None, ALU.mult))
            dve.wait_ge(S_["consts"], 3)
            dist = iT[:, 0, 0:P].bitcast(I32)
            rowi = iT[:, 0, P:2 * P].bitcast(I32)
            coli = iT[:, 0, 2 * P:3 * P].bitcast(I32)
            md = iT[:, 1, 0:P].bitcast(I32)
            xr = iT[:, 1, P:2 * P].bitcast(I32)
            lt = iT[:, 1, 2 * P:3 * P]
            xf = iT[:, 2, 0:P]
            ge = [iT[:, 2, P:2 * P], iT[:, 2, 2 * P:3 * P]]
            for k in range(2):
                seq(v.tensor_scalar(md, dist, (3, 15)[k], None, ALU.bitwise_and))
                seq(v.tensor_scalar(mstride[:, k, 0:P], md, 0.0, NEG, ALU.is_gt, ALU.mult))
                seq(v.tensor_copy(mstride[:, k, P:NT * P].rearrange("p (b n) -> p b n", b=NT - 1),
                                  mstride[:, k, 0:P].unsqueeze(1).to_broadcast([P, NT - 1, P])))
            seq(v.tensor_tensor(xr, rowi, coli, ALU.bitwise_xor))
            seq(v.tensor_tensor(lt, coli, rowi, ALU.is_gt))
            seq(v.tensor_tensor(xf, xr, lt, ALU.mult))
            seq(v.tensor_scalar(ge[0], xf, 1.0, None, ALU.is_ge))
            for l in range(LEVELS):
                seq(v.tensor_scalar(ge[(l + 1) % 2], xf, 2.0 ** (l + 1), None, ALU.is_ge))
                seq(v.tensor_tensor(lmask[:, l], ge[l % 2], ge[(l + 1) % 2], ALU.subtract))
            v.memset(small[:, 256:257], 0.0).then_inc(S_["tab_ok"], 1)

            def act_fn():
                dve.wait_ge(S_["prep_q"], 1)
                v.tensor_scalar(qF, qF, SCALE_A, None, ALU.mult).then_inc(S_["prep_ok"], 1)
                dve.wait_ge(S_["prep_e"], 2)
                v.tensor_tensor(kF, kF, f2(omlb, NTOK), ALU.mult).then_inc(S_["prep_ok"], 1)
                for c in range(3):
                    fb = wk[:].rearrange("p a n -> p (a n)")[:, c * NTOK:(c + 1) * NTOK]
                    seq(v.tensor_scalar(bF[:, c], bF[:, c], omlb[:, c:c + 1], lb[:, c:c + 1], ALU.mult, ALU.add))
                    seq(v.tensor_scalar(bF[:, c], bF[:, c], float(np.finfo(np.float32).tiny), None, ALU.max))
                    seq(v.tensor_scalar(fb, bF[:, c], LN_SPLIT, 1.0 / LN_SPLIT, ALU.min, ALU.mult))
                    v.tensor_scalar(bF[:, c], bF[:, c], LN_SPLIT, None, ALU.max).then_inc(S_["prep_f"], 1)

            def log_f():
                for c in range(3):
                    fb = wk[:].rearrange("p a n -> p (a n)")[:, c * NTOK:(c + 1) * NTOK]
                    dve.wait_ge(S_["prep_ln"], c + 1)
                    seq(v.tensor_tensor(bF[:, c], bF[:, c], fb, ALU.add))
                    for i in range(NT):
                        sl = bF[:, c, i * P:(i + 1) * P]
                        last = v.tensor_tensor_scan(sl, ones[:], sl, 0.0, ALU.mult, ALU.add)
                    seq(last)
                v.memset(small[:, 257:258], 0.0).then_inc(S_["prep_ok"], 1)

            def gate_fn():
                dve.wait_ge(S_["unit_ok"], max(LASTU[3], SUMU[3]) + 1)
                v.tensor_copy(gT[0:NS, NT, :], samp[:, 3 * SLAB:4 * SLAB]).then_inc(S_["gate_e"], 1)
                dve.wait_ge(S_["gate_ok"], 1)
                gt = gT.rearrange("p i n -> p (i n)").rearrange("p (h v) -> p h v", v=64)
                seq(v.tensor_tensor(gt, gt, hg[:].unsqueeze(1).to_broadcast([P, 30, 64]), ALU.mult))

            def lev_d(j):
                i, l = divmod(j, LEVELS)
                B = 2 ** l
                b4 = rows_of(bF, i).rearrange("p c (n w) -> p c n w", w=2 * B)
                N = P // (2 * B)
                out = work[:, (j % 2) * SLAB:(j % 2 + 1) * SLAB].rearrange("p (c n w) -> p c n w", c=3, n=N)
                if N == 1:
                    v.tensor_tensor(out[:, :, 0], b4[:, :, 0], f2(b4[:, :, 0, B - 1], 2 * B),
                                    ALU.subtract).then_inc(S_["lev_d"], 1)
                else:
                    v.tensor_tensor(out, b4, b4[:, :, :, B - 1:B].to_broadcast([P, 3, N, 2 * B]),
                                    ALU.subtract).then_inc(S_["lev_d"], 1)

            def lev_q(j):
                i, l = divmod(j, LEVELS)
                B = 2 ** l
                N = P // (2 * B)
                dve.wait_ge(S_["lev_e"], j + 1)
                if j >= 2:
                    i2, l2 = divmod(j - 2, LEVELS)
                    dve.wait_ge(S_["lev_pe"], i2 * (LEVELS + 1) + l2 + 2)
                E = work[:, (j % 2) * SLAB:(j % 2 + 1) * SLAB].rearrange("p (c n e t) -> p c n e t", c=3, n=N, e=2)
                QK = work[:, (2 + j % 2) * SLAB:(3 + j % 2) * SLAB].rearrange("p (c n e t) -> p c n e t", c=3, n=N, e=2)
                src = [rows_of(f, i).rearrange("p c (n e t) -> p c n e t", n=N, e=2) for f in (kF, qF)]
                for e in (0, 1):
                    o_, a_, b_ = QK[:, :, :, e], E[:, :, :, e], src[e][:, :, :, e]
                    if N == 1:
                        o_, a_, b_ = o_[:, :, 0], a_[:, :, 0], b_[:, :, 0]
                    last = v.tensor_tensor(o_, a_, b_, ALU.mult)
                last.then_inc(S_["lev_q"], 1)

            def lev_cp(i, l):
                k = i * (LEVELS + 1) + l
                dve.wait_ge(S_["lev_pe"], k + 1)
                if l == 0 and i:
                    dve.wait_ge(S_["h_out_pe"], i)
                for e in range(2):
                    att = work2[:, e * SLAB:(e + 1) * SLAB].rearrange("p (c t) -> p c t", c=3)
                    src = ps[:, 2 + 2 * (k % 2) + e, 0:SLAB].rearrange("p (c t) -> p c t", c=3)
                    if l == 0:
                        last = v.tensor_tensor(att, src, ident[:].unsqueeze(1).to_broadcast([P, 3, P]), ALU.mult)
                    else:
                        last = v.copy_predicated(att, lmask[:, l - 1].unsqueeze(1).to_broadcast([P, 3, P]), src)
                last.then_inc(S_["lev_cp"], 1)
                dve.wait_ge(S_["lev_cp"], k + 1)

            def io_a(i):
                if i:
                    dve.wait_ge(S_["kt_pe"], i)
                b = rows_of(bF, i)
                v.tensor_tensor(work2[:, 1152:1536].rearrange("p (c t) -> p c t", c=3), b,
                                f2(b[:, :, P - 1], P), ALU.subtract).then_inc(S_["io_d"], 1)

            def io_b(i):
                dve.wait_ge(S_["io_e"], i + 1)
                qI = work2[:, 768:1152].rearrange("p (c t) -> p c t", c=3)
                kI = work2[:, 1152:1536].rearrange("p (c t) -> p c t", c=3)
                seq(v.tensor_copy(ebl, qI[:, :, P - 1]))
                v.tensor_tensor(qI, qI, rows_of(qF, i), ALU.mult)
                v.tensor_tensor(kI, kI, rows_of(kF, i), ALU.mult).then_inc(S_["io_ok"], 1)

            def h_state(i):
                dve.wait_ge(S_["h_st_pe"], i + 1)
                src = ps[:, 7, 0:SLAB].rearrange("p (c n) -> p c n", c=3)
                bm = blk[:].unsqueeze(1).to_broadcast([P, 3, P])
                if i:
                    dve.wait_ge(S_["h_out_pe"], i + 1)
                    seq(v.tensor_tensor(Sadd, src, bm, ALU.mult))
                    seq(v.tensor_tensor(S, S, f2(ebl, P), ALU.mult))
                    v.tensor_tensor(S, S, Sadd, ALU.add).then_inc(S_["h_st_ok"], 1)
                else:
                    dve.wait_ge(S_["consts"], 5)
                    v.tensor_tensor(S, src, bm, ALU.mult).then_inc(S_["h_st_ok"], 1)
                dve.wait_ge(S_["h_st_ok"], i + 1)

            def d_s(n):
                K = (n // HB + 1) * P
                dve.wait_ge(S_["d_s_pe"], n + 1)
                if n >= 2:
                    dve.wait_ge(S_["d_exp"], n - 1)
                v.tensor_reduce(negm[:, 2 * (n % 2):2 * (n % 2) + 2], ps[:, 2 + 2 * (n % 2):4 + 2 * (n % 2), 0:K],
                                AX.X, ALU.max, negate=True).then_inc(S_["d_max"], 1)

            def d_t(n):
                K = (n // HB + 1) * P
                dve.wait_ge(S_["d_exp"], n + 1)
                r = rec[:, 2 * (n % 2):2 * (n % 2) + 2]
                W = wk[:, n % 2, :]
                seq(v.reciprocal(r, den[:, 2 * (n % 2):2 * (n % 2) + 2]))
                seq(v.tensor_scalar(r[:, 1:2], r[:, 1:2], nlam, None, ALU.mult))
                seq(v.tensor_scalar(W[:, 0:K], W[:, 0:K], r[:, 0:1], None, ALU.mult))
                v.scalar_tensor_tensor(out=W[:, 0:K], in0=W[:, SEQ:SEQ + K], scalar=r[:, 1:2], in1=W[:, 0:K],
                                       op0=ALU.mult, op1=ALU.add).then_inc(S_["d_a"], 1)

            def c_s(n):
                i, h = divmod(n, HC)
                K = (i + 1) * P
                K0 = min(i + 1, 2) * P
                dve.wait_ge(S_["c_s_pe"], n + 1)
                if n >= 2:
                    dve.wait_ge(S_["c_exp"], n - 1)
                v.tensor_reduce(tmp[:, 8:9], ps[:, 2, 0:K0], AX.X, ALU.max, negate=True)
                seq(v.tensor_reduce(tmp[:, 9:10], ps[:, 3:5, 0:K], AX.XY, ALU.max, negate=True))
                v.tensor_tensor(negm[:, n % 2:n % 2 + 1], tmp[:, 8:9], tmp[:, 9:10], ALU.min).then_inc(S_["c_max"], 1)
                dve.wait_ge(S_["c_max"], n + 1)

            def c_pv(k):
                n = DG[k][0]
                i, h = divmod(n, HC)
                if DG[k][3] and h == HC - 1:
                    dve.wait_ge(S_["c_exp"], n + 1)
                    d = small[:, 128 + 8 * (i % 2):136 + 8 * (i % 2)].rearrange("p (h e) -> p h e", e=2)
                    r = small[:, 144:148]
                    seq(v.tensor_tensor(r, d[:, :, 0], d[:, :, 1], ALU.add))
                    seq(v.reciprocal(r, r))
                    dve.wait_ge(S_["c_o_pe"], k + 1)
                    v.tensor_tensor(XM[:, i, 2 * SLAB:D].rearrange("p (h d) -> p h d", h=HC),
                                    ps[:, 7, 0:256].rearrange("p (h d) -> p h d", h=HC), f2(r, 64),
                                    ALU.mult).then_inc(S_["c_o_ok"], 1)

            samp3 = samp[:, C_COL:].rearrange("b (g s n) -> b g s n", g=NG, s=3)

            def dec_new():
                seq(v.tensor_reduce(hms, ident[0:96, 0:96].rearrange("p (b r) -> p r b", b=NS), AX.X, ALU.add))
                seq(v.tensor_reduce(mB, ident[0:96, 0:96].rearrange("p (b r) -> p b r", b=NS), AX.X, ALU.add))
                seq(v.tensor_reduce(hsel, ident[0:32, 0:32].rearrange("p (b r) -> p r b", b=NS), AX.X, ALU.add))
                seq(v.tensor_reduce(mC, ident[0:32, 0:32].rearrange("p (b r) -> p b r", b=NS), AX.X, ALU.add))
                seq(v.tensor_reduce(st96[:, 3:4], hms.rearrange("p (h m) -> p m h", m=2)[:, 1:2, :], AX.X, ALU.add))
                seq(v.tensor_scalar(st96[:, 4:5], lam[0:96, :], 1.0, None, ALU.add))
                seq(v.tensor_tensor(st96[:, 3:4], st96[:, 3:4], st96[:, 4:5], ALU.mult))
                seq(v.tensor_scalar(st96[:, 3:4], st96[:, 3:4], -1.0, 1.0, ALU.mult, ALU.add))
                seq(v.tensor_tensor(dcst[:, 0:SLAB], samp[:, 4 * SLAB:5 * SLAB], samp[:, 5 * SLAB:6 * SLAB], ALU.mult))
                seq(v.tensor_reduce(snd, dcst[:, 0:SLAB].rearrange("p (r d) -> p r d", d=32), AX.X, ALU.add))
                for g in range(NG):
                    seq(v.tensor_tensor(dcst[:, 0:256], samp3[:, g, 0], samp3[:, g, 1], ALU.mult))
                    seq(v.tensor_reduce(snc[:, g], dcst[:, 0:256].rearrange("p (r d) -> p r d", d=64), AX.X, ALU.add))
                seq(v.tensor_tensor(MD.rearrange("p (b r) -> p b r", b=NS), snd.unsqueeze(1).to_broadcast([NS, NS, 12]),
                                    f2(ident[0:NS, 0:NS], 12), ALU.mult))
                for g in range(NG):
                    last = v.tensor_tensor(MC[:, g], snc[:, g].unsqueeze(1).to_broadcast([NS, NS, HC]),
                                           f2(ident[0:NS, 0:NS], HC), ALU.mult)
                last.then_inc(S_["new_ok"], 1)

            def dec_q(b):
                kp, kd = kpage[b % 2], kdil[b % 2]
                if b == 0:
                    dve.wait_ge(S_["s_o_pe"], 1)
                dve.wait_ge(S_["bq_ok"], b + 1)
                v.tensor_reduce(SD[:, :, 12 * b:12 * b + 12], kp.rearrange("p j (r d) -> p j r d", d=32), AX.X, ALU.add)
                v.tensor_reduce(SC[:, 0:2, 4 * b:4 * b + 4], kd[:, 0:2].rearrange("p g (r d) -> p g r d", d=64),
                                AX.X, ALU.add)
                v.tensor_reduce(SC[0:32, 2, 4 * b:4 * b + 4], kd[0:32, 2].rearrange("p (r d) -> p r d", d=64), AX.X,
                                ALU.add).then_inc(S_["kused"], 1)

            def dec_soft():
                dve.wait_ge(S_["sc_pe"], 1)
                seq(v.tensor_scalar(RD[:, 0:PAST], ps[0:96, 0, :], SCALE_B, None, ALU.mult))
                seq(v.tensor_scalar(RD[:, PAST:PAST + 1], ps[0:96, 1, 320:321], SCALE_B, None, ALU.mult))
                seq(v.tensor_scalar(RC[:, 0:NDIL], ps[0:32, 1, 0:NDIL], SCALE_C, None, ALU.mult))
                seq(v.tensor_scalar(RC[:, NDIL:NDIL + NG], ps[0:32, 1, 321:321 + NG], SCALE_C, None, ALU.mult))
                v.tensor_reduce(st96[:, 0:1], RD, AX.X, ALU.max, negate=True)
                v.tensor_reduce(st32[:, 0:1], RC, AX.X, ALU.max, negate=True).then_inc(S_["row_ok"], 1)
                dve.wait_ge(S_["row_e"], 1)
                seq(v.reciprocal(st96[:, 2:3], st96[:, 1:2]))
                seq(v.reciprocal(st32[:, 2:3], st32[:, 1:2]))
                seq(v.tensor_tensor(st96[:, 2:3], st96[:, 2:3], st96[:, 3:4], ALU.mult))
                seq(v.tensor_scalar(RD, RD, st96[:, 2:3], None, ALU.mult))
                seq(v.tensor_scalar(RC, RC, st32[:, 2:3], None, ALU.mult))
                seq(v.tensor_scalar(LD, mB, RD[:, PAST:PAST + 1], None, ALU.mult))
                for g in range(NG):
                    last = v.tensor_scalar(LC[:, g], mC, RC[:, NDIL + g:NDIL + g + 1], None, ALU.mult)
                last.then_inc(S_["w_ok"], 1)

            def dec_wt():
                dve.wait_ge(S_["kr_pe"], len(KU))
                dve.wait_ge(S_["d_s_pe"], NT * HB)
                v.memset(ADz, 0.0)
                seq(v.memset(ACz, 0.0))
                dve.wait_ge(S_["wt_pe"], 1)
                for j in range(PAGES):
                    v.tensor_reduce(ADz[:, j, :, 0:HB],
                                    ps[:, 0, j * 96:(j + 1) * 96].rearrange("p (b h m) -> p b h m", b=NS, m=2), AX.X, ALU.add)
                for g in range(NG):
                    r = (P, P, 32)[g]
                    v.tensor_copy(ACz[0:r, g, :, 0:HC], ps[0:r, 1, 32 * g:32 * g + 32].rearrange("p (b h) -> p b h", b=NS))
                v.tensor_reduce(anew[:, 0:6], ps[0:NS, 1, 128:140].rearrange("p (h m) -> p h m", m=2), AX.X, ALU.add)
                v.tensor_copy(anew[:, 8:20], ps[0:NS, 1, 144:156]).then_inc(S_["aw_ok"], 1)

            def dec_v(u):
                b, win = divmod(u, 2)
                dve.wait_ge(S_["pv_pe"], u + 1)
                if win:
                    v.tensor_tensor(prodC[:, b].rearrange("p (h d) -> p h d", h=HC),
                                    ps[0:96, 1, 0:256].rearrange("p (h d) -> p h d", h=HC),
                                    f2(sel4[0:96, 0:HC], 64), ALU.mult).then_inc(S_["pv_ok"], 1)
                else:
                    if b == 0:
                        dve.wait_ge(S_["kused"], NS)
                    v.tensor_tensor(prodD[:, b].rearrange("p (h d) -> p h d", h=HB),
                                    ps[:, 0, 0:SLAB].rearrange("p (h d) -> p h d", h=HB),
                                    f2(sel4[:, 0:HB], 64), ALU.mult).then_inc(S_["pv_ok"], 1)

            def dst_v(b):
                if b == 0:
                    dve.wait_ge(S_["stload"], 16 * 6)
                    dve.wait_ge(S_["h_out_pe"], NT)
                dve.wait_ge(S_["vb_pe"], b + 1)
                vb = ps[:, 6 + b % 2, 0:SLAB].rearrange("p (c e v) -> p c e v", c=3, e=2)
                for e in range(2):
                    h = slice(64 * e, 64 * e + 64)
                    last = v.tensor_tensor(stK[h, b], vb[h, :, e],
                                           f2(kF[h, :, SEQ + b], 64), ALU.mult)
                last.then_inc(S_["kv_ok"], 1)

            def dst_new():
                seq(v.memset(id8, 0.0))
                seq(v.memset(id8[:, 0:64:9], 1.0))
                dve.wait_ge(S_["kv_ok"], NS)
                dve.wait_ge(S_["fx_ok"], 1)
                for c in range(3):
                    seq(v.tensor_tensor(stS[:, :, c], stS[:, :, c], f2(fex[:, c], 64), ALU.mult))
                seq(v.tensor_tensor(Qz, id8.rearrange("p (b e) -> p b e", b=NS).unsqueeze(1).to_broadcast([P, 3, NS, NS]),
                                    qF[:, :, SEQ:NTOK].unsqueeze(3).to_broadcast([P, 3, NS, NS]), ALU.mult))
                v.tensor_tensor(stS, stS, stK, ALU.add).then_inc(S_["s_new"], 1)

            def dst_o():
                dve.wait_ge(S_["s_o_pe"], 1)
                for e in range(2):
                    last = v.tensor_copy(XM[0:NS, NT, 0:SLAB].rearrange("p (c e v) -> p c e v", c=3, e=2)[:, :, e],
                                         ps[0:NS, 6 + e, 0:192].rearrange("p (c v) -> p c v", c=3))
                last.then_inc(S_["s_o_ok"], 1)

            def dec_out():
                dve.wait_ge(S_["ot_pe"], 2)
                md = dcst[:, 0:SLAB].rearrange("p (h d) -> p h d", h=HB)
                seq(v.tensor_tensor(md, samp[:, 6 * SLAB:7 * SLAB].rearrange("p (h d) -> p h d", h=HB),
                                    f2(anew[:, 0:6], 64), ALU.mult))
                seq(v.tensor_tensor(XM[0:NS, NT, SLAB:2 * SLAB], dcst[:, 0:SLAB], ps[0:NS, 0, 0:SLAB], ALU.add))
                out = XM[0:NS, NT, 2 * SLAB:D]
                seq(v.tensor_copy(out, ps[0:NS, 1, 0:256]))
                for g in range(NG):
                    seq(v.tensor_tensor(dcst[:, 0:256].rearrange("p (h d) -> p h d", h=HC),
                                        samp3[:, g, 2].rearrange("p (h d) -> p h d", h=HC),
                                        f2(anew[:, 8 + 4 * g:12 + 4 * g], 64), ALU.mult))
                    ins = v.tensor_tensor(out, out, dcst[:, 0:256], ALU.add)
                    if g < NG - 1:
                        seq(ins)
                ins.then_inc(S_["dec_done"], 1)
                dve.wait_ge(S_["dec_done"], 1)

            def ro(i):
                r = P
                if i < NT:
                    dve.wait_ge(S_["h_out_ok"], i + 1)
                    dve.wait_ge(S_["d_o_ok"], i + 1)
                if i == 0:
                    dve.wait_ge(S_["s_o_pe"], 1)
                q = small[:, 160 + 12 * (i % 2):172 + 12 * (i % 2)]
                X = XM[:, i, 0:2 * SLAB]
                sq = rosq
                X3 = X.rearrange("p (h v) -> p h v", h=12)
                seq(v.tensor_tensor(sq, X, X, ALU.mult))
                v.tensor_reduce(q, sq.rearrange("p (h v) -> p h v", h=12), AX.X, ALU.add).then_inc(S_["ro_sq"], 1)
                dve.wait_ge(S_["ro_e"], i + 1)
                seq(v.tensor_tensor(X3, X3, f2(q, 64), ALU.mult))
                v.tensor_tensor(X[:, 0:SLAB], X[:, 0:SLAB], gT[:, i], ALU.mult)
                v.tensor_tensor(X3[:, 6:12], X3[:, 6:12], dg[:].unsqueeze(1).to_broadcast([P, 6, 64]),
                                ALU.mult).then_inc(S_["ro_ok"], 1)

            def finish(i):
                r = tile_rows(i)
                b = i % 2
                dve.wait_ge(S_["pg_sig"], i + 1)
                if i == 0:
                    dve.wait_ge(S_["pp_o"], T5)
                seq(v.tensor_tensor(sig[b][0:r], sig[b][0:r], pproj[i][0:r], ALU.mult))
                v.tensor_tensor(XM[0:r, i, :], XM[0:r, i, :], sig[b][0:r], ALU.add).then_inc(S_["po_ok"], 1)

            def last_norm(i):
                r = tile_rows(i)
                dve.wait_ge(S_["n4_e"], i + 1)
                dve.wait_ge(S_["pleload"], 32)
                v.scalar_tensor_tensor(out=XM[0:r, i, :], in0=XM[0:r, i, :], scalar=rstd[0:r, i:i + 1],
                                       in1=nfin[0:r, :], op0=ALU.mult, op1=ALU.mult).then_inc(S_["y_ok"], 1)

            does = dict(act_fn=act_fn, log_f=log_f, gate_fn=gate_fn, lev_d=lev_d, lev_q=lev_q, lev_cp=lev_cp, io_a=io_a, io_b=io_b, h_state=h_state,
                        d_s=d_s, d_t=d_t, c_s=c_s, c_pv=c_pv, dec_new=dec_new, dec_q=dec_q, dec_soft=dec_soft,
                        dec_wt=dec_wt, dec_v=dec_v, dst_v=dst_v, dst_new=dst_new, dst_o=dst_o, dec_out=dec_out, ro=ro)
            for step, *arg in STEPS:
                if step in does:
                    does[step](*arg)

            for i in range(T5):
                r = tile_rows(i)
                bk = 2 + 2 * (i % 2)
                dve.wait_ge(xload[i], 32)
                dve.wait_ge(S_["wo_pe"], i + 1)
                v.tensor_tensor(XM[0:r, i, :], XM[0:r, i, :], ps[0:r, bk:bk + 2, :].rearrange("p b n -> p (b n)"),
                                ALU.add).then_inc(S_["hres_ok"], 1)
                dve.wait_ge(S_["n2_e"], i + 1)
                if i >= 3:
                    dve.wait_ge(S_["u_st"], 16 * i)
                    dve.wait_ge(S_["ut_pe"], i - 2)
                if i == 0:
                    dve.wait_ge(kr_out[0], KR_ALL[0])
                    dve.wait_ge(kr_out[1], KR_ALL[1])
                v.tensor_scalar(Ub[i % 3][0:r, :], XM[0:r, i, :], rstd[0:r, i:i + 1], None,
                                ALU.mult).then_inc(S_["u_ok"], 1)
                dve.wait_ge(S_["ut_pe"], i + 1)
                if i >= 4:
                    dve.wait_ge(S_["rl_pe"], i - 3)
                v.tensor_tensor(RT[i % 4][:, :, 0:r], ps[:, 6:8, :].rearrange("p b (c t) -> p (b c) t", c=4)[:, :, 0:r],
                                f2(gains[:, 8:16], r), ALU.mult).then_inc(S_["ut_ok"], 1)
            dve.wait_ge(S_["iot"], 1)
            dve.wait_ge(S_["rl_pe"], T5)
            seq(v.tensor_tensor(L[:, 0:NT], ps[:, 0, 0:80].rearrange("p (i n) -> p i n", i=NT),
                                rbias[:].unsqueeze(1).to_broadcast([P, NT, 20]), ALU.add))
            seq(v.tensor_tensor(L[0:NS, NT], ps[0:NS, 0, 80:100], rbias[0:NS, :], ALU.add))
            seq(v.tensor_copy(erow, iti[:, 0:NE]))
            seq(v.tensor_copy(jrow, iti[:, 0:4]))
            seq(v.tensor_copy(xrow, iti[:, 0:8]))
            seq(v.tensor_copy(tokf, toki))
            gl = L[:, :, 0:4]
            el = L[:, :, 4:20].rearrange("p i (g e) -> p i g e", g=NGRP)

            def onehot(out, vals, best, tmp4):
                seq(v.tensor_reduce(best, vals, AX.X, ALU.max))
                seq(v.tensor_tensor(tmp4, vals, f2(best, 4), ALU.is_equal))
                seq(v.scalar_tensor_tensor(out=tmp4, in0=tmp4, scalar=-1000.0,
                                           in1=jrow.unsqueeze(1).to_broadcast([P, T5, 4]), op0=ALU.mult, op1=ALU.add))
                seq(v.tensor_reduce(mn, tmp4, AX.X, ALU.min))
                seq(v.tensor_tensor(out, tmp4, f2(mn, 4), ALU.is_equal))

            onehot(og, gl, gm, t4)
            v.tensor_tensor(t4, gl, f2(gm, 4), ALU.subtract).then_inc(S_["rt_e"], 1)
            t44 = t16.rearrange("p i (g e) -> p i g e", g=NGRP)
            seq(v.tensor_tensor(t44, el, og.unsqueeze(3).to_broadcast([P, T5, 4, 4]), ALU.mult))
            seq(v.tensor_reduce(es, t44.rearrange("p i g e -> p i e g"), AX.X, ALU.add))
            dve.wait_ge(S_["gexp"], 1)
            seq(v.tensor_reduce(gs, t4, AX.X, ALU.add))
            seq(v.reciprocal(gw, gs))
            onehot(o1, es, m1, t4)
            seq(v.scalar_tensor_tensor(out=es2, in0=o1, scalar=-BIG, in1=es, op0=ALU.mult, op1=ALU.add))
            onehot(o2, es2, m2, t4)
            v.tensor_tensor(e2, m2, m1, ALU.subtract).then_inc(S_["rt_e"], 1)
            for O, o_ in ((O1, o1), (O2, o2)):
                seq(v.tensor_tensor(O.rearrange("p i (g e) -> p i g e", g=NGRP), og.unsqueeze(3).to_broadcast([P, T5, 4, 4]),
                                    o_.unsqueeze(2).to_broadcast([P, T5, 4, 4]), ALU.mult))
            seq(v.tensor_scalar(mn, tokf, float(NTOK), None, ALU.is_lt))
            seq(v.tensor_tensor(C, O1, O2, ALU.add))
            v.tensor_tensor(C, C, f2(mn, NE), ALU.mult).then_inc(S_["c_ok"], 1)
            dve.wait_ge(S_["gexp"], 2)
            seq(v.tensor_scalar(gs, e2, 1.0, None, ALU.add))
            seq(v.reciprocal(w1, gs))
            seq(v.tensor_tensor(w1, w1, gw, ALU.mult))
            seq(v.tensor_tensor(w2, w1, e2, ALU.mult))
            dve.wait_ge(S_["rank_pe"], 1)
            seq(v.tensor_copy(rank, ps[:, 1, 0:T5 * NE].rearrange("p (i e) -> p i e", i=T5)))
            seq(v.tensor_copy(cnt, ps[:, 1, T5 * NE:(T5 + 1) * NE]))
            seq(v.tensor_scalar(nx, cnt, float(P), None, ALU.is_gt))
            for k in range(2, (NTOK + P - 1) // P):
                seq(v.scalar_tensor_tensor(out=nx, in0=cnt, scalar=float(k * P), in1=nx, op0=ALU.is_gt, op1=ALU.add))
            for k in range(1, (NTOK + P - 1) // P):
                seq(v.scalar_tensor_tensor(out=q_, in0=rank, scalar=float(k * P), in1=q_, op0=ALU.is_ge, op1=ALU.add))
            seq(v.tensor_tensor_scan(incl, ones[:, 0:NE], nx, 0.0, ALU.mult, ALU.add))
            seq(v.tensor_tensor(exc, incl, nx, ALU.subtract))
            seq(v.scalar_tensor_tensor(out=exc, in0=exc, scalar=float(NE - 1), in1=erow, op0=ALU.add, op1=ALU.subtract))
            eb = exc.unsqueeze(1).to_broadcast([P, T5, NE])
            seq(v.tensor_tensor(tl, q_, eb, ALU.add))
            seq(v.tensor_scalar(t16, q_, 1.0, None, ALU.min))
            seq(v.tensor_tensor(tl, tl, t16, ALU.mult))
            seq(v.tensor_tensor(tl, tl, erow.unsqueeze(1).to_broadcast([P, T5, NE]), ALU.add))
            seq(v.scalar_tensor_tensor(out=rank, in0=q_, scalar=-float(P), in1=rank, op0=ALU.mult, op1=ALU.add))
            seq(v.scalar_tensor_tensor(out=slotY, in0=tl, scalar=float(P), in1=rank, op0=ALU.mult, op1=ALU.add))
            seq(v.scalar_tensor_tensor(out=slotL, in0=rank, scalar=float(MAXT), in1=tl, op0=ALU.mult, op1=ALU.add))
            for k, (O, sl) in enumerate(((O1, slotY), (O2, slotY), (O1, slotL), (O2, slotL))):
                seq(v.tensor_tensor(t16, O, sl, ALU.mult))
                seq(v.tensor_reduce(sel[:, k], t16, AX.X, ALU.add))
            v.tensor_copy(seli, sel).then_inc(S_["rank_ok"], 1)
            seq(v.tensor_tensor(xcmp, incl.unsqueeze(1).to_broadcast([P, 8, NE]), f2(xrow, NE), ALU.is_le))
            seq(v.tensor_reduce(tabf[:, NE:MAXT], xcmp, AX.X, ALU.add))
            seq(v.tensor_scalar(tabf[:, NE:MAXT], tabf[:, NE:MAXT], float(NE - 1), None, ALU.min))
            seq(v.tensor_copy(tabf[:, 0:NE], erow))
            seq(v.tensor_copy(tabi, tabf))
            seq(v.memset(npf, NE / 2))
            for k in range((MAXT - NE) // 2):
                seq(v.scalar_tensor_tensor(out=npf[:, 0:1], in0=incl[:, NE - 1:NE], scalar=float(2 * k), in1=npf[:, 0:1],
                                           op0=ALU.is_gt, op1=ALU.add))
            seq(v.tensor_scalar(npf[:, 1:2], npf[:, 0:1], -1.0, None, ALU.add))
            v.tensor_copy(npi, npf).then_inc(S_["tab_rdy"], 1)
            dve.wait_ge(S_["tab_rdy"], 1)
            npairs = dve.value_load(npi[0:1, 0:1], min_val=NE // 2, max_val=MAXT // 2)
            last_pair = dve.value_load(npi[0:1, 1:2], min_val=NE // 2 - 1, max_val=MAXT // 2 - 1)

            def front(j1, b):
                dve.wait_ge(S_["mx_pe"], j1)
                v.tensor_tensor(xgT[b], ps[:, 0:2, :].rearrange("p b (c t) -> p (b c) t", c=4),
                                f2(gains[:, 8:16], P), ALU.mult).then_inc(S_["mx_ok"], 1)

            def product(j1, b):
                dve.wait_ge(S_["sil_ok"], j1)
                dve.wait_ge(S_["u_pe"], j1)
                v.tensor_tensor(hb[b], hb[b], ps[:, 3 + 2 * b, :], ALU.mult).then_inc(S_["h_ok"], 1)

            def yhalf(j1, b, n_st):
                dve.wait_ge(S_["y_pe"], j1)
                if n_st is not None:
                    dve.wait_ge(ystore[b], n_st)
                v.tensor_copy(yb_[b][:, FF:D], ps[:, 7, :]).then_inc(S_["yb_ok"], 1)

            front(1, 0)
            front(2, 1)
            product(1, 0)
            front(3, 0)
            product(2, 1)
            dve.wait_ge(S_["u_st"], 16 * T5)
            yhalf(1, 0, None)
            front(4, 1)
            product(3, 0)
            yhalf(2, 1, None)
            with dve.Fori(1, last_pair) as i:
                front(2 * i + 3, 0)
                product(2 * i + 2, 1)
                yhalf(2 * i + 1, 0, i * 16)
                front(2 * i + 4, 1)
                product(2 * i + 3, 0)
                yhalf(2 * i + 2, 1, i * 16)
            product(npairs * 2, 1)
            yhalf(last_pair * 2 + 1, 0, last_pair * 16)
            yhalf(npairs * 2, 1, last_pair * 16)

            for i in range(T5):
                r = tile_rows(i)
                dve.wait_ge(yload[i % 2], 32 * (i // 2 + 1))
                seq(v.scalar_tensor_tensor(out=XM[0:r, i, :], in0=ybuf[i % 2][0][0:r, :], scalar=w1[0:r, i:i + 1],
                                           in1=XM[0:r, i, :], op0=ALU.mult, op1=ALU.add))
                v.scalar_tensor_tensor(out=XM[0:r, i, :], in0=ybuf[i % 2][1][0:r, :], scalar=w2[0:r, i:i + 1],
                                       in1=XM[0:r, i, :], op0=ALU.mult, op1=ALU.add).then_inc(S_["comb_ok"], 1)
                dve.wait_ge(S_["hn_e"], i + 1)
                if i == 0:
                    for b in range(2):
                        dve.wait_ge(ystore[b], npairs * 16)
                if i >= 3:
                    dve.wait_ge(S_["hnt_pe"], i - 2)
                v.tensor_scalar(Ub[i % 3][0:r, :], XM[0:r, i, :], rstd[0:r, i:i + 1], None,
                                ALU.mult).then_inc(S_["hn_ok"], 1)
                dve.wait_ge(S_["hnt_pe"], i + 1)
                if i >= 2:
                    dve.wait_ge(S_["pg_pe"], i - 1)
                if i == NT:
                    v.memset(hnT[0][:, :, NS:32], 0.0)
                v.tensor_tensor(hnT[i % 2][:, :, 0:r], ps[:, 0:2, :].rearrange("p b (c t) -> p (b c) t", c=4)[:, :, 0:r],
                                f2(gains[:, 16:24], r), ALU.mult).then_inc(S_["hnt_ok"], 1)
                if i:
                    finish(i - 1)
                if i >= 2:
                    last_norm(i - 2)
            finish(NT)
            for i in range(T5 - 2, T5):
                last_norm(i)

        @block.tensor
        def _(pe):
            t = nc.tensor
            pe.wait_ge(S_["consts"], 2)
            pe.wait_ge(S_["cload"], 16 * 10)
            t.transpose(ps[:, 7, 0:27], work2[0:27, 0:P], ident[0:27, 0:27]).then_inc(S_["gain_pe"], 1)
            for i in range(NT + 1):
                r = tile_rows(i)
                pe.wait_ge(S_["xn_ok"], i + 1)
                if i >= 2:
                    pe.wait_ge(S_["xt_ok"], 2 * (i - 1))
                for c in range(DC):
                    last = t.transpose(ps[:, 2 * (i % 2) + c // 4, (c % 4) * P:(c % 4) * P + r],
                                       XM[0:r, i, c * P:(c + 1) * P], ident[0:r, 0:r])
                last.then_inc(S_["xt_pe"], 1)
            pe.wait_ge(S_["xt_ok"], 2 * (NT + 1) + 1)

            def proj(u, k0, k1):
                kind, sl, c0, w, at = UNITS[u]
                if k0 == 0:
                    pe.wait_ge(slabload[sl % 2], 16 * (sl // 2 + 1))
                if k0 == 0 and u >= 2:
                    pe.wait_ge(S_["unit_ok"], u if kind == "SS" and UNITS[u - 1][0] == "SM" else u - 1)
                for c in range(k0, k1):
                    if kind == "FM":
                        last = t.matmul(ps[:, u % 2, :], slab[sl % 2][:, c, c0:c0 + w], xT[:, c, 0:SEQ],
                                        start=(c == 0), stop=(c == DC - 1))
                    elif kind == "TM":
                        i = at[1]
                        last = t.matmul(ps[:, u % 2, 0:w], xT[:, c, i * P:(i + 1) * P],
                                        slab[sl % 2][:, c, c0:c0 + w], start=(c == 0), stop=(c == DC - 1))
                    elif kind == "SM":
                        last = t.matmul(ps[32 * (c % 4):32 * (c % 4) + 32, u % 2, 0:w], xS[:, c, :],
                                        slab[sl % 2][:, c, :], start=(c < 4), stop=(c >= 4))
                if kind == "SS":
                    last = t.matmul(ps[0:NS, u % 2, 0:w], sel4, part, start=True, stop=True)
                if k1 == DC or kind == "SS":
                    last.then_inc(S_["unit_pe"], 1)

            def samp_t():
                pe.wait_ge(S_["unit_ok"], SUMU[1] + 1)
                for c in range(6):
                    last = t.transpose(ps[:, 2, 8 * c:8 * c + 8], samp[:, c * P:(c + 1) * P], ident[0:NS, 0:NS])
                last.then_inc(S_["samp_t_pe"], 1)

            def lev_mm(i, l):
                k = i * (LEVELS + 1) + l
                if l == 0:
                    pe.wait_ge(S_["prep_ok"], 3)
                    L, R = kF, qF
                    L, R = rows_of(L, i), rows_of(R, i)
                else:
                    j = i * LEVELS + l - 1
                    pe.wait_ge(S_["lev_q"], j + 1)
                    L = R = work[:, (2 + j % 2) * SLAB:(3 + j % 2) * SLAB].rearrange("p (c t) -> p c t", c=3)
                if k >= 2:
                    pe.wait_ge(S_["lev_cp"], k - 1)
                for e in range(2):
                    h = slice(64 * e, 64 * e + 64)
                    for c in range(3):
                        last = t.matmul(ps[:, 2 + 2 * (k % 2) + e, c * P:(c + 1) * P], L[h, c, :], R[h, c, :],
                                        start=True, stop=True)
                last.then_inc(S_["lev_pe"], 1)

            def kt(i):
                pe.wait_ge(S_["io_ok"], i + 1)
                if i:
                    pe.wait_ge(S_["h_st_ok"], i)
                for c in range(3):
                    last = t.transpose(ps[:, 7, c * P:(c + 1) * P], work2[:, 1152 + c * P:1152 + (c + 1) * P], ident[:])
                last.then_inc(S_["kt_pe"], 1)

            def h_out(i):
                pe.wait_ge(S_["lev_cp"], (i + 1) * (LEVELS + 1))
                if i:
                    pe.wait_ge(S_["h_out_ok"], i)
                    pe.wait_ge(S_["h_st_ok"], i)
                for c in range(3):
                    for e in range(2):
                        h = 2 * c + e
                        if i:
                            t.matmul(ps[:, 6, h * 64:h * 64 + 64], work2[:, 768 + c * P:768 + (c + 1) * P],
                                     S[:, c, e * 64:e * 64 + 64], start=True, stop=False)
                        last = t.matmul(ps[:, 6, h * 64:h * 64 + 64], work2[:, e * SLAB + c * P:e * SLAB + (c + 1) * P],
                                        iT[:, i, h * 64:h * 64 + 64], start=(i == 0), stop=True)
                last.then_inc(S_["h_out_pe"], 1)

            def h_state(i):
                pe.wait_ge(S_["kt_ok"], i + 1)
                for c in range(3):
                    last = t.matmul(ps[:, 7, c * P:(c + 1) * P], PT[:, 0, c * P:(c + 1) * P],
                                    iT[:, i, c * P:(c + 1) * P], start=True, stop=True)
                last.then_inc(S_["h_st_pe"], 1)

            def d_s(n):
                i, h = divmod(n, HB)
                K = (i + 1) * P
                if n == 0:
                    pe.wait_ge(S_["unit_ok"], LASTU[6] + 1)
                    pe.wait_ge(S_["consts"], 6)
                    pe.wait_ge(S_["lev_cp"], NT * (LEVELS + 1))
                if n >= 2:
                    pe.wait_ge(S_["d_exp"], n - 1)
                c, e = divmod(h, 2)
                for m in range(2):
                    r = slice(64 * e + 32 * m, 64 * e + 32 * m + 32)
                    bank = 2 + 2 * (n % 2) + m
                    q = dF[r, 0, c, i * P:(i + 1) * P]
                    if i:
                        t.matmul(ps[:, bank, 0:i * P], q, dF[r, 1, c, 0:i * P], start=True, stop=True)
                    t.matmul(ps[:, bank, i * P:K], q, dF[r, 1, c, i * P:K], start=True, stop=False)
                    last = t.matmul(ps[:, bank, i * P:K], identb[:], mband[:, P:2 * P], start=False, stop=True)
                last.then_inc(S_["d_s_pe"], 1)

            def d_t(n):
                i = n // HB
                pe.wait_ge(S_["d_a"], n + 1)
                if n >= 1:
                    pe.wait_ge(S_["d_t_ok"], n)
                else:
                    pe.wait_ge(S_["s_o_ok"], 1)
                for k in range(i + 1):
                    last = t.transpose(ps[:, 6, k * P:(k + 1) * P], wk[:, n % 2, k * P:(k + 1) * P], ident[:])
                last.then_inc(S_["d_t_pe"], 1)

            def d_pv(n):
                i, h = divmod(n, HB)
                pe.wait_ge(S_["d_t_ok"], n + 1)
                if h == 0:
                    if i:
                        pe.wait_ge(S_["d_o_ok"], i)
                    else:
                        pe.wait_ge(S_["h_st_ok"], NT)
                for k in range(i + 1):
                    last = t.matmul(ps[:, 7, h * 64:h * 64 + 64], PT[:, n % 2, k * P:(k + 1) * P],
                                    bvT[:, k, h * 64:h * 64 + 64], start=(k == 0), stop=(k == i))
                last.then_inc(S_["d_o_pe"], 1)

            def c_s(n):
                i, h = divmod(n, HC)
                K = (i + 1) * P
                lo = max(i - 1, 0) * P
                if n == 0:
                    pe.wait_ge(S_["unit_ok"], NU)
                    pe.wait_ge(S_["d_exp"], NT * HB)
                else:
                    pe.wait_ge(S_["c_exp"], n)
                c, e = divmod(h, 2)
                r = slice(64 * e, 64 * e + 64)
                for g in range(NG):
                    k0 = lo if g == 0 else 0
                    q, k = cF[r, g, c, i * P:K], cF[r, g, 2 + c, k0:K]
                    mk = mband[:, 2 * P - (K - k0):2 * P] if g == 0 else mstride[:, g - 1, (NT - 1 - i) * P:NT * P]
                    t.matmul(ps[:, 2 + g, 0:K - k0], q, k, start=True, stop=False)
                    last = t.matmul(ps[:, 2 + g, 0:K - k0], identb[:], mk, start=False, stop=True)
                last.then_inc(S_["c_s_pe"], 1)

            def c_t(k):
                n, blocks, _, _ = DG[k]
                pe.wait_ge(S_["c_exp"], n + 1)
                if k >= 2:
                    pe.wait_ge(S_["c_t_ok"], k - 1)
                else:
                    pe.wait_ge(S_["d_t_ok"], NT * HB)
                for x, (g, kt_, col) in enumerate(blocks):
                    last = t.transpose(ps[:, 5 + k % 2, x * P:(x + 1) * P], wk[:, n % 2, col:col + P], ident[:])
                last.then_inc(S_["c_t_pe"], 1)

            def c_pv(k):
                n, blocks, first, final = DG[k]
                i, h = divmod(n, HC)
                pe.wait_ge(S_["c_t_ok"], k + 1)
                if first and h == 0:
                    if i:
                        pe.wait_ge(S_["c_o_ok"], i)
                    else:
                        pe.wait_ge(S_["d_o_ok"], NT)
                for x, (g, kt_, col) in enumerate(blocks):
                    last = t.matmul(ps[:, 7, h * 64:h * 64 + 64], PT[:, k % 2, x * P:(x + 1) * P],
                                    cvT[:, g, kt_, h * 64:h * 64 + 64], start=(first and x == 0),
                                    stop=(final and x == len(blocks) - 1))
                last.then_inc(S_["c_o_pe"], 1)

            def krows(u):
                i, groups = KU[u]
                if u == 0:
                    pe.wait_ge(S_["unit_ok"], NU)
                elif u >= 2:
                    pe.wait_ge(S_["kr_ok"], u - 1)
                if groups is None:
                    blocks = [dF[:, 1, c, i * P:(i + 1) * P] for c in range(3)]
                else:
                    blocks = [cF[:, g, 2 + c, i * P:(i + 1) * P] for g in groups for c in range(2)]
                for k, b in enumerate(blocks):
                    last = t.transpose(ps[:, u % 2, k * P:(k + 1) * P], b, ident[:])
                last.then_inc(S_["kr_pe"], 1)

            def dec_soft():
                pe.wait_ge(S_["kused"], NS)
                pe.wait_ge(S_["new_ok"], 1)
                pe.wait_ge(S_["kr_ok"], len(KU))
                for j in range(PAGES):
                    t.transpose(ps[0:96, 0, j * P:(j + 1) * P], SD[:, j, :], ident[:])
                t.transpose(ps[0:32, 1, 0:P], SC[:, 0, :], ident[:])
                t.transpose(ps[0:32, 1, P:2 * P], SC[:, 1, :], ident[:])
                t.transpose(ps[0:32, 1, 2 * P:2 * P + 32], SC[0:32, 2, :], ident[0:32, 0:32])
                t.matmul(ps[0:96, 1, 320:321], MD, ones[0:NS, 0:1], start=True, stop=True)
                for g in range(NG):
                    last = t.matmul(ps[0:32, 1, 321 + g:322 + g], MC[:, g].rearrange("p b h -> p (b h)"), ones[0:NS, 0:1],
                                    start=True, stop=True)
                last.then_inc(S_["sc_pe"], 1)

            def dec_wt():
                pe.wait_ge(S_["w_ok"], 1)
                for j in range(PAGES):
                    t.transpose(ps[:, 0, j * 96:(j + 1) * 96], RD[:, j * P:(j + 1) * P], ident[0:96, 0:96])
                t.transpose(ps[:, 1, 0:32], RC[:, 0:P], ident[0:32, 0:32])
                t.transpose(ps[:, 1, 32:64], RC[:, P:2 * P], ident[0:32, 0:32])
                t.transpose(ps[0:32, 1, 64:96], RC[:, 2 * P:2 * P + 32], ident[0:32, 0:32])
                t.matmul(ps[0:NS, 1, 128:140], LD, hms, start=True, stop=True)
                for g in range(NG):
                    last = t.matmul(ps[0:NS, 1, 144 + 4 * g:148 + 4 * g], LC[:, g], hsel, start=True, stop=True)
                last.then_inc(S_["wt_pe"], 1)

            def dst_v(b):
                if b == 0:
                    pe.wait_ge(S_["h_out_ok"], NT)
                    pe.wait_ge(S_["h_st_ok"], NT)
                elif b >= 2:
                    pe.wait_ge(S_["kv_ok"], b - 1)
                t.matmul(ps[:, 6 + b % 2, 0:SLAB], ident[0:NS, b:b + 1].to_broadcast([NS, P]),
                         samp[:, 2 * SLAB:3 * SLAB], start=True, stop=True).then_inc(S_["vb_pe"], 1)

            def dst_o():
                pe.wait_ge(S_["s_new"], 1)
                for e in range(2):
                    h = slice(64 * e, 64 * e + 64)
                    for c in range(3):
                        for b in range(NS):
                            last = t.matmul(ps[0:NS, 6 + e, c * 64:c * 64 + 64], Qz[h, c, b, :], stS[h, b, c, :],
                                            start=(b == 0), stop=(b == NS - 1))
                last.then_inc(S_["s_o_pe"], 1)

            def dec_v(u):
                b, win = divmod(u, 2)
                if u < 2:
                    pe.wait_ge(S_["aw_ok"], 1)
                else:
                    pe.wait_ge(S_["pv_ok"], u - 1)
                if win:
                    for g in range(NG):
                        r = (P, P, 32)[g]
                        last = t.matmul(ps[32 * g:32 * g + 32, 1, 0:256], ACz[0:r, g, b], kdil[b % 2][0:r, g],
                                        start=True, stop=True)
                else:
                    pe.wait_ge(kvload[b % 2], 16 * ((KPER + 1) * (NS // 2) + KPER * (b // 2 + 1)))
                    for j in range(PAGES):
                        last = t.matmul(ps[32 * j:32 * j + 32, 0, 0:SLAB], ADz[:, j, b], kpage[b % 2][:, j],
                                        start=True, stop=True)
                last.then_inc(S_["pv_pe"], 1)

            def dec_out():
                pe.wait_ge(S_["pv_ok"], 2 * NS)
                for b in range(NS):
                    last = t.matmul(ps[0:NS, 0, 0:SLAB], one_col[:, NS - b:2 * NS - b], prodD[:, b],
                                    start=(b == 0), stop=(b == NS - 1))
                last.then_inc(S_["ot_pe"], 1)
                for b in range(NS):
                    last = t.matmul(ps[0:NS, 1, 0:256], one_col[0:96, NS - b:2 * NS - b], prodC[:, b],
                                    start=(b == 0), stop=(b == NS - 1))
                last.then_inc(S_["ot_pe"], 1)

            def mt(i):
                r = tile_rows(i)
                pe.wait_ge(S_["ro_ok"], i + 1)
                pe.wait_ge(S_["c_o_ok"], min(i + 1, NT))
                if i == 0:
                    pe.wait_ge(S_["c_exp"], NT * HC)
                    pe.wait_ge(S_["c_t_ok"], len(DG))
                elif i == NT:
                    pe.wait_ge(S_["dec_done"], 1)
                elif i >= 2:
                    pe.wait_ge(S_["mt_ok"], i - 1)
                b = MT_BANK[i]
                for c in range(DC):
                    last = t.transpose(ps[:, b + c // 4, (c % 4) * P:(c % 4) * P + r], XM[0:r, i, c * P:(c + 1) * P],
                                       ident[0:r, 0:r])
                last.then_inc(S_["mt_pe"], 1)

            does = dict(proj=proj, samp_t=samp_t, lev_mm=lev_mm, kt=kt, h_out=h_out, h_state=h_state, d_s=d_s,
                        d_t=d_t, d_pv=d_pv, c_s=c_s, c_t=c_t, c_pv=c_pv, krows=krows, dec_soft=dec_soft,
                        dec_wt=dec_wt, dst_v=dst_v, dst_o=dst_o, dec_v=dec_v, dec_out=dec_out, mt=mt)
            for step, *arg in STEPS:
                if step in does:
                    does[step](*arg)

            def rows_to_columns(src, r, bank):
                for c in range(DC):
                    last = t.transpose(ps[:, bank + c // 4, (c % 4) * P:(c % 4) * P + r], src[0:r, c * P:(c + 1) * P],
                                       ident[0:r, 0:r])
                return last

            pe.wait_ge(S_["woload"], 32)
            d_chunks = list(range(d0 // D, 2 * DC * SLAB // D))
            wo_order = [c for c in range(DC) if c not in d_chunks] + d_chunks

            def sample_product(cols, w, bank):
                for hf in range(2):
                    for c in range(DC):
                        last = t.matmul(ps[32 * (c % 4):32 * (c % 4) + 32, bank + hf, :], cols[:, c, 0:32],
                                        w[:, c, hf * 512:(hf + 1) * 512], start=(c < 4), stop=(c >= 4))
                last.then_inc(S_["sp_pe"], 1)

            def sample_sum(bank, count):
                pe.wait_ge(S_["sp_cp"], count)
                for hf in range(2):
                    last = t.matmul(ps[0:NS, bank + hf, :], sel4, PT[:, hf, :], start=True, stop=True)
                return last

            def wout(i):
                r = tile_rows(i)
                pe.wait_ge(S_["mt_ok"], max(i + 1, 3 + i % 2) if i < NT else T5)
                if i >= 2:
                    pe.wait_ge(S_["hres_ok"], i - 1)
                if i == NT:
                    return sample_product(xS, wout_, 2)
                for x, c in enumerate(wo_order):
                    if i == 0 and c == d_chunks[0]:
                        pe.wait_ge(S_["woload_last"], 16)
                    for hf in range(2):
                        last = t.matmul(ps[0:r, 2 + 2 * (i % 2) + hf, :], xT[:, c, i * P:i * P + r],
                                        wout_[:, c, hf * 512:(hf + 1) * 512], start=(x == 0), stop=(x == DC - 1))
                last.then_inc(S_["wo_pe"], 1)

            def router(i):
                r = tile_rows(i)
                pe.wait_ge(S_["u_ok"], i + 1)
                if i:
                    pe.wait_ge(S_["ut_ok"], i)
                rows_to_columns(Ub[i % 3], r, 6).then_inc(S_["ut_pe"], 1)
                pe.wait_ge(S_["ut_ok"], i + 1)
                pe.wait_ge(S_["mt_ok"], T5)
                for c in range(DC):
                    last = t.matmul(ps[0:r, 0, i * 20:i * 20 + 20], RT[i % 4][:, c, 0:r], rw[:, c, :],
                                    start=(c == 0), stop=(c == DC - 1))
                last.then_inc(S_["rl_pe"], 1)

            wout(0)
            mt(NT)
            for i in range(1, NT):
                wout(i)
                router(i - 1)
            wout(NT)
            router(NT - 1)
            sample_sum(2, 1).then_inc(S_["wo_pe"], 1)
            router(NT)

            def pcolumns(i):
                r = tile_rows(i)
                if i == 0:
                    pe.wait_ge(S_["pload"], 16 * (T5 + 1))
                if i >= 2:
                    pe.wait_ge(S_["pp_c"], i - 1)
                for c in range(PC):
                    last = t.transpose(ps[:, 2 + i % 2, c * P:c * P + r], prow[i][0:r, c * P:(c + 1) * P], ident[0:r, 0:r])
                last.then_inc(S_["pp_t"], 1)

            def pproducts(i):
                r = tile_rows(i)
                pe.wait_ge(S_["pp_c"], i + 1)
                if i >= 2:
                    pe.wait_ge(S_["pp_o"], i - 1)
                for hf in range(2):
                    for c in range(PC):
                        last = t.matmul(ps[0:r, 4 + 2 * (i % 2) + hf, :], pTt[i % 2][:, c, 0:r],
                                        plp_[:, c, hf * 512:(hf + 1) * 512], start=(c == 0), stop=(c == PC - 1))
                last.then_inc(S_["pp_m"], 1)

            pcolumns(0)
            pcolumns(1)
            pproducts(0)
            pproducts(1)
            pe.wait_ge(S_["c_ok"], 1)
            for i in range(T5):
                for k in range(i):
                    t.matmul(ps[:, 1, i * NE:(i + 1) * NE], ones[:], C[:, k], start=(k == 0), stop=False)
                t.matmul(ps[:, 1, i * NE:(i + 1) * NE], tri, C[:, i], start=(i == 0), stop=True)
            for k in range(T5):
                last = t.matmul(ps[:, 1, T5 * NE:(T5 + 1) * NE], ones[:], C[:, k], start=(k == 0), stop=(k == T5 - 1))
            last.then_inc(S_["rank_pe"], 1)
            pcolumns(2)
            pcolumns(3)
            pproducts(2)
            pcolumns(4)
            pproducts(3)
            pproducts(4)

            pe.wait_ge(S_["tab_rdy"], 1)
            npairs = pe.value_load(npi[0:1, 0:1], min_val=NE // 2, max_val=MAXT // 2)
            last_pair = pe.value_load(npi[0:1, 1:2], min_val=NE // 2 - 1, max_val=MAXT // 2 - 1)

            def gate(j1, b, n_ld, prev):
                pe.wait_ge(S_["mx_ok"], j1)
                pe.wait_ge(wload["wg"][b], n_ld)
                if prev is not None:
                    pe.wait_ge(S_["ht_ok"], prev)
                for c in range(DC):
                    last = t.matmul(ps[:, 2 + 2 * b, :], xgT[b][:, c, :], wg_[b][:, c, :], start=(c == 0), stop=(c == DC - 1))
                last.then_inc(S_["g_pe"], 1)

            def up(j1, b, n_ld):
                pe.wait_ge(wload["wu"][b], n_ld)
                for c in range(DC):
                    last = t.matmul(ps[:, 3 + 2 * b, :], xgT[b][:, c, :], wu_[b][:, c, :], start=(c == 0), stop=(c == DC - 1))
                last.then_inc(S_["u_pe"], 1)

            def rows(j, b, n_ld):
                pe.wait_ge(xgload[b], n_ld)
                if j is not None:
                    pe.wait_ge(S_["mx_ok"], j)
                rows_to_columns(xg[b], P, 0).then_inc(S_["mx_pe"], 1)

            def products(j1, b):
                pe.wait_ge(S_["h_ok"], j1)
                for c in range(FC):
                    last = t.transpose(ps[:, 2 + 2 * b, c * P:(c + 1) * P], hb[b][:, c * P:(c + 1) * P], ident[:])
                last.then_inc(S_["ht_pe"], 1)

            def down(j1, b, n_ld, prev):
                pe.wait_ge(S_["ht_ok"], j1)
                pe.wait_ge(wload["wd"][b], n_ld)
                if prev is not None:
                    pe.wait_ge(S_["ya_ok"], prev)
                    pe.wait_ge(S_["yb_ok"], prev)
                for hf in range(2):
                    for c in range(FC):
                        last = t.matmul(ps[:, 6 + hf, :], hT[b][:, c, :], wd_[b][:, c, hf * 512:(hf + 1) * 512],
                                        start=(c == 0), stop=(c == FC - 1))
                last.then_inc(S_["y_pe"], 1)

            pe.wait_ge(S_["rank_ok"], 1)
            pe.wait_ge(S_["pp_o"], T5)
            rows(None, 0, 16)
            gate(1, 0, 16, None)
            rows(1, 1, 16)
            up(1, 0, 16)
            gate(2, 1, 16, None)
            rows(2, 0, 32)
            products(1, 0)
            up(2, 1, 16)
            down(1, 0, 16, None)
            gate(3, 0, 32, 1)
            rows(3, 1, 32)
            products(2, 1)
            up(3, 0, 32)
            down(2, 1, 16, 1)
            with pe.Fori(1, last_pair) as i:
                gate(2 * i + 2, 1, i * 16 + 16, i * 2)
                rows(2 * i + 2, 0, i * 16 + 32)
                products(2 * i + 1, 0)
                up(2 * i + 2, 1, i * 16 + 16)
                down(2 * i + 1, 0, i * 16 + 16, i * 2)
                gate(2 * i + 3, 0, i * 16 + 32, i * 2 + 1)
                rows(2 * i + 3, 1, i * 16 + 32)
                products(2 * i + 2, 1)
                up(2 * i + 3, 0, i * 16 + 32)
                down(2 * i + 2, 1, i * 16 + 16, i * 2 + 1)
            gate(npairs * 2, 1, npairs * 16, last_pair * 2)
            products(last_pair * 2 + 1, 0)
            up(npairs * 2, 1, npairs * 16)
            down(last_pair * 2 + 1, 0, npairs * 16, last_pair * 2)
            products(npairs * 2, 1)
            down(npairs * 2, 1, npairs * 16, last_pair * 2 + 1)

            pe.wait_ge(S_["pleload"], 32)

            def columns(i):
                r = tile_rows(i)
                pe.wait_ge(S_["hn_ok"], i + 1)
                if i:
                    pe.wait_ge(S_["hnt_ok"], i)
                rows_to_columns(Ub[i % 3], r, 0).then_inc(S_["hnt_pe"], 1)

            def ple(i):
                r = tile_rows(i)
                pe.wait_ge(S_["hnt_ok"], i + 1)
                if i >= 2:
                    pe.wait_ge(S_["pg_sig"], i - 1)
                if i == NT:
                    sample_product(hnT[0], ple_, 4)
                    return sample_sum(4, 2).then_inc(S_["pg_pe"], 1)
                for hf in range(2):
                    for c in range(DC):
                        last = t.matmul(ps[0:r, 4 + 2 * (i % 2) + hf, :], hnT[i % 2][:, c, 0:r],
                                        ple_[:, c, hf * 512:(hf + 1) * 512], start=(c == 0), stop=(c == DC - 1))
                last.then_inc(S_["pg_pe"], 1)

            columns(0)
            for i in range(T5):
                ple(i)
                if i < NT:
                    columns(i + 1)


INS = ['x_prompt', 'x_sample', 'state_hgrn', 'cache_k_diff', 'cache_v_diff', 'cache_win128', 'cache_win512',
       'cache_win2048', 'page_table', 'p_prompt', 'p_sample', 'w_in', 'hgrn_lb_logits', 'hgrn_norm',
       'diff_lambda', 'diff_norm', 'w_out', 'router_group_w', 'router_group_b', 'router_expert_w',
       'router_expert_b', 'moe_w_gate', 'moe_w_up', 'moe_w_down', 'ple_w_gate', 'ple_w_proj', 'norm_final']
OUTS = {'y_prompt': (1, 512, 1024), 'y_sample': (8, 1, 1024),
        'state_hgrn_prompt': (1, 1, 6, 64, 64), 'state_hgrn_sample': (1, 8, 6, 64, 64),
        'k_diff_prompt': (1, 1, 512, 6, 2, 32), 'k_diff_sample': (1, 8, 1, 6, 2, 32),
        'v_diff_prompt': (1, 1, 512, 6, 64), 'v_diff_sample': (1, 8, 1, 6, 64),
        'win128_prompt': (1, 1, 128, 2, 4, 64), 'win128_sample': (1, 8, 128, 2, 4, 64),
        'win512_prompt': (1, 1, 512, 2, 4, 64), 'win512_sample': (1, 8, 512, 2, 4, 64),
        'win2048_prompt': (1, 1, 512, 2, 4, 64), 'win2048_sample': (1, 8, 512, 2, 4, 64)}


def kernel(**inputs):
    import numpy as _np
    import concourse.bacc as _bacc
    from concourse import mybir as _mybir
    from concourse.bass_utils import run_bass_kernel_spmd as _run

    nc = _bacc.Bacc("TRN2", target_bir_lowering=False, num_devices=1)
    host = {name: _np.ascontiguousarray(inputs[name]) for name in INS}
    host["norms"] = _np.concatenate([_np.asarray(inputs[k]).reshape(8, 128) for k in ("norm_mix", "norm_ffn", "norm_ple")])
    a, arrays = {}, {}
    for name, x in host.items():
        arrays["in_" + name] = x
        a[name] = nc.dram_tensor("in_" + name, x.shape, _mybir.dt.from_np(x.dtype), kind="ExternalInput").ap()
    o = {name: nc.dram_tensor("out_" + name, shape, _mybir.dt.float32, kind="ExternalOutput").ap()
         for name, shape in OUTS.items()}
    o["win_prompt"] = [o["win128_prompt"], o["win512_prompt"], o["win2048_prompt"]]
    o["win_sample"] = [o["win128_sample"], o["win512_sample"], o["win2048_sample"]]
    hybrid_kernel(nc, a, o)
    r = _run(nc, [arrays], core_ids=[0])
    return tuple(r.results[0]["out_" + name] for name in OUTS)
```
